# Optimizing a Trainium2 kernel written in Bass

```python
import math
import jax
import jax.numpy as jnp
from jax import lax
import numpy as np

D_MODEL = 1024
BATCH = 1
SEQ = 1024
DEPTH = 1
DEC_BATCH = 8
DEC_SEQ = 1
PAST_LEN = 2048
PAGE_SIZE = 128

MIX_W = D_MODEL
ATTN_W = MIX_W // 2
POOL_W = MIX_W - ATTN_W
HEAD_DIM = 64
N_HEADS = ATTN_W // (2 * HEAD_DIM)
V_DIM = 2 * HEAD_DIM
IN_COLS = 3 * ATTN_W + POOL_W
POOL_WINDOWS = (2, 4, 8, 16)
N_POOL_GROUPS = len(POOL_WINDOWS)
POOL_GW = POOL_W // N_POOL_GROUPS
POOL_BUF = max(POOL_WINDOWS) - 1
ROPE_THETA = 10000.0
Q_BLOCK = 128
N_EXPERTS = 64
TOP_K = 8
N_EXPERT_GROUPS = 8
TOPK_GROUPS = 4
EXPERT_DIM = 256
SHARED_DIM = 256
ROUTED_SCALE = 2.5
MOE_BLOCK = 128
EPS = 1e-6

kernel_name = "hybrid_diffattn_pool_moe_step"

def rmsnorm(x, g):
    xf = x.astype(jnp.float32)
    y = xf * lax.rsqrt(jnp.mean(xf * xf, axis=-1, keepdims=True) + EPS)
    return (y * g.astype(jnp.float32)).astype(x.dtype)

def ada_mod(c, w, b):
    mod = jax.nn.silu(c) @ w + b
    return jnp.split(mod, 6, axis=-1)

def modulate(h, shift, scale):
    return h * (1.0 + scale[:, None, :]) + shift[:, None, :]

def in_proj(h, w_in):
    proj = h @ w_in
    lead = proj.shape[:-1]
    q = proj[..., :ATTN_W].reshape(*lead, N_HEADS, 2, HEAD_DIM)
    k = proj[..., ATTN_W:2 * ATTN_W].reshape(*lead, N_HEADS, 2, HEAD_DIM)
    v = proj[..., 2 * ATTN_W:3 * ATTN_W].reshape(*lead, N_HEADS, V_DIM)
    z = proj[..., 3 * ATTN_W:]
    return q, k, v, z

def rope(x, pos):
    half = HEAD_DIM // 2
    inv_freq = ROPE_THETA ** (-jnp.arange(half, dtype=jnp.float32) / half)
    ang = pos.astype(jnp.float32)[:, None] * inv_freq[None, :]
    cos = jnp.cos(ang)[None, :, None, None, :]
    sin = jnp.sin(ang)[None, :, None, None, :]
    x1 = x[..., :half].astype(jnp.float32)
    x2 = x[..., half:].astype(jnp.float32)
    return jnp.concatenate([x1 * cos - x2 * sin, x2 * cos + x1 * sin], axis=-1).astype(x.dtype)

def diff_lambda(lq1, lk1, lq2, lk2, lam_init):
    return (jnp.exp(jnp.sum(lq1 * lk1).astype(jnp.float32))
            - jnp.exp(jnp.sum(lq2 * lk2).astype(jnp.float32)) + lam_init)

def diff_weights(logits, mask, lam):
    p = jax.nn.softmax(jnp.where(mask, logits, -jnp.inf), axis=-1)
    return p[0] - lam * p[1]

def diff_attn_prompt(q, k, v, lam):
    b, s = q.shape[:2]
    nb = s // Q_BLOCK
    q_blocks = jnp.moveaxis(q.reshape(b, nb, Q_BLOCK, N_HEADS, 2, HEAD_DIM), 1, 0)
    k_pos = jnp.arange(s)
    scale = HEAD_DIM ** -0.5

    def one_block(args):
        qb, i = args
        q_pos = i * Q_BLOCK + jnp.arange(Q_BLOCK)
        causal = k_pos[None, :] <= q_pos[:, None]
        logits = jnp.einsum('bqhmd,bkhmd->mbhqk', qb, k).astype(jnp.float32) * scale
        wts = diff_weights(logits, causal, lam)
        return jnp.einsum('bhqk,bkhe->bqhe', wts.astype(v.dtype), v)

    out = lax.map(one_block, (q_blocks, jnp.arange(nb)))
    return jnp.moveaxis(out, 0, 1).reshape(b, s, N_HEADS, V_DIM)

def diff_attn_sample(q, k, v, lam, k_past, v_past):
    n_new = q.shape[1]
    n_past = k_past.shape[1]
    scale = HEAD_DIM ** -0.5
    l_past = jnp.einsum('bqhmd,bkhmd->mbhqk', q, k_past)
    l_new = jnp.einsum('bqhmd,bkhmd->mbhqk', q, k)
    logits = jnp.concatenate([l_past, l_new], axis=-1).astype(jnp.float32) * scale
    t = jnp.arange(n_new)
    mask = jnp.concatenate([jnp.ones((n_new, n_past), dtype=bool), t[None, :] <= t[:, None]], axis=-1)
    wts = diff_weights(logits, mask, lam).astype(v.dtype)
    return (jnp.einsum('bhqk,bkhe->bqhe', wts[..., :n_past], v_past)
            + jnp.einsum('bhqk,bkhe->bqhe', wts[..., n_past:], v))

def pool_mix(z, pos, w_pool, pool_scale):
    b, L = z.shape[:2]
    zf = z.astype(jnp.float32).reshape(b, L, N_POOL_GROUPS, POOL_GW)
    cs = jnp.cumsum(zf, axis=1)
    outs = []
    for g, w in enumerate(POOL_WINDOWS):
        csg = cs[:, :, g]
        prev = jnp.pad(csg, ((0, 0), (w, 0), (0, 0)))[:, :L]
        cnt = jnp.minimum(pos + 1, w).astype(jnp.float32)[None, :, None]
        outs.append((csg - prev) / cnt - zf[:, :, g])
    d = jnp.stack(outs, axis=2)
    y = jnp.einsum('blgc,gcf->blgf', d, w_pool.astype(jnp.float32)).reshape(b, L, POOL_W)
    return (y * pool_scale.astype(jnp.float32)).astype(z.dtype)

def pool_prompt(z, pos, w_pool, pool_scale):
    return pool_mix(z, pos, w_pool, pool_scale), z[:, -POOL_BUF:]

def pool_sample(z, buf, past_len, w_pool, pool_scale):
    zc = jnp.concatenate([buf.astype(z.dtype), z], axis=1)
    pos = past_len - POOL_BUF + jnp.arange(zc.shape[1])
    return pool_mix(zc, pos, w_pool, pool_scale)[:, POOL_BUF:], zc[:, -POOL_BUF:]

def route(x, w_router, router_bias):
    t = x.shape[0]
    scores = jax.nn.sigmoid((x @ w_router).astype(jnp.float32))
    sel = (scores + router_bias.astype(jnp.float32)).reshape(t, N_EXPERT_GROUPS, -1)
    group_score = jnp.sum(lax.top_k(sel, 2)[0], axis=-1)
    _, gidx = lax.top_k(group_score, TOPK_GROUPS)
    gmask = jnp.zeros((t, N_EXPERT_GROUPS), dtype=bool).at[jnp.arange(t)[:, None], gidx].set(True)
    masked = jnp.where(gmask[:, :, None], sel, -jnp.inf).reshape(t, N_EXPERTS)
    _, idx = lax.top_k(masked, TOP_K)
    w = jnp.take_along_axis(scores, idx, axis=-1)
    w = w / jnp.sum(w, axis=-1, keepdims=True) * ROUTED_SCALE
    return idx, w

def routed_experts(x, idx, wts, w_gate, w_up, w_down):
    t, d = x.shape
    a = t * TOP_K
    flat_e = idx.reshape(a)
    flat_t = jnp.repeat(jnp.arange(t, dtype=jnp.int32), TOP_K)
    flat_w = wts.reshape(a)
    order = jnp.argsort(flat_e)
    e_s, t_s, w_s = flat_e[order], flat_t[order], flat_w[order]
    counts = jnp.bincount(flat_e, length=N_EXPERTS)
    pcounts = (counts + MOE_BLOCK - 1) // MOE_BLOCK * MOE_BLOCK
    start = jnp.cumsum(counts) - counts
    pend = jnp.cumsum(pcounts)
    pstart = pend - pcounts
    dest = pstart[e_s] + jnp.arange(a) - start[e_s]
    n_blocks = -(-a // MOE_BLOCK) + N_EXPERTS
    n_rows = n_blocks * MOE_BLOCK
    tok_p = jnp.full((n_rows,), t, dtype=jnp.int32).at[dest].set(t_s)
    w_p = jnp.zeros((n_rows,), dtype=wts.dtype).at[dest].set(w_s)
    blk_e = jnp.minimum(jnp.searchsorted(pend, jnp.arange(n_blocks) * MOE_BLOCK, side='right'), N_EXPERTS - 1)
    x_pad = jnp.concatenate([x, jnp.zeros((1, d), x.dtype)], axis=0)

    def one_block(args):
        tok_b, w_b, e = args
        xb = x_pad[tok_b]
        hb = jax.nn.silu(xb @ w_gate[e]) * (xb @ w_up[e])
        return (hb @ w_down[e]) * w_b[:, None]

    out = lax.map(one_block, (tok_p.reshape(n_blocks, MOE_BLOCK), w_p.reshape(n_blocks, MOE_BLOCK), blk_e))
    return jax.ops.segment_sum(out.reshape(n_rows, d), tok_p, num_segments=t + 1)[:t]

def moe_ffn(h, lw):
    lead = h.shape[:-1]
    x = h.reshape(-1, h.shape[-1])
    idx, wts = route(x, lw['router_w'], lw['router_bias'])
    routed = routed_experts(x, idx, wts.astype(x.dtype), lw['expert_w_gate'], lw['expert_w_up'], lw['expert_w_down'])
    shared = (jax.nn.silu(x @ lw['shared_w_gate']) * (x @ lw['shared_w_up'])) @ lw['shared_w_down']
    return (routed + shared).reshape(*lead, -1)

def trunk_layer(x, c, pos, lam_init, attend, pool, lw):
    sh1, sc1, g1, sh2, sc2, g2 = ada_mod(c, lw['ada_w'], lw['ada_b'])
    h = modulate(rmsnorm(x, lw['pre_mix_g']), sh1, sc1)
    q, k, v, z = in_proj(h, lw['w_in'])
    q = rope(q, pos)
    k = rope(k, pos)
    lam = diff_lambda(lw['lambda_q1'], lw['lambda_k1'], lw['lambda_q2'], lw['lambda_k2'], lam_init)
    o = attend(q, k, v, lam)
    o = rmsnorm(o, lw['subln_g']) * (1.0 - lam_init)
    pz, pool_state = pool(z)
    m = jnp.concatenate([o.reshape(*o.shape[:2], ATTN_W), pz], axis=-1) @ lw['w_out']
    x = x + g1[:, None, :] * rmsnorm(m, lw['post_mix_g'])
    h2 = modulate(rmsnorm(x, lw['pre_ffn_g']), sh2, sc2)
    f = moe_ffn(h2, lw)
    x = x + g2[:, None, :] * rmsnorm(f, lw['post_ffn_g'])
    k_rows = k.reshape(*k.shape[:3], 2 * HEAD_DIM)
    return x, k_rows, v, pool_state

def setup_inputs(seed: int = 0) -> dict:
    key = jax.random.key(seed)
    ks = jax.random.split(key, 32)
    f32 = jnp.float32

    def nrm(k, shape, s):
        return jax.random.normal(k, shape, f32) * s

    n_pages = PAST_LEN // PAGE_SIZE
    n_used = DEC_BATCH * n_pages
    n_phys = n_used + n_used // 4
    page_table = jax.random.permutation(ks[0], n_phys)[:n_used].reshape(DEC_BATCH, n_pages).astype(jnp.int32)
    kv_shape = (DEPTH, n_phys, PAGE_SIZE, N_HEADS, 2 * HEAD_DIM)
    return {
        'x_prompt': nrm(ks[1], (BATCH, SEQ, D_MODEL), 1.0),
        'x_sample': nrm(ks[2], (DEC_BATCH, DEC_SEQ, D_MODEL), 1.0),
        'c_prompt': nrm(ks[3], (BATCH, D_MODEL), 1.0),
        'c_sample': nrm(ks[4], (DEC_BATCH, D_MODEL), 1.0),
        'cache_k': nrm(ks[5], kv_shape, 1.0),
        'cache_v': nrm(ks[6], kv_shape, 1.0),
        'state_pool': nrm(ks[7], (DEPTH, DEC_BATCH, POOL_BUF, POOL_W), 1.0),
        'page_table': page_table,
        'ada_w': nrm(ks[8], (DEPTH, D_MODEL, 6 * D_MODEL), 0.2 * D_MODEL ** -0.5),
        'ada_b': nrm(ks[9], (DEPTH, 6 * D_MODEL), 0.02),
        'pre_mix_g': 1.0 + nrm(ks[10], (DEPTH, D_MODEL), 0.02),
        'post_mix_g': 1.0 + nrm(ks[11], (DEPTH, D_MODEL), 0.02),
        'pre_ffn_g': 1.0 + nrm(ks[12], (DEPTH, D_MODEL), 0.02),
        'post_ffn_g': 1.0 + nrm(ks[13], (DEPTH, D_MODEL), 0.02),
        'w_in': nrm(ks[14], (DEPTH, D_MODEL, IN_COLS), D_MODEL ** -0.5),
        'w_out': nrm(ks[15], (DEPTH, MIX_W, D_MODEL), MIX_W ** -0.5),
        'lambda_q1': nrm(ks[16], (DEPTH, HEAD_DIM), 0.1),
        'lambda_k1': nrm(ks[17], (DEPTH, HEAD_DIM), 0.1),
        'lambda_q2': nrm(ks[18], (DEPTH, HEAD_DIM), 0.1),
        'lambda_k2': nrm(ks[19], (DEPTH, HEAD_DIM), 0.1),
        'subln_g': 1.0 + nrm(ks[20], (DEPTH, V_DIM), 0.02),
        'pool_w': nrm(ks[21], (DEPTH, N_POOL_GROUPS, POOL_GW, POOL_GW), POOL_GW ** -0.5),
        'pool_scale': 1.0 + nrm(ks[22], (DEPTH, POOL_W), 0.1),
        'router_w': nrm(ks[23], (DEPTH, D_MODEL, N_EXPERTS), D_MODEL ** -0.5),
        'router_bias': nrm(ks[24], (DEPTH, N_EXPERTS), 0.01),
        'expert_w_gate': nrm(ks[25], (DEPTH, N_EXPERTS, D_MODEL, EXPERT_DIM), D_MODEL ** -0.5),
        'expert_w_up': nrm(ks[26], (DEPTH, N_EXPERTS, D_MODEL, EXPERT_DIM), D_MODEL ** -0.5),
        'expert_w_down': nrm(ks[27], (DEPTH, N_EXPERTS, EXPERT_DIM, D_MODEL), EXPERT_DIM ** -0.5),
        'shared_w_gate': nrm(ks[28], (DEPTH, D_MODEL, SHARED_DIM), D_MODEL ** -0.5),
        'shared_w_up': nrm(ks[29], (DEPTH, D_MODEL, SHARED_DIM), D_MODEL ** -0.5),
        'shared_w_down': nrm(ks[30], (DEPTH, SHARED_DIM, D_MODEL), SHARED_DIM ** -0.5),
    }

def reference(x_prompt, x_sample, c_prompt, c_sample, cache_k, cache_v, state_pool, page_table,
              ada_w, ada_b, pre_mix_g, post_mix_g, pre_ffn_g, post_ffn_g, w_in, w_out,
              lambda_q1, lambda_k1, lambda_q2, lambda_k2, subln_g, pool_w, pool_scale,
              router_w, router_bias, expert_w_gate, expert_w_up, expert_w_down,
              shared_w_gate, shared_w_up, shared_w_down):
    seq = x_prompt.shape[1]
    dec_batch, dec_seq = x_sample.shape[:2]
    past_len = page_table.shape[1] * cache_k.shape[2]
    pos_p = jnp.arange(seq)
    pos_s = past_len + jnp.arange(dec_seq)
    y_p, y_s = x_prompt, x_sample
    kp, vp, pp, ksm, vsm, psm = [], [], [], [], [], []
    for l in range(DEPTH):
        lw = {
            'ada_w': ada_w[l], 'ada_b': ada_b[l],
            'pre_mix_g': pre_mix_g[l], 'post_mix_g': post_mix_g[l],
            'pre_ffn_g': pre_ffn_g[l], 'post_ffn_g': post_ffn_g[l],
            'w_in': w_in[l], 'w_out': w_out[l],
            'lambda_q1': lambda_q1[l], 'lambda_k1': lambda_k1[l],
            'lambda_q2': lambda_q2[l], 'lambda_k2': lambda_k2[l],
            'subln_g': subln_g[l],
            'router_w': router_w[l], 'router_bias': router_bias[l],
            'expert_w_gate': expert_w_gate[l], 'expert_w_up': expert_w_up[l],
            'expert_w_down': expert_w_down[l],
            'shared_w_gate': shared_w_gate[l], 'shared_w_up': shared_w_up[l],
            'shared_w_down': shared_w_down[l],
        }
        lam_init = 0.8 - 0.6 * math.exp(-0.3 * l)
        y_p, k_rows, v_rows, buf = trunk_layer(
            y_p, c_prompt, pos_p, lam_init, diff_attn_prompt,
            lambda z: pool_prompt(z, pos_p, pool_w[l], pool_scale[l]), lw)
        kp.append(k_rows)
        vp.append(v_rows)
        pp.append(buf)
        k_past = cache_k[l, page_table].reshape(dec_batch, past_len, N_HEADS, 2, HEAD_DIM)
        v_past = cache_v[l, page_table].reshape(dec_batch, past_len, N_HEADS, V_DIM)
        y_s, k_rows, v_rows, buf = trunk_layer(
            y_s, c_sample, pos_s, lam_init,
            lambda q, k, v, lam: diff_attn_sample(q, k, v, lam, k_past, v_past),
            lambda z: pool_sample(z, state_pool[l], past_len, pool_w[l], pool_scale[l]), lw)
        ksm.append(k_rows)
        vsm.append(v_rows)
        psm.append(buf)
    return (y_p, y_s, jnp.stack(kp), jnp.stack(vp), jnp.stack(pp), jnp.stack(ksm), jnp.stack(vsm), jnp.stack(psm))


_drawn_inputs = setup_inputs


def setup_inputs(seed=0):
    import zlib

    import numpy as np

    out = dict(_drawn_inputs(seed))
    spreads = {}
    factors = {'pre_mix_g': 2.929,
     'post_mix_g': 4.997,
     'pre_ffn_g': 4.352,
     'post_ffn_g': 8.0,
     'lambda_q1': 3.598,
     'lambda_q2': 5.222,
     'lambda_k2': 4.075,
     'subln_g': 8.0,
     'pool_scale': 4.886}
    for name, (base, spread) in spreads.items():
        noise = np.random.default_rng([zlib.crc32(name.encode()), seed]).standard_normal(out[name].shape)
        drawn = base * np.exp(spread * noise) if base else spread * noise
        out[name] = jnp.asarray(drawn.astype(out[name].dtype))
    for name, factor in factors.items():
        out[name] = (out[name] * factor).astype(out[name].dtype)
    return out
```

```python
import math
from contextlib import ExitStack, contextmanager

import numpy as np

import concourse.bass as bass
from concourse import mybir

F32 = mybir.dt.float32
I32 = mybir.dt.int32
U32 = mybir.dt.uint32
ALU = mybir.AluOpType
ACT = mybir.ActivationFunctionType
AX_X = mybir.AxisListType.X
RED = bass.bass_isa.ReduceOp

P = 128
D = 1024
KC = D // P
SEQ = 1024
NT = SEQ // P
NS = 8
PAST = 2048
PAGE = 128
NPG = PAST // PAGE
NH = 4
HD = 64
HM = 2 * NH
AW = NH * 2 * HD
POOL_WINDOWS = (2, 4, 8, 16)
NG = len(POOL_WINDOWS)
BUF = max(POOL_WINDOWS) - 1
IN_COLS = 3 * AW + NG * P
NE = 64
TOPK = 8
EG = 8
TOPG = 4
F = 256
FC = F // P
SCALE_ROUTED = 2.5
EPS = 1e-6
LAM_INIT = 0.8 - 0.6 * math.exp(0.0)
NTOK = SEQ + NS
NBLK = NTOK * TOPK // P + NE
NBLK += NBLK % 2
TOK_STRIDE = 256
NEG = -1e30
SLOTS = 3
MODS = 6



def constants():
    parts, at, pos = [], {}, 0

    def put(name, a):
        nonlocal pos
        full = np.zeros((P, a.shape[1]), np.float32)
        full[:a.shape[0]] = a
        parts.append(full)
        at[name] = (pos, pos + a.shape[1])
        pos += a.shape[1]

    r = np.arange(P)
    put("ident", np.eye(P))
    put("causal", np.where(r[None, :] <= r[:, None], 0.0, NEG))
    put("before", (r[:, None] < r[None, :]).astype(np.float32))
    put("ones", np.ones((P, P)))
    half = HD // 2
    inv = (10000.0 ** (-np.arange(half) / half)).astype(np.float32)
    pos_of = np.concatenate([np.full((P, 1), PAST), np.arange(SEQ).reshape(NT, P).T], 1).astype(np.float32)
    ang = (pos_of[:, :, None] * inv.astype(np.float32)[None, None, :]).astype(np.float32).astype(np.float64)
    put("cos", np.concatenate([np.cos(ang), np.cos(ang)], 2).reshape(P, -1))
    put("sin", np.concatenate([-np.sin(ang), np.sin(ang)], 2).reshape(P, -1))
    t_in, t_out = r[:, None], r[None, :]
    first, later, prev, samp = [], [], [], []
    for w in POOL_WINDOWS:
        inside = (t_out - t_in >= 0) & (t_out - t_in < w)
        first.append(np.where(inside, 1.0 / np.minimum(t_out + 1, w), 0) - np.eye(P))
        later.append(np.where(inside, 1.0 / w, 0) - np.eye(P))
        prev.append(np.where(t_out + P - t_in < w, 1.0 / w, 0))
        s = np.zeros((P, NS))
        for q in range(NS):
            for j in range(BUF - (w - 1), BUF):
                s[q * BUF + j, q] = 1.0 / w
            s[NS * BUF + q, q] = 1.0 / w - 1.0
        samp.append(s)
    put("band", np.concatenate(first + later, 1))
    put("band_prev", np.concatenate(prev, 1))
    put("band_samp", np.concatenate(samp, 1))
    put("iota_e", np.tile(np.arange(NE), (P, 1)))
    put("lower_g", np.tile((np.arange(EG)[None, :] < np.arange(EG)[:, None]).reshape(1, -1), (P, 1)))
    put("steps_128", np.tile(P * np.arange(1, 9), (P, 1)))
    put("steps_3", np.tile(SLOTS * np.arange(1, NE // SLOTS + 1), (P, 1)))
    put("block_id", r[:, None])
    put("is_sample", (r[:, None] < NS))
    return np.concatenate(parts, 1).astype(np.float32), at


def int_constants():
    r = np.arange(P)
    ids = np.stack([SEQ + r] + [t * P + r for t in range(NT)], 1)
    return np.concatenate([ids, np.full((P, TOK_STRIDE), NTOK)], 1).astype(np.int32)


class Step:

    def __init__(self, n, par, turn):
        self.n, self.par, self.turn = n, par, turn

    @property
    def next(self):
        return Step(self.n + 1, 1 - self.par, self.turn + self.par)


def fixed(n):
    return Step(n, n % 2, n // 2)


def wait(eng, sem, value):
    if not isinstance(value, int) or value > 0:
        eng.wait_ge(sem, value)


def addressed(eng, *aps):
    for ap in aps:
        if not isinstance(ap.offset, int):
            eng.lower_val(ap.offset * 4)
    return aps


class Own:

    def __init__(self, eng, sem):
        self.eng, self.sem, self.base, self.n = eng, sem, 0, 0

    def __call__(self, ins):
        ins.then_inc(self.sem, 1)
        self.n += 1
        return ins

    def wait(self):
        self.eng.wait_ge(self.sem, self.base + self.n)

    @contextmanager
    def loop(self, count, per):
        start = self.base + self.n
        with self.eng.Fori(0, count) as i:
            self.base, self.n = i * per + start, 0
            yield i
            assert self.n == per, f"{self.n} steps in the loop, not {per}"
        self.base, self.n = start + count * per, 0


def build(nc, ins, outs):
    (x_prompt, x_sample, c_prompt, c_sample, cache_k, cache_v, state_pool, page_table, ada_w, ada_b,
     pre_mix_g, post_mix_g, pre_ffn_g, post_ffn_g, w_in, w_out, lq1, lk1, lq2, lk2, subln_g, pool_w,
     pool_scale, router_w, router_bias, ew_gate, ew_up, ew_down, sw_gate, sw_up, sw_down, const_d, consti_d) = ins
    y_prompt, y_sample, k_prompt, v_prompt, pool_prompt, k_sample, v_sample, pool_sample = outs
    _, at = constants()
    ctx = ExitStack()
    with ctx:
        ctx.enter_context(nc.allow_non_contiguous_dma(reason="small tables"))
        base = nc.sbuf_base + (-nc.sbuf_base) % 64

        def place(name, kb, shape, dt=F32):
            return nc.alloc_sbuf_tensor_at(name, shape, dt, offset=base + int(kb * 1024))

        used = []

        def sem(name, keep=False):
            s = nc.alloc_semaphore(name)
            if not keep:
                used.append(s)
            return s

        def free_semaphores():
            nc.clear_and_free_semaphores(used)
            nc.all_engine_barrier()
            used.clear()

        def dram(name, shape, dt=F32):
            return nc.dram_tensor(name, shape, dt, kind="Internal").ap()

        ps = ctx.enter_context(nc.psum_tensor("ps", [P, 8, 512], F32))

        mod_d = dram("mod_d", (NS + 1, MODS * D))
        q_samp_d = dram("q_samp_d", (NS, AW))
        v_samp_d = dram("v_samp_d", (NS, AW))
        qT_d = dram("qT_d", (NH, P, SEQ))
        mix_d = dram("mix_d", (NT + 1, P, KC, P))
        x1_d = dram("x1_d", (NTOK, D))
        h2_d = dram("h2_d", (NTOK + 1, D))
        h2T_d = dram("h2T_d", (NT + 1, P, KC * P))
        tok_d = dram("tok_d", (P * TOK_STRIDE, 1), I32)
        blk_d = dram("blk_d", (P, 4), I32)
        rows_d = dram("rows_d", (NBLK * P, D))

        NCONST = const_d.shape[1]
        const = place("const", 0, [P, NCONST])
        consti = place("consti", 13.5, [P, NT + 1 + TOK_STRIDE], I32)
        tbl = place("tbl", 14.75, [1, 512], I32)
        neglam = place("neglam", 16.75, [P, 1])
        subln = place("subln", 16.875, [P, 1])
        mods = place("mods", 17, [P, MODS, D])
        assert NCONST * 4 <= 13.5 * 1024

        def c(name, rows=P):
            a, b = at[name]
            return const[0:rows, a:b]

        ident = c("ident")
        B1, A1, G1, B2, A2, G2 = range(MODS)

        w_in_sb = place("w_in_sb", 139, [P, KC, IN_COLS])
        adaw = [place(f"adaw{j}", 41 + 16 * j, [P, KC, 512]) for j in range(3)]
        modr = place("modr", 89, [NS + 1, MODS * D])
        gains = place("gains", 113, [NS + 1, 4, D])
        c_all = place("c_all", 129, [NS + 1, D])
        c_act = place("c_act", 133, [NS + 1, D])
        cT = place("cT", 137, [P, KC, 16])
        lqk = place("lqk", 137.5, [P, 4, HD])
        lsum = place("lsum", 138.5, [P, 4])
        w_in_here = sem("w_in_here")
        consti_in, subln_in = sem("consti_in"), sem("subln_in")
        const_in, c_in, gain_in, lam_in = sem("const_in"), sem("c_in"), sem("gain_in"), sem("lam_in")
        ada_in = [sem(f"ada_in{j}") for j in range(3)]
        c_silu, c_sig, cT_tr, cT_here = sem("c_silu"), sem("c_sig"), sem("cT_tr"), sem("cT_here")
        ada_mm, ada_added, mods_made, mod_out, mods_in = (
            sem("ada_mm"), sem("ada_added"), sem("mods_made"), sem("mod_out"), sem("mods_in"))
        lam_dot, lam_exp, init_out, dve0 = sem("lam_dot"), sem("lam_exp"), sem("init_out"), sem("dve0")
        ada_v = ada_w[0].rearrange("(p k) n -> p k n", k=KC)
        NCH = MODS * D // 512

        with nc.Block() as block:
            @block.sync
            def _(sp):
                sp.dma_start(const[:, :], const_d).then_inc(const_in, 16)
                sp.dma_start(c_all[0:NS, :], c_sample).then_inc(c_in, 16)
                sp.dma_start(c_all[NS:NS + 1, :], c_prompt).then_inc(c_in, 16)
                for n in range(3):
                    sp.dma_start(adaw[n][:, :, :], ada_v[:, :, n * 512:(n + 1) * 512]).then_inc(ada_in[n], 16)
                sp.dma_start(modr[:, :], ada_b[0].partition_broadcast(NS + 1)).then_inc(gain_in, 16)
                for j, g in enumerate((pre_mix_g, post_mix_g, pre_ffn_g, post_ffn_g)):
                    sp.dma_start(gains[:, j, :], g[0].partition_broadcast(NS + 1)).then_inc(gain_in, 16)
                for j, l in enumerate((lq1, lk1, lq2, lk2)):
                    sp.dma_start(lqk[:, j, :], l[0].partition_broadcast(P)).then_inc(lam_in, 16)
                sp.dma_start(consti[:, :], consti_d).then_inc(consti_in, 16)
                sp.dma_start(subln[:, :], subln_g[0].rearrange("(p o) -> p o", o=1)).then_inc(subln_in, 16)
                sp.dma_start(tbl[:, 0:NS * NPG], page_table.rearrange("a b -> (a b)").rearrange(
                    "(o n) -> o n", o=1)).then_inc(consti_in, 16)
                for n in range(3, NCH):
                    sp.wait_ge(ada_mm, n - 2)
                    sp.dma_start(adaw[n % 3][:, :, :], ada_v[:, :, n * 512:(n + 1) * 512]).then_inc(ada_in[n % 3], 16)
                sp.dma_start(w_in_sb[:, :, :], w_in[0].rearrange("(p k) n -> p k n", k=KC)).then_inc(w_in_here, 16)
                sp.wait_ge(consti_in, 32)
                sp.dma_start(tok_d.rearrange("(p s) o -> p (s o)", p=P), consti[:, NT + 1:]).then_inc(init_out, 16)
                sp.wait_ge(mods_made, 1)
                sp.dma_start(mod_d, modr[:, :]).then_inc(mod_out, 16)
                sp.wait_ge(mod_out, 16)
                sp.dma_start(mods.rearrange("p m d -> p (m d)"), mod_d[NS].partition_broadcast(P)).then_inc(mods_in, 16)
                sp.wait_ge(mods_in, 16)
                sp.wait_ge(init_out, 16)

            @block.scalar
            def _(act):
                act.wait_ge(c_in, 32)
                act.activation(c_act[:, :], c_all[:, :], ACT.Sigmoid).then_inc(c_sig, 1)
                act.wait_ge(cT_tr, 1)
                act.activation(cT[:, :, 0:NS + 1], ps[:, 0, 0:KC * (NS + 1)].rearrange("p (k n) -> p k n", k=KC),
                               ACT.Copy).then_inc(cT_here, 1)
                act.wait_ge(lam_dot, 1)
                act.activation(lsum[:, 2:4], lsum[:, 0:2], ACT.Exp).then_inc(lam_exp, 1)

            @block.tensor
            def _(pe):
                pe.wait_ge(const_in, 16)
                pe.wait_ge(c_silu, 1)
                cv = c_act.rearrange("n (p k) -> n k p", k=KC)
                for k in range(KC):
                    m = pe.transpose(ps[:, 0, k * (NS + 1):(k + 1) * (NS + 1)], cv[:, k, :], c("ident", NS + 1)[:, 0:NS + 1])
                m.then_inc(cT_tr, 1)
                pe.wait_ge(cT_here, 1)
                for n in range(NCH):
                    pe.wait_ge(ada_in[n % 3], 16 * (n // 3 + 1))
                    if n >= 2:
                        pe.wait_ge(ada_added, n - 1)
                    for k in range(KC):
                        m = pe.matmul(ps[0:NS + 1, 1 + n % 2, :], cT[:, k, 0:NS + 1], adaw[n % 3][:, k, :],
                                      start=(k == 0), stop=(k == KC - 1))
                    m.then_inc(ada_mm, 1)

            @block.vector
            def _(dve):
                own = Own(dve, dve0)
                dve.wait_ge(c_sig, 1)
                dve.tensor_tensor(c_act[:, :], c_act[:, :], c_all[:, :], ALU.mult).then_inc(c_silu, 1)
                dve.wait_ge(lam_in, 64)
                for j in range(2):
                    own(dve.tensor_tensor(lqk[:, 2 * j, :], lqk[:, 2 * j, :], lqk[:, 2 * j + 1, :], ALU.mult))
                own.wait()
                dve.tensor_reduce(lsum[:, 0:2], lqk.rearrange("p (a b) d -> p a b d", b=2)[:, :, 0, :], AX_X,
                                  ALU.add).then_inc(lam_dot, 1)
                dve.wait_ge(lam_exp, 1)
                own(dve.tensor_tensor(lsum[:, 0:1], lsum[:, 3:4], lsum[:, 2:3], ALU.subtract))
                own.wait()
                own(dve.tensor_scalar(neglam[:, :], lsum[:, 0:1], -LAM_INIT, None, ALU.add))
                dve.wait_ge(subln_in, 16)
                own(dve.tensor_scalar(subln[:, :], subln[:, :], 1.0 - LAM_INIT, None, ALU.mult))
                dve.wait_ge(gain_in, 80)
                for n in range(NCH):
                    dve.wait_ge(ada_mm, n + 1)
                    col = modr[:, n * 512:(n + 1) * 512]
                    dve.tensor_tensor(col, ps[0:NS + 1, 1 + n % 2, :], col, ALU.add).then_inc(ada_added, 1)
                dve.wait_ge(ada_added, NCH)
                own.wait()
                mv = modr.rearrange("n (m d) -> n m d", m=MODS)
                for m, g, plus in ((A1, 0, 1.0), (G1, 1, 0.0), (A2, 2, 1.0), (G2, 3, 0.0)):
                    own(dve.scalar_tensor_tensor(out=mv[:, m, :], in0=mv[:, m, :], scalar=plus, in1=gains[:, g, :],
                                                 op0=ALU.add, op1=ALU.mult))
                own.wait()
                dve.sem_inc(mods_made, 1)

        kT = place("kT", 41, [P, NH, SEQ])
        v_all = place("v_all", 57, [P, NT, AW])
        xb = [place(f"xb{j}", 73 + 4 * j, [P, D]) for j in range(2)]
        hbuf = place("hbuf", 81, [P, D])
        tmp = place("tmp", 85, [P, D])
        hT = place("hT", 89, [P, KC, P])
        ra = place("ra", 93, [P, 2 * HM, HD])
        rb = place("rb", 97, [P, 2 * HM, HD])
        qk = place("qk", 101, [P, 2 * HM, HD])
        zb = [place(f"zb{j}", 105 + 2 * j, [P, AW]) for j in range(2)]
        dT = place("dT", 109, [P, NG, P])
        yT = place("yT", 111, [P, NG, P])
        qTs = place("qTs", 113, [P, NH, P])
        vs = place("vs", 115, [NS, AW])
        zc = place("zc", 117, [P, AW])
        kring = [place(f"kring{j}", 119 + 2 * j, [P, AW]) for j in range(4)]
        prod = [place(f"prod{j}", 127 + 2 * j, [P, AW]) for j in range(2)]
        qbc = [place(f"qbc{j}", 131 + 2 * j, [P, AW]) for j in range(2)]
        zs = place("zs", 135, [NS, AW])
        wp = place("wp", 137, [P, NG, P])
        sc = place("sc", 203, [P, NS, NPG + 1, HM])
        st = place("st", 207.375, [P, 16])
        ms1 = place("ms1", 41, [NS, 2, D])
        ssn = place("ssn", 207.5, [NS, HM])
        psc = st[:, 8:12]
        st_ss, st_ms, st_rt, st_r = (st[:, j:j + 1] for j in range(4))

        x_in = [sem(f"x_in{j}") for j in range(2)]
        ms_in, wp_in, zc_in, zc_z = sem("ms_in"), sem("wp_in"), sem("zc_in"), sem("zc_z")
        ms_ready, rt_ready, h_made, hT_tr, hT_here = (
            sem("ms_ready"), sem("rt_ready"), sem("h_made"), sem("hT_tr"), sem("hT_here"))
        z_proj, v_proj, qk_proj = sem("z_proj"), sem("v_proj"), sem("qk_proj")
        z_here, v_here, rope_read, qk_ready = sem("z_here"), sem("v_here"), sem("rope_read"), sem("qk_ready")
        pool_mm, dT_here, y_mm, yT_here = sem("pool_mm"), sem("dT_here"), sem("y_mm"), sem("yT_here")
        qk_tr, qkT_here = sem("qk_tr"), sem("qkT_here")
        k_out, v_out, qT_out, mix_out, misc_out = (
            sem("k_out"), sem("v_out"), sem("qT_out"), sem("mix_out"), sem("misc_out"))
        qs_ready, qs_out, sc_new, sc_new_in = sem("qs_ready"), sem("qs_out"), sem("sc_new"), sem("sc_new_in")
        k_in = [sem(f"k_in{j}") for j in range(4)]
        q_in = [sem(f"q_in{j}") for j in range(2)]
        z_zero = sem("z_zero")
        prod_made, prod_read, dve1 = sem("prod_made"), sem("prod_read"), sem("dve1")
        ck, cv = (t[0].rearrange("g p h d -> g p (h d)") for t in (cache_k, cache_v))

        with nc.Block() as block:
            @block.sync
            def _(sp):
                def load_x(s):
                    src = x_sample.rearrange("b s d -> (b s) d") if isinstance(s.n, int) and s.n == 0 else \
                        x_prompt[0][bass.ds((s.n - 1) * P, P), :]
                    rows = src.shape[0]
                    addressed(sp, src)
                    wait(sp, h_made, s.n - 1)
                    sp.dma_start(xb[s.par][0:rows, :], src).then_inc(x_in[s.par], 16)

                def load_keys(s):
                    seq = s.n - 1
                    query, = addressed(sp, q_samp_d[bass.ds(seq, 1), :].rearrange("o d -> (o d)").partition_broadcast(P))
                    sp.wait_ge(prod_made, NPG * s.n)
                    sp.dma_start(qbc[s.par][:, :], query).then_inc(q_in[s.par], 16)
                    for g in range(NPG):
                        page = sp.value_load(tbl[0:1, bass.ds(seq * NPG + g, 1)], min_val=0, max_val=cache_k.shape[1] - 1)
                        keys, = addressed(sp, ck[bass.ds(page, 1)].rearrange("o p d -> p (o d)"))
                        sp.wait_ge(prod_made, NPG * seq + g - 3 + 2 * NPG)
                        sp.dma_start(kring[g % 4][:, :], keys).then_inc(k_in[g % 4], 16)

                def stores(s):
                    k_to, k_from, q_to, y_to = addressed(
                        sp, k_prompt[0, 0][bass.ds((s.n - 1) * P, P)].rearrange("t h d -> t (h d)"),
                        qk[:, HM:, :].rearrange("p a d -> p (a d)"),
                        qT_d[:, :, bass.ds((s.n - 1) * P, P)].rearrange("h p t -> p h t"),
                        mix_d[bass.ds(s.n, 1), :, NH:, :].rearrange("o p c t -> p (o c) t"))
                    sp.wait_ge(qk_ready, s.n + 1)
                    sp.dma_start(k_to, k_from).then_inc(k_out, 16)
                    sp.wait_ge(qkT_here, s.n + 1)
                    sp.dma_start(q_to, qTs[:, :, :]).then_inc(qT_out, 16)
                    sp.wait_ge(yT_here, s.n + 1)
                    sp.dma_start(y_to, yT[:, :, :]).then_inc(mix_out, 16)

                sp.sem_inc(qT_out, 16)
                sp.dma_start(ms1[:, :, :], mod_d[0:NS, 0:2 * D].rearrange("n (m d) -> n m d", m=2)).then_inc(ms_in, 16)
                load_x(fixed(0))
                load_x(fixed(1))
                sp.dma_start(wp[:, :, :], pool_w[0].rearrange("g c f -> c g f")).then_inc(wp_in, 16)
                sp.dma_start(psc, pool_scale[0].rearrange("(g p) -> p g", p=P)).then_inc(wp_in, 16)
                sp.dma_start(zc[0:NS * BUF, :], state_pool[0].rearrange("b r c -> (b r) c")).then_inc(zc_in, 16)
                sp.dma_start(pool_sample[0, :, 0:BUF - 1, :], state_pool[0, :, 1:BUF, :]).then_inc(misc_out, 16)
                sp.wait_ge(z_here, 1)
                sp.dma_start(zc[NS * BUF:P, :], zs[:, :]).then_inc(zc_z, 16)
                sp.dma_start(pool_sample[0, :, BUF - 1, :], zs[:, :]).then_inc(misc_out, 16)
                sp.wait_ge(v_here, 1)
                sp.dma_start(v_sample[0, :, 0].rearrange("b h d -> b (h d)"), vs[:, :]).then_inc(misc_out, 16)
                sp.dma_start(v_samp_d, vs[:, :]).then_inc(misc_out, 16)
                sp.wait_ge(qk_ready, 1)
                sp.dma_start(k_sample[0, :, 0].rearrange("b h d -> b (h d)"),
                             qk[0:NS, HM:, :].rearrange("p a d -> p (a d)")).then_inc(k_out, 16)
                sp.wait_ge(qs_ready, 1)
                sp.dma_start(q_samp_d, ra[0:NS, 0:HM, :].rearrange("p a d -> p (a d)")).then_inc(qs_out, 16)
                sp.wait_ge(sc_new, 1)
                for q in range(NS):
                    sp.dma_start(sc[0:1, q, NPG, :], ssn[q:q + 1, :]).then_inc(sc_new_in, 16)
                sp.wait_ge(yT_here, 1)
                sp.dma_start(mix_d[0, :, NH:, 0:NS], yT[:, :, 0:NS]).then_inc(mix_out, 16)
                sp.wait_ge(qs_out, 16)
                with sp.Fori(0, 3) as it:
                    for s in (Step(2 * it + 1, 1, it), Step(2 * it + 2, 0, it + 1)):
                        load_x(s.next)
                        load_keys(s)
                        stores(s)
                for n in (7, 8):
                    if n < NT:
                        load_x(fixed(n + 1))
                    load_keys(fixed(n))
                    stores(fixed(n))
                sp.wait_ge(v_here, NT + 1)
                sp.dma_start(v_prompt[0, 0].rearrange("(n p) h d -> p n (h d)", p=P), v_all[:, :, :]).then_inc(v_out, 16)
                sp.dma_start(pool_prompt[0, 0], zb[0][P - BUF:P, :]).then_inc(misc_out, 16)
                for s_, v in ((k_out, 16 * (NT + 1)), (v_out, 16), (qT_out, 16 * (NT + 1)), (mix_out, 16 * (NT + 1)),
                              (misc_out, 80), (sc_new_in, 16 * NS)):
                    sp.wait_ge(s_, v)

            @block.gpsimd
            def _(pool):
                def products(s):
                    pool.wait_ge(q_in[s.par], 16 * (s.turn + s.par))
                    for g in range(NPG):
                        q = NPG * (s.n - 1) + g
                        pool.wait_ge(k_in[g % 4], (s.n - 1) * 64 + 16 * (g // 4 + 1))
                        wait(pool, prod_read, q - 1)
                        pool.tensor_tensor(prod[g % 2][:, :], kring[g % 4][:, :], qbc[s.par][:, :], ALU.mult
                                           ).then_inc(prod_made, 1)

                pool.sem_inc(prod_made, 2 * NPG)
                products(fixed(1))
                with pool.Fori(0, 3) as it:
                    for s in (Step(2 * it + 2, 0, it + 1), Step(2 * it + 3, 1, it + 1)):
                        products(s)
                products(fixed(8))

            @block.scalar
            def _(act):
                def root(s, rows=P):
                    wait(act, ms_ready, s.n + 1)
                    act.activation(st_rt[0:rows], st_ms[0:rows], ACT.Sqrt).then_inc(rt_ready, 1)

                def hT_copy(s, rows):
                    act.wait_ge(hT_tr, s.n + 1)
                    wait(act, qk_proj, s.n)
                    act.activation(hT[:, :, 0:rows], ps[:, 0:2, :].rearrange("p b (k t) -> p (b k) t", t=P)[:, :, 0:rows],
                                   ACT.Copy).then_inc(hT_here, 1)

                def z_v(s, rows, z_to, v_to):
                    act.wait_ge(z_proj, s.n + 1)
                    wait(act, pool_mm, s.n)
                    act.activation(z_to, ps[0:rows, 4, :], ACT.Copy).then_inc(z_here, 1)
                    act.wait_ge(v_proj, s.n + 1)
                    act.activation(v_to, ps[0:rows, 5, :], ACT.Copy).then_inc(v_here, 1)

                def dT_copy(s, rows):
                    act.wait_ge(pool_mm, s.n + 1)
                    wait(act, y_mm, s.n)
                    act.activation(dT[:, :, 0:rows], ps[:, 6, :].rearrange("p (g t) -> p g t", t=P)[:, :, 0:rows],
                                   ACT.Copy).then_inc(dT_here, 1)

                def qkT_copy(s):
                    act.wait_ge(qk_tr, s.n + 1)
                    wait(act, qT_out, 16 * s.n)
                    act.activation(qTs[:, :, :], ps[:, 0, :].rearrange("p (h t) -> p h t", t=P), ACT.Copy, scale=HD ** -0.5)
                    act.activation(kT[:, :, bass.ds((s.n - 1) * P, P)], ps[:, 1, :].rearrange("p (h t) -> p h t", t=P),
                                   ACT.Copy).then_inc(qkT_here, 1)

                def step(s):
                    z_v(s, P, zb[s.par][:, :], v_all[:, bass.ds(s.n - 1, 1), :].rearrange("p o d -> p (o d)"))

                act.sem_inc(qkT_here, 1)
                root(fixed(0), NS)
                hT_copy(fixed(0), NS)
                z_v(fixed(0), NS, zs[:, :], vs[:, :])
                root(fixed(1))
                hT_copy(fixed(1), P)
                dT_copy(fixed(0), NS)

                def body(s, last=False):
                    step(s)
                    if not last:
                        root(s.next)
                        hT_copy(s.next, P)
                    dT_copy(s, P)
                    qkT_copy(s)

                with act.Fori(0, 3) as it:
                    for s in (Step(2 * it + 1, 1, it), Step(2 * it + 2, 0, it + 1)):
                        body(s)
                body(fixed(7))
                body(fixed(8), last=True)

            @block.tensor
            def _(pe):
                def turn_h(s, rows):
                    pe.wait_ge(h_made, s.n + 1)
                    wait(pe, qkT_here, s.n - 1)
                    for k in range(KC):
                        m = pe.transpose(ps[:, k // 4, (k % 4) * P:(k % 4) * P + rows], hbuf[0:rows, k * P:(k + 1) * P],
                                         c("ident", rows)[:, 0:rows])
                    m.then_inc(hT_tr, 1)

                def project(s, rows):
                    pe.wait_ge(hT_here, s.n + 1)
                    for bank, col, done, free in ((4, 3 * AW, z_proj, z_here), (5, 2 * AW, v_proj, v_here),
                                                  (2, 0, None, rope_read), (3, AW, qk_proj, rope_read)):
                        wait(pe, free, s.n)
                        for k in range(KC):
                            m = pe.matmul(ps[0:rows, bank, :], hT[:, k, 0:rows], w_in_sb[:, k, col:col + AW],
                                          start=(k == 0), stop=(k == KC - 1))
                        if done is not None:
                            m.then_inc(done, 1)

                def pool_in(s, first):
                    pe.wait_ge(z_here, s.n + 1)
                    wait(pe, dT_here, s.n)
                    for g in range(NG):
                        col = slice(g * P, (g + 1) * P)
                        pe.matmul(ps[:, 6, col], zb[s.par][:, col],
                                  const[:, bass.ds(at["band"][0] + first * (NG * P) + g * P, P)], start=True, stop=False)
                        m = pe.matmul(ps[:, 6, col], zb[1 - s.par][:, col],
                                      const[:, at["band_prev"][0] + g * P:at["band_prev"][0] + (g + 1) * P],
                                      start=False, stop=True)
                    m.then_inc(pool_mm, 1)

                def pool_out(s, rows):
                    pe.wait_ge(dT_here, s.n + 1)
                    wait(pe, yT_here, s.n)
                    for g in range(NG):
                        m = pe.matmul(ps[:, 7, g * P:g * P + rows], wp[:, g, :], dT[:, g, 0:rows], start=True, stop=True)
                    m.then_inc(y_mm, 1)

                def turn_qk(s):
                    pe.wait_ge(qk_ready, s.n + 1)
                    last = s.n if isinstance(s.n, int) else 0
                    if last < NT:
                        pe.wait_ge(hT_here, s.n + 2)
                    qkf = qk.rearrange("p a d -> p (a d)")
                    for h in range(2 * NH):
                        m = pe.transpose(ps[:, h // NH, (h % NH) * P:(h % NH + 1) * P], qkf[:, h * P:(h + 1) * P], ident)
                    m.then_inc(qk_tr, 1)

                pe.sem_inc(qk_tr, 1)
                pe.wait_ge(w_in_here, 16)
                pe.wait_ge(z_zero, 1)
                pe.wait_ge(wp_in, 32)
                turn_h(fixed(0), NS)
                project(fixed(0), NS)
                turn_h(fixed(1), P)
                pe.wait_ge(zc_in, 16)
                pe.wait_ge(zc_z, 16)
                for g in range(NG):
                    m = pe.matmul(ps[:, 6, g * P:g * P + NS], zc[:, g * P:(g + 1) * P],
                                  c("band_samp")[:, g * NS:(g + 1) * NS], start=True, stop=True)
                m.then_inc(pool_mm, 1)
                pool_out(fixed(0), NS)

                def body(s, first, last=False):
                    project(s, P)
                    if not last:
                        turn_h(s.next, P)
                    pool_in(s, first)
                    turn_qk(s)
                    pool_out(s, P)

                with pe.Fori(0, 3) as it:
                    body(Step(2 * it + 1, 1, it), (it + 3) // 4)
                    body(Step(2 * it + 2, 0, it + 1), 1)
                body(fixed(7), 1)
                body(fixed(8), 1, last=True)

            @block.vector
            def _(dve):
                own = Own(dve, dve1)

                def modulate(s, rows, a1, b1):
                    x = xb[s.par][0:rows, :]
                    dve.wait_ge(x_in[s.par], 16 * (s.turn + 1))
                    wait(dve, h_made, s.n)
                    own.wait()
                    own(dve.scalar_tensor_tensor(out=tmp[0:rows, :], in0=x, scalar=1.0, in1=x, op0=ALU.mult, op1=ALU.mult,
                                                 accum_out=st_ss[0:rows]))
                    own.wait()
                    dve.tensor_scalar(st_ms[0:rows], st_ss[0:rows], 1.0 / D, EPS, ALU.mult, ALU.add).then_inc(ms_ready, 1)
                    dve.wait_ge(rt_ready, s.n + 1)
                    own(dve.reciprocal(st_r[0:rows], st_rt[0:rows]))
                    own.wait()
                    own(dve.scalar_tensor_tensor(out=tmp[0:rows, :], in0=x, scalar=st_r[0:rows], in1=a1,
                                                 op0=ALU.mult, op1=ALU.mult))
                    own.wait()
                    wait(dve, hT_tr, s.n)
                    dve.tensor_tensor(hbuf[0:rows, :].rearrange("t (k p) -> t p k", k=KC),
                                      tmp[0:rows, :].rearrange("t (p k) -> t p k", k=KC),
                                      b1.rearrange("t (p k) -> t p k", k=KC), ALU.add).then_inc(h_made, 1)

                def key_sums(s, pages):
                    for g in pages:
                        dve.wait_ge(prod_made, NPG * (s.n - 1) + g + 1 + 2 * NPG)
                        dve.tensor_reduce(sc[:, bass.ds(s.n - 1, 1), g, :].rearrange("p o m -> p (o m)"),
                                          prod[g % 2].rearrange("p (m d) -> p m d", d=HD), AX_X, ALU.add).then_inc(prod_read, 1)

                def rope(s, rows):
                    half = HD // 2
                    dve.wait_ge(qk_proj, s.n + 1)
                    own.wait()
                    src = ps[0:rows, 2:4, :].rearrange("p b (a d) -> p (b a) d", d=HD)
                    cos = const[0:rows, bass.ds(at["cos"][0] + s.n * HD, HD)].unsqueeze(1).to_broadcast([rows, 2 * HM, HD])
                    sin = [const[0:rows, bass.ds(at["sin"][0] + s.n * HD + half * j, half)].unsqueeze(1).to_broadcast(
                        [rows, 2 * HM, half]) for j in range(2)]
                    own(dve.tensor_tensor(ra[0:rows], src, cos, ALU.mult))
                    own(dve.tensor_tensor(rb[0:rows, :, 0:half], src[:, :, half:], sin[0], ALU.mult))
                    own(dve.tensor_tensor(rb[0:rows, :, half:], src[:, :, 0:half], sin[1], ALU.mult))
                    own.wait()
                    dve.sem_inc(rope_read, 1)
                    wait(dve, k_out, 16 * s.n)
                    wait(dve, qk_tr, s.n)
                    own(dve.tensor_tensor(qk[0:rows], ra[0:rows], rb[0:rows], ALU.add))
                    own.wait()
                    dve.sem_inc(qk_ready, 1)

                def pooled(s, rows):
                    dve.wait_ge(y_mm, s.n + 1)
                    wait(dve, mix_out, 16 * s.n)
                    dve.tensor_tensor(yT[:, :, 0:rows], ps[:, 7, :].rearrange("p (g t) -> p g t", t=P)[:, :, 0:rows],
                                      psc.unsqueeze(2).to_broadcast([P, NG, rows]), ALU.mult).then_inc(yT_here, 1)

                dve.memset(sc[:, :, NPG, :], NEG)
                dve.memset(zb[0][:, :], 0.0).then_inc(z_zero, 1)
                dve.wait_ge(ms_in, 16)
                modulate(fixed(0), NS, ms1[:, 1, :], ms1[:, 0, :])
                modulate(fixed(1), P, mods[:, A1, :], mods[:, B1, :])
                rope(fixed(0), NS)
                own(dve.tensor_scalar(ra[0:NS, 0:HM, :], qk[0:NS, 0:HM, :], HD ** -0.5, None, ALU.mult))
                own.wait()
                dve.sem_inc(qs_ready, 1)
                own(dve.tensor_tensor(rb[0:NS, 0:HM, :], ra[0:NS, 0:HM, :], qk[0:NS, HM:, :], ALU.mult))
                own.wait()
                dve.tensor_reduce(ssn[:, :], rb[0:NS, 0:HM, :], AX_X, ALU.add).then_inc(sc_new, 1)
                dve.wait_ge(wp_in, 32)
                pooled(fixed(0), NS)
                dve.wait_ge(qs_out, 16)

                def body(s, last=False):
                    if not last:
                        modulate(s.next, P, mods[:, A1, :], mods[:, B1, :])
                    key_sums(s, range(0, NPG // 2))
                    rope(s, P)
                    key_sums(s, range(NPG // 2, NPG))
                    pooled(s, P)

                with own.loop(3, 14) as it:
                    for s in (Step(2 * it + 1, 1, it), Step(2 * it + 2, 0, it + 1)):
                        body(s)
                body(fixed(7))
                body(fixed(8), last=True)

        exps = [[place(f"exps{j}{m}", 73 + 8 * j + 4 * m, [P, SEQ]) for m in range(2)] for j in range(2)]
        wts = [place(f"wts{j}", 89 + 4 * j, [P, SEQ]) for j in range(2)]
        wtsT = [place(f"wtsT{j}", 97 + 4 * j, [P, NT, P]) for j in range(2)]
        qz = [place(f"qz{m}", 105 + 4 * m, [P, SEQ]) for m in range(2)]
        o_h = place("o_h", 113, [P, NT, P])
        mixh = place("mixh", 117, [P, NT, P])
        vring = [place(f"vring{j}", 121 + 2 * j, [P, AW]) for j in range(8)]
        wV = place("wV", 137, [P, NS, NPG + 1, NH])
        junk = place("junk", 140, [P, P])
        vnew = [place(f"vnew{j}", 144 + 2 * j, [1, AW]) for j in range(2)]
        s2 = [place(f"s2{j}", 148 + 0.0625 * j, [P, 16]) for j in range(2)]
        so = place("so", 148.25, [P, 32])
        dm = place("dm", 148.5, [P, 4, NS * HM])
        zero = place("zero", 150, [P, P])
        oTs = place("oTs", 151, [P, NS * NH])
        od = place("od", 151.25, [NS * NH, 2, P])
        sd = place("sd", 152.5, [NS * NH, 4])
        mixs = place("mixs", 153, [P, NH, NS])
        wtmp = place("wtmp", 154, [P, NS, NPG + 1, NH])
        w_out_sb = place("w_out_sb", 160, [P, KC, D])
        w_out_here = sem("w_out_here", keep=True)
        qz_in, qz_free, zeroed = sem("qz_in"), sem("qz_free"), sem("zeroed")
        vn_in = [sem(f"vn_in{j}") for j in range(2)]
        v_in = [sem(f"v_in{j}") for j in range(8)]
        v_used, dec_mm, dec_here = sem("v_used"), sem("dec_mm"), sem("dec_here")
        s_done = [sem(f"s_done{m}") for m in range(2)]
        nmax_here = [sem(f"nmax_here{m}") for m in range(2)]
        exp_done = [sem(f"exp_done{m}") for m in range(2)]
        w_made, wt_tr, wt_here, pv_done, o_here, o_sq = (
            sem("w_made"), sem("wt_tr"), sem("wt_here"), sem("pv_done"), sem("o_here"), sem("o_sq"))
        ms2, rt2, o_scaled, oT_tr, mixh_here, mixh_out = (
            sem("ms2"), sem("rt2"), sem("o_scaled"), sem("oT_tr"), sem("mixh_here"), sem("mixh_out"))
        dmax, gmax, sc_sub, sc_exp, dsum, gsum, wv_made, dve2 = (
            sem("dmax"), sem("gmax"), sem("sc_sub"), sem("sc_exp"), sem("dsum"), sem("gsum"), sem("wv_made"), sem("dve2"))
        od_tr, od_ms, od_rt, od_made, odT_tr, mixs_here, mixs_out = (
            sem("od_tr"), sem("od_ms"), sem("od_rt"), sem("od_made"), sem("odT_tr"), sem("mixs_here"), sem("mixs_out"))
        CR_EXP, CR_W, CR_WTT, CR_WT, CR_PV, CR_O, CR_DEC, CR_DECM, CR_MIX, CR_QZ, CR_V = 1, 2, 2, 1, 2, 1, 1, 2, 1, 1, 8

        with nc.Block() as block:
            @block.sync
            def _(sp):
                sp.dma_start(w_out_sb[:, :, :], w_out[0].rearrange("(c p) n -> p c n", p=P)).then_inc(w_out_here, 16)
                sp.wait_ge(zeroed, 3)
                with sp.Fori(0, NH) as hd:
                    top, low = addressed(sp, qT_d[bass.ds(hd, 1), 0:HD, :].rearrange("o p t -> p (o t)"),
                                         qT_d[bass.ds(hd, 1), HD:P, :].rearrange("o p t -> p (o t)"))
                    sp.wait_ge(qz_free, hd + CR_QZ)
                    sp.dma_start(qz[0][0:HD, :], top).then_inc(qz_in, 16)
                    sp.dma_start(qz[1][HD:P, :], low).then_inc(qz_in, 16)
                    for j in range(2):
                        row, = addressed(sp, v_samp_d[bass.ds(2 * hd + j, 1), :])
                        sp.wait_ge(dec_mm, 2 * hd + j - 1 + CR_DECM)
                        sp.dma_start(vnew[j][:, :], row).then_inc(vn_in[j], 16)
                    for q in range(2 * NPG):
                        page = sp.value_load(tbl[0:1, bass.ds(hd * (2 * NPG) + q, 1)], min_val=0, max_val=cache_v.shape[1] - 1)
                        vals, = addressed(sp, cv[bass.ds(page, 1)].rearrange("o p d -> p (o d)"))
                        sp.wait_ge(v_used, hd * (2 * NPG) + q - 7 + CR_V)
                        sp.dma_start(vring[q % 8][:, :], vals).then_inc(v_in[q % 8], 16)
                sp.wait_ge(mixs_here, 1)
                sp.dma_start(mix_d[0, :, 0:NH, 0:NS], mixs[:, :, :]).then_inc(mixs_out, 16)
                sp.wait_ge(mixs_out, 16)

            @block.gpsimd
            def _(pool):
                pool.wait_ge(dmax, 1)
                pool.partition_all_reduce(dm[:, 1, :], dm[:, 0, :], P, RED.max).then_inc(gmax, 1)
                pool.wait_ge(dsum, 1)
                pool.partition_all_reduce(dm[:, 3, :], dm[:, 2, :], P, RED.add).then_inc(gsum, 1)

            @block.scalar
            def _(act):
                act.sem_inc(exp_done[0], CR_EXP)
                act.sem_inc(exp_done[1], CR_EXP)
                act.sem_inc(wt_here, CR_WT)
                act.sem_inc(dec_here, CR_DEC)
                act.sem_inc(mixh_here, CR_MIX)
                act.sem_inc(mixh_out, 16)
                act.wait_ge(sc_sub, 1)
                scf = sc.rearrange("p s g c -> p (s g c)")
                act.activation(scf, scf, ACT.Exp).then_inc(sc_exp, 1)

                def decoded(seq, n):
                    act.wait_ge(dec_mm, seq + 1 + CR_DECM)
                    act.activation(oTs[:, bass.ds(seq * NH, NH)], ps[:, 7, 0:NH], ACT.Copy).then_inc(dec_here, 1)

                with act.Fori(0, NH) as hd:
                    def turned(i):
                        s = hd * NT + i
                        act.wait_ge(wt_tr, s + 1 + CR_WTT)
                        act.wait_ge(pv_done, s - 1 + CR_PV)
                        act.activation(wtsT[i % 2][:, 0:i + 1, :], ps[:, 4:6, :].rearrange("p b (k t) -> p (b k) t", t=P)[:, 0:i + 1],
                                       ACT.Copy).then_inc(wt_here, 1)

                    def square(i):
                        act.wait_ge(o_here, hd * NT + i + 1 + CR_O)
                        wait(act, o_sq, hd * NT + i) if i else None
                        act.activation(junk[:, :], o_h[:, i, :], ACT.Square, accum_out=so[:, i:i + 1]).then_inc(o_sq, 1)

                    for i in range(NT):
                        s = hd * NT + i
                        if i == NT // 2:
                            decoded(2 * hd, 0)
                        for m in range(2):
                            act.wait_ge(nmax_here[m], s + 1)
                            act.wait_ge(w_made, s - 1 + CR_W)
                            act.activation(exps[i % 2][m][:, 0:(i + 1) * P],
                                           ps[:, 2 * m:2 * m + 2, :].rearrange("p b t -> p (b t)")[:, 0:(i + 1) * P], ACT.Exp,
                                           bias=s2[i % 2][:, m:m + 1], accum_out=s2[i % 2][:, 2 + m:3 + m]).then_inc(exp_done[m], 1)
                        if i >= 1:
                            turned(i - 1)
                        if i >= 2:
                            square(i - 2)
                    turned(NT - 1)
                    square(NT - 2)
                    square(NT - 1)
                    act.wait_ge(ms2, hd + 1)
                    act.activation(so[:, 16:24], so[:, 8:16], ACT.Sqrt).then_inc(rt2, 1)
                    decoded(2 * hd + 1, 1)
                    mix_to, = addressed(act, mix_d[1:NT + 1, :, bass.ds(hd, 1), :].rearrange("n p o t -> p n (o t)"))
                    act.wait_ge(oT_tr, hd + 1)
                    act.wait_ge(mixh_out, 16 * hd + 16)
                    act.activation(mixh[:, :, :], ps[:, 4:6, :].rearrange("p b (k t) -> p (b k) t", t=P), ACT.Copy,
                                   scale=subln[:, 0:1]).then_inc(mixh_here, 1)
                    act.wait_ge(mixh_here, hd + 1 + CR_MIX)
                    act.dma_start(mix_to, mixh[:, :, :]).then_inc(mixh_out, 16)
                act.wait_ge(od_ms, 1)
                act.activation(sd[:, 2:3], sd[:, 1:2], ACT.Sqrt).then_inc(od_rt, 1)
                act.wait_ge(mixh_out, 16 * NH + 16)

            @block.tensor
            def _(pe):
                pe.sem_inc(wt_tr, CR_WTT)
                pe.sem_inc(pv_done, CR_PV)
                pe.sem_inc(dec_mm, CR_DECM)
                pe.sem_inc(qz_free, CR_QZ)
                pe.sem_inc(v_used, CR_V)
                pe.sem_inc(oT_tr, 1) if False else None
                pe.wait_ge(zeroed, 3)
                pe.wait_ge(wv_made, 1)
                with pe.Fori(0, NH) as hd:
                    def scores(i):
                        s = hd * NT + i
                        if i == 0:
                            pe.wait_ge(qz_in, 32 * hd + 32)
                        for m in range(2):
                            pe.wait_ge(exp_done[m], s + CR_EXP)
                            for b in range(i // 4 + 1):
                                n = min(512, (i + 1) * P - 512 * b)
                                last = pe.matmul(ps[:, 2 * m + b, 0:n], qz[m][:, i * P:(i + 1) * P],
                                                 kT[:, bass.ds(hd, 1), 512 * b:512 * b + n].rearrange("p o t -> p (o t)"),
                                                 start=True, stop=True)
                            c0 = (i % 4) * P
                            last = pe.matmul(ps[:, 2 * m + i // 4, c0:c0 + P], ident, c("causal"), start=False, stop=True,
                                             skip_group_check=True)
                            last.then_inc(s_done[m], 1)
                        if i == NT - 1:
                            pe.wait_ge(s_done[1], hd * NT + NT)
                            pe.sem_inc(qz_free, 1)

                    def values(i):
                        for j in range(4):
                            q = 4 * i + j
                            seq, g = 2 * hd + q // NPG, q % NPG
                            if g == 0:
                                pe.wait_ge(dec_here, seq + CR_DEC)
                                pe.matmul(ps[:, 7, 0:NH], zero[:, :], zero[:, 0:NH], start=True, stop=True)
                            pe.wait_ge(v_in[q % 8], 64 * hd + 16 * (q // 8 + 1))
                            for h in range(NH):
                                last = pe.matmul(ps[:, 7, h:h + 1], vring[q % 8][:, h * P:(h + 1) * P],
                                                 wV[:, bass.ds(seq, 1), g, h:h + 1].rearrange("p o h -> p (o h)"),
                                                 start=False, stop=True, skip_group_check=True)
                            last.then_inc(v_used, 1)
                            if g == NPG - 1:
                                pe.wait_ge(vn_in[q // NPG], 16 * hd + 16)
                                for h in range(NH):
                                    last = pe.matmul(ps[:, 7, h:h + 1], vnew[q // NPG][:, h * P:(h + 1) * P],
                                                     wV[0:1, bass.ds(seq, 1), NPG, h:h + 1].rearrange("p o h -> p (o h)"),
                                                     start=False, stop=True, skip_group_check=True)
                                last.then_inc(dec_mm, 1)

                    def turn(i):
                        s = hd * NT + i
                        pe.wait_ge(w_made, s + 1 + CR_W)
                        pe.wait_ge(wt_here, s + CR_WT)
                        if i == 0:
                            pe.wait_ge(mixh_here, hd + CR_MIX)
                        for j in range(i + 1):
                            last = pe.transpose(ps[:, 4 + j // 4, (j % 4) * P:(j % 4 + 1) * P], wts[i % 2][:, j * P:(j + 1) * P], ident)
                        last.then_inc(wt_tr, 1)

                    def product(i):
                        s = hd * NT + i
                        pe.wait_ge(wt_here, s + 1 + CR_WT)
                        pe.wait_ge(o_here, s + CR_O)
                        for j in range(i + 1):
                            last = pe.matmul(ps[:, 6, 0:P], wtsT[i % 2][:, j, :], v_all[:, j, bass.ds(hd * P, P)],
                                             start=(j == 0), stop=(j == i))
                        last.then_inc(pv_done, 1)

                    for i in range(NT):
                        scores(i)
                        values(i)
                        if i >= 1:
                            turn(i - 1)
                            product(i - 1)
                    turn(NT - 1)
                    product(NT - 1)
                    pe.wait_ge(o_scaled, hd + 1)
                    for i in range(NT):
                        last = pe.transpose(ps[:, 4 + i // 4, (i % 4) * P:(i % 4 + 1) * P], o_h[:, i, :], ident)
                    last.then_inc(oT_tr, 1)
                pe.wait_ge(dec_here, NS + CR_DEC)
                pe.transpose(ps[0:NS * NH, 0, 0:P], oTs[:, :], ident).then_inc(od_tr, 1)
                pe.wait_ge(od_made, 1)
                pe.transpose(ps[:, 1, 0:NS * NH], od[:, 1, :], c("ident", NS * NH)[:, 0:NS * NH]).then_inc(odT_tr, 1)

            @block.vector
            def _(dve):
                own = Own(dve, dve2)
                dve.sem_inc(w_made, CR_W)
                dve.sem_inc(o_here, CR_O)
                dve.memset(zero[:, :], 0.0).then_inc(zeroed, 1)
                dve.memset(qz[0][:, :], 0.0).then_inc(zeroed, 1)
                dve.memset(qz[1][:, :], 0.0).then_inc(zeroed, 1)
                dmv = dm.rearrange("p a (s c) -> p a s c", s=NS)
                by_page = sc.rearrange("p s g c -> p s c g")
                dve.tensor_reduce(dmv[:, 0], by_page, AX_X, ALU.max).then_inc(dmax, 1)
                dve.wait_ge(gmax, 1)
                dve.tensor_tensor(sc[:, :, :, :], sc[:, :, :, :], dmv[:, 1].unsqueeze(2).to_broadcast([P, NS, NPG + 1, HM]),
                                  ALU.subtract).then_inc(sc_sub, 1)
                dve.wait_ge(sc_exp, 1)
                dve.tensor_reduce(dmv[:, 2], by_page, AX_X, ALU.add).then_inc(dsum, 1)
                dve.wait_ge(gsum, 1)
                own(dve.reciprocal(dm[:, 0, :], dm[:, 3, :]))
                own.wait()
                r = dm[:, 0, :].rearrange("p (s h m) -> p s h m", s=NS, m=2)
                own(dve.tensor_scalar(r[:, :, :, 1], r[:, :, :, 1], neglam[:, 0:1], None, ALU.mult))
                own.wait()
                e = sc.rearrange("p s g (h m) -> p s g h m", m=2)
                own(dve.tensor_tensor(wV[:, :, :, :], e[:, :, :, :, 0],
                                      r[:, :, :, 0].unsqueeze(2).to_broadcast([P, NS, NPG + 1, NH]), ALU.mult))
                own(dve.tensor_tensor(wtmp[:, :, :, :], e[:, :, :, :, 1],
                                      r[:, :, :, 1].unsqueeze(2).to_broadcast([P, NS, NPG + 1, NH]), ALU.mult))
                own.wait()
                dve.tensor_tensor(wV[:, :, :, :], wV[:, :, :, :], wtmp[:, :, :, :], ALU.add).then_inc(wv_made, 1)

                with own.loop(NH, 8 * 3 + 1) as hd:
                    def maxima(i):
                        s = hd * NT + i
                        for m in range(2):
                            dve.wait_ge(s_done[m], s + 1)
                            dve.tensor_reduce(s2[i % 2][:, m:m + 1],
                                              ps[:, 2 * m:2 * m + 2, :].rearrange("p b t -> p (b t)")[:, 0:(i + 1) * P], AX_X,
                                              ALU.max, negate=True).then_inc(nmax_here[m], 1)

                    def combine(i):
                        s = hd * NT + i
                        st_, k = s2[i % 2], (i + 1) * P
                        for m in range(2):
                            dve.wait_ge(exp_done[m], s + 1 + CR_EXP)
                        own(dve.reciprocal(st_[:, 4:6], st_[:, 2:4]))
                        own.wait()
                        own(dve.tensor_scalar(st_[:, 6:7], st_[:, 5:6], neglam[:, 0:1], None, ALU.mult))
                        own.wait()
                        own(dve.tensor_scalar(exps[i % 2][1][:, 0:k], exps[i % 2][1][:, 0:k], st_[:, 6:7], None, ALU.mult))
                        own.wait()
                        dve.wait_ge(wt_tr, s - 1 + CR_WTT)
                        dve.scalar_tensor_tensor(out=wts[i % 2][:, 0:k], in0=exps[i % 2][0][:, 0:k], scalar=st_[:, 4:5],
                                                 in1=exps[i % 2][1][:, 0:k], op0=ALU.mult, op1=ALU.add).then_inc(w_made, 1)

                    def o_copy(i):
                        dve.wait_ge(pv_done, hd * NT + i + 1 + CR_PV)
                        dve.tensor_copy(o_h[:, i, :], ps[:, 6, 0:P]).then_inc(o_here, 1)

                    for i in range(NT):
                        maxima(i)
                        if i >= 1:
                            combine(i - 1)
                        if i >= 2:
                            o_copy(i - 2)
                    combine(NT - 1)
                    o_copy(NT - 2)
                    o_copy(NT - 1)
                    dve.wait_ge(o_sq, hd * NT + NT)
                    dve.tensor_scalar(so[:, 8:16], so[:, 0:8], 1.0 / P, EPS, ALU.mult, ALU.add).then_inc(ms2, 1)
                    dve.wait_ge(rt2, hd + 1)
                    own(dve.reciprocal(so[:, 24:32], so[:, 16:24]))
                    own.wait()
                    dve.tensor_tensor(o_h[:, :, :], o_h[:, :, :], so[:, 24:32].unsqueeze(2).to_broadcast([P, NT, P]),
                                      ALU.mult).then_inc(o_scaled, 1)
                    dve.wait_ge(oT_tr, hd + 1)
                dve.wait_ge(od_tr, 1)
                own(dve.tensor_copy(od[:, 0, :], ps[0:NS * NH, 0, 0:P]))
                own.wait()
                own(dve.scalar_tensor_tensor(out=od[:, 1, :], in0=od[:, 0, :], scalar=1.0, in1=od[:, 0, :], op0=ALU.mult,
                                             op1=ALU.mult, accum_out=sd[:, 0:1]))
                own.wait()
                dve.tensor_scalar(sd[:, 1:2], sd[:, 0:1], 1.0 / P, EPS, ALU.mult, ALU.add).then_inc(od_ms, 1)
                dve.wait_ge(od_rt, 1)
                own(dve.reciprocal(sd[:, 3:4], sd[:, 2:3]))
                own.wait()
                dve.tensor_scalar(od[:, 1, :], od[:, 0, :], sd[:, 3:4], None, ALU.mult).then_inc(od_made, 1)
                dve.wait_ge(odT_tr, 1)
                dve.tensor_scalar(mixs[:, :, :], ps[:, 1, 0:NS * NH].rearrange("p (s h) -> p h s", h=NH), subln[:, 0:1], None,
                                  ALU.mult).then_inc(mixs_here, 1)

        free_semaphores()

        T9 = NT + 1
        mixr = [place(f"mixr{j}", 41 + 4 * j, [P, KC, P]) for j in range(2)]
        xr = [place(f"xr{j}", 49 + 4 * j, [P, D]) for j in range(2)]
        x1b = [place(f"x1b{j}", 57 + 4 * j, [P, D]) for j in range(2)]
        t3 = place("t3", 65, [P, D])
        h2b = [place(f"h2b{j}", 69 + 4 * j, [P, D]) for j in range(2)]
        h2T = [place(f"h2T{j}", 77 + 4 * j, [P, KC, P]) for j in range(2)]
        rw = place("rw", 85, [P, KC, NE])
        msamp = place("msamp", 87, [NS, 3, D])
        lg = place("lg", 99, [P, T9, NE])
        sig = place("sig", 101.5, [P, T9, NE])
        sel = place("sel", 104, [P, T9, NE])
        mask = place("mask", 106.5, [P, T9, NE])
        pairs = place("pairs", 109, [P, T9 * EG, 28])
        cmp_a = place("cmp_a", 117, [P, T9 * EG, EG])
        cmp_b = place("cmp_b", 119.5, [P, T9 * EG, EG])
        onehot = place("onehot", 122, [P, T9 * TOPK, NE])
        picked = place("picked", 140, [P, T9 * TOPK, NE])
        s3 = place("s3", 192, [P, 8])
        junk3 = place("junk3", 192.125, [P, D])
        gsc = place("gsc", 196.25, [P, T9 * EG])
        grank = place("grank", 196.75, [P, T9 * EG])
        top = place("top", 197.25, [P, T9, TOPK])
        top_i = place("top_i", 197.75, [P, T9, TOPK], U32)
        top_f = place("top_f", 198.25, [P, T9 * TOPK])
        wraw = place("wraw", 198.75, [P, T9, TOPK])
        wsum = place("wsum", 199.25, [P, 2, T9])
        dst_f = place("dst_f", 199.5, [P, T9 * TOPK])
        first_b = place("first_b", 200, [P, NE])
        first_r = place("first_r", 200.25, [P, NE])
        rbias = place("rbias", 200.5, [P, NE])
        bt = place("bt", 200.75, [P, 8])
        bt_i = place("bt_i", 200.8125, [P, 4], I32)
        nbT = place("nbT", 201, [NE, P])
        tots = place("tots", 109, [P, T9, NE])
        cntc = place("cntc", 112, [NE, P, 8])
        dst_t = place("dst_t", 202, [P, T9 * TOPK], I32)
        zrow = place("zrow", 204.5, [2, D // 2])
        route_w = place("route_w", 203, [P, T9, TOPK])
        dst_i = place("dst_i", 203.5, [P, T9 * TOPK], I32)
        addr = place("addr", 204, [P, T9 * TOPK], I32)

        m_in = [sem(f"m_in{j}") for j in range(2)]
        xr_in = [sem(f"xr_in{j}") for j in range(2)]
        rw_in, msamp_in, rb_in = sem("rw_in"), sem("msamp_in"), sem("rb_in")
        out_mm, ss_here, ms_a, rt_a, t_made, x1_made = (
            sem("out_mm"), sem("ss_here"), sem("ms_a"), sem("rt_a"), sem("t_made"), sem("x1_made"))
        ms_b, rt_b, h2_made, h2_tr, h2T_here, r_mm, lg_here = (
            sem("ms_b"), sem("rt_b"), sem("h2_made"), sem("h2_tr"), sem("h2T_here"), sem("r_mm"), sem("lg_here"))
        x1_out = [sem(f"x1_out{j}") for j in range(2)]
        h2_out = [sem(f"h2_out{j}") for j in range(2)]
        h2T_out = [sem(f"h2T_out{j}") for j in range(2)]
        sig_here, mask_made, rank_mm, nbT_made, first_mm, addr_made, bt_made, bt_out, tok_out = (
            sem("sig_here"), sem("mask_made"), sem("rank_mm"), sem("nbT_made"), sem("first_mm"), sem("addr_made"),
            sem("bt_made"), sem("bt_out"), sem("tok_out"))
        z_made, z_out, bt_in, dve3 = sem("z_made"), sem("z_out"), sem("bt_in"), sem("dve3")

        def tokens(s):
            return (SEQ, NS) if isinstance(s.n, int) and s.n == 0 else ((s.n - 1) * P, P)

        with nc.Block() as block:
            @block.sync
            def _(sp):
                def loads(s):
                    a, rows = tokens(s)
                    x_from = x_sample.rearrange("b s d -> (b s) d") if rows == NS else x_prompt[0][bass.ds(a, P), :]
                    m_from = mix_d[0, :, :, 0:NS] if rows == NS else mix_d[bass.ds(s.n, 1)].rearrange("o p c t -> p (o c) t")
                    addressed(sp, x_from, m_from)
                    wait(sp, out_mm, s.n - 1)
                    sp.dma_start(mixr[s.par][:, :, 0:rows], m_from).then_inc(m_in[s.par], 16)
                    wait(sp, x1_made, s.n - 1)
                    sp.dma_start(xr[s.par][0:rows, :], x_from).then_inc(xr_in[s.par], 16)

                def stores(s):
                    a, rows = tokens(s)
                    x1_to, h2_to = x1_d[bass.ds(a, rows), :], h2_d[bass.ds(a, rows), :]
                    hT_to = h2T_d[bass.ds(s.n, 1)].rearrange("o p (k t) -> p (o k) t", k=KC)[:, :, 0:rows]
                    addressed(sp, x1_to, h2_to, hT_to)
                    sp.wait_ge(x1_made, s.n + 1)
                    sp.dma_start(x1_to, x1b[s.par][0:rows, :]).then_inc(x1_out[s.par], 16)
                    sp.wait_ge(h2_made, s.n + 1)
                    sp.dma_start(h2_to, h2b[s.par][0:rows, :]).then_inc(h2_out[s.par], 16)
                    sp.wait_ge(h2T_here, s.n + 1)
                    sp.dma_start(hT_to, h2T[s.par][:, :, 0:rows]).then_inc(h2T_out[s.par], 16)

                for j in range(2):
                    sp.sem_inc(x1_out[j], 16)
                    sp.sem_inc(h2_out[j], 16)
                    sp.sem_inc(h2T_out[j], 16)
                loads(fixed(0))
                sp.dma_start(msamp[:, :, :], mod_d[0:NS, 2 * D:5 * D].rearrange("n (m d) -> n m d", m=3)).then_inc(msamp_in, 16)
                loads(fixed(1))
                sp.dma_start(rw[:, :, :], router_w[0].rearrange("(p k) e -> p k e", k=KC)).then_inc(rw_in, 16)
                sp.dma_start(rbias[:, :], router_bias[0].partition_broadcast(P)).then_inc(rb_in, 16)
                sp.wait_ge(z_made, 1)
                sp.dma_start(h2_d[NTOK:NTOK + 1, :].rearrange("o (a b) -> (o a) b", a=2),
                             zrow[:, :]).then_inc(z_out, 16)
                stores(fixed(0))
                with sp.Fori(0, 3) as it:
                    for s in (Step(2 * it + 1, 1, it), Step(2 * it + 2, 0, it + 1)):
                        loads(s.next)
                        stores(s)
                loads(fixed(8))
                stores(fixed(7))
                stores(fixed(8))
                for j in range(2):
                    for o in (x1_out, h2_out, h2T_out):
                        sp.wait_ge(o[j], 16 * (NT // 2 + 1 - j) + 16)
                sp.wait_ge(z_out, 16)
                sp.wait_ge(bt_made, 1)
                sp.dma_start(blk_d, bt_i[:, :]).then_inc(bt_out, 16)
                sp.wait_ge(bt_out, 16)
                sp.dma_start(tbl[:, :], blk_d.rearrange("(o b) c -> o (b c)", o=1)).then_inc(bt_in, 16)
                sp.wait_ge(bt_in, 16)

            @block.gpsimd
            def _(pool):
                pool.wait_ge(addr_made, 1)
                for t in range(T9):
                    rows = NS if t == 0 else P
                    for k in range(TOPK):
                        pool.indirect_dma_start(
                            out=tok_d[:, :], out_offset=bass.IndirectOffsetOnAxis(ap=addr[0:rows, t * TOPK + k:t * TOPK + k + 1], axis=0),
                            in_=consti[0:rows, t:t + 1], in_offset=None).then_inc(tok_out, 16)
                pool.wait_ge(tok_out, 16 * T9 * TOPK)

            @block.scalar
            def _(act):
                def body(s, rows):
                    act.wait_ge(out_mm, s.n + 1)
                    act.activation(junk3[0:rows, :], ps[0:rows, 2 * s.par:2 * s.par + 2, :].rearrange("p b n -> p (b n)"),
                                   ACT.Square, accum_out=s3[0:rows, 0:1]).then_inc(ss_here, 1)
                    act.wait_ge(ms_a, s.n + 1)
                    act.activation(s3[0:rows, 2:3], s3[0:rows, 1:2], ACT.Sqrt).then_inc(rt_a, 1)
                    act.wait_ge(ms_b, s.n + 1)
                    act.activation(s3[0:rows, 6:7], s3[0:rows, 5:6], ACT.Sqrt).then_inc(rt_b, 1)
                    act.wait_ge(h2_tr, s.n + 1)
                    wait(act, r_mm, s.n)
                    act.wait_ge(h2T_out[s.par], 16 * s.turn + 16)
                    act.activation(h2T[s.par][:, :, 0:rows], ps[:, 4:6, :].rearrange("p b (k t) -> p (b k) t", t=P)[:, :, 0:rows],
                                   ACT.Copy).then_inc(h2T_here, 1)
                    act.wait_ge(r_mm, s.n + 1)
                    act.activation(lg[0:rows, bass.ds(s.n, 1), :].rearrange("p o e -> p (o e)"), ps[0:rows, 6, 0:NE],
                                   ACT.Copy).then_inc(lg_here, 1)

                act.wait_ge(z_made, 1)
                body(fixed(0), NS)
                with act.Fori(0, NT // 2) as it:
                    for s in (Step(2 * it + 1, 1, it), Step(2 * it + 2, 0, it + 1)):
                        body(s, P)
                act.wait_ge(lg_here, T9)
                act.activation(sig[:, :, :], lg[:, :, :], ACT.Sigmoid).then_inc(sig_here, 1)

            @block.tensor
            def _(pe):
                def out(s, rows):
                    pe.wait_ge(m_in[s.par], 16 * s.turn + 16)
                    wait(pe, t_made, s.n - 1)
                    for half in range(2):
                        for k in range(KC):
                            last = pe.matmul(ps[0:rows, 2 * s.par + half, :], mixr[s.par][:, k, 0:rows],
                                             w_out_sb[:, k, 512 * half:512 * half + 512], start=(k == 0), stop=(k == KC - 1))
                    last.then_inc(out_mm, 1)

                def route(s, rows):
                    pe.wait_ge(h2_made, s.n + 1)
                    wait(pe, h2T_here, s.n)
                    for k in range(KC):
                        last = pe.transpose(ps[:, 4 + k // 4, (k % 4) * P:(k % 4) * P + rows], h2b[s.par][0:rows, k * P:(k + 1) * P],
                                            c("ident", rows)[:, 0:rows])
                    last.then_inc(h2_tr, 1)
                    pe.wait_ge(h2T_here, s.n + 1)
                    wait(pe, lg_here, s.n)
                    for k in range(KC):
                        last = pe.matmul(ps[0:rows, 6, 0:NE], h2T[s.par][:, k, 0:rows], rw[:, k, :], start=(k == 0), stop=(k == KC - 1))
                    last.then_inc(r_mm, 1)

                pe.wait_ge(w_out_here, 16)
                pe.wait_ge(rw_in, 16)
                out(fixed(0), NS)
                out(fixed(1), P)
                route(fixed(0), NS)
                with pe.Fori(0, 3) as it:
                    for s in (Step(2 * it + 1, 1, it), Step(2 * it + 2, 0, it + 1)):
                        out(s.next, P)
                        route(s, P)
                out(fixed(8), P)
                route(fixed(7), P)
                route(fixed(8), P)

                pe.wait_ge(mask_made, 1)
                for t in range(T9):
                    dst = ps[:, 0, t * NE:(t + 1) * NE] if t < NT else ps[:, 1, 0:NE]
                    pe.matmul(dst, c("before"), mask[:, t, :], start=True, stop=(t == 0))
                    for u in range(t):
                        pe.matmul(dst, c("ones"), mask[:, u, :], start=False, stop=(u == t - 1))
                for t in range(T9):
                    last = pe.matmul(ps[0:NE, 3, 0:P], mask[:, t, :], c("ones"), start=(t == 0), stop=(t == T9 - 1))
                last.then_inc(rank_mm, 1)
                pe.wait_ge(nbT_made, 1)
                pe.matmul(ps[:, 4, 0:NE], nbT[:, :], c("before", NE)[:, 0:NE], start=True, stop=True).then_inc(first_mm, 1)

            @block.vector
            def _(dve):
                own = Own(dve, dve3)

                def body(s, rows, g1, b2, a2):
                    m = ps[0:rows, 2 * s.par:2 * s.par + 2, :].rearrange("p b n -> p (b n)")
                    x1, t = x1b[s.par][0:rows, :], t3[0:rows, :]
                    dve.wait_ge(ss_here, s.n + 1)
                    dve.tensor_scalar(s3[0:rows, 1:2], s3[0:rows, 0:1], 1.0 / D, EPS, ALU.mult, ALU.add).then_inc(ms_a, 1)
                    dve.wait_ge(rt_a, s.n + 1)
                    own(dve.reciprocal(s3[0:rows, 3:4], s3[0:rows, 2:3]))
                    own.wait()
                    wait(dve, h2_made, s.n)
                    dve.scalar_tensor_tensor(out=t, in0=m, scalar=s3[0:rows, 3:4], in1=g1, op0=ALU.mult, op1=ALU.mult
                                             ).then_inc(t_made, 1)
                    dve.wait_ge(t_made, s.n + 1)
                    dve.wait_ge(xr_in[s.par], 16 * s.turn + 16)
                    dve.wait_ge(x1_out[s.par], 16 * s.turn + 16)
                    dve.tensor_tensor(x1, t, xr[s.par][0:rows, :], ALU.add).then_inc(x1_made, 1)
                    dve.wait_ge(x1_made, s.n + 1)
                    own(dve.scalar_tensor_tensor(out=t, in0=x1, scalar=1.0, in1=x1, op0=ALU.mult, op1=ALU.mult,
                                                 accum_out=s3[0:rows, 4:5]))
                    own.wait()
                    dve.tensor_scalar(s3[0:rows, 5:6], s3[0:rows, 4:5], 1.0 / D, EPS, ALU.mult, ALU.add).then_inc(ms_b, 1)
                    dve.wait_ge(rt_b, s.n + 1)
                    own(dve.reciprocal(s3[0:rows, 7:8], s3[0:rows, 6:7]))
                    own.wait()
                    own(dve.scalar_tensor_tensor(out=t, in0=x1, scalar=s3[0:rows, 7:8], in1=a2, op0=ALU.mult, op1=ALU.mult))
                    own.wait()
                    dve.wait_ge(h2_out[s.par], 16 * s.turn + 16)
                    wait(dve, h2_tr, s.n - 1 if isinstance(s.n, int) else s.n)
                    dve.tensor_tensor(h2b[s.par][0:rows, :].rearrange("t (k p) -> t p k", k=KC),
                                      t.rearrange("t (p k) -> t p k", k=KC), b2.rearrange("t (p k) -> t p k", k=KC),
                                      ALU.add).then_inc(h2_made, 1)

                own(dve.memset(lg[:, 0, :], 0.0))
                own.wait()
                dve.memset(zrow[:, :], 0.0).then_inc(z_made, 1)
                dve.wait_ge(msamp_in, 16)
                body(fixed(0), NS, msamp[:, 0, :], msamp[:, 1, :], msamp[:, 2, :])
                with own.loop(NT // 2, 8) as it:
                    for s in (Step(2 * it + 1, 1, it), Step(2 * it + 2, 0, it + 1)):
                        body(s, P, mods[:, G1, :], mods[:, B2, :], mods[:, A2, :])

                def do(ins):
                    own(ins)
                    own.wait()

                dve.wait_ge(rb_in, 16)
                dve.wait_ge(sig_here, 1)
                do(dve.tensor_tensor(sel[:, :, :], sig[:, :, :], rbias[:, :].unsqueeze(1).to_broadcast([P, T9, NE]), ALU.add))
                selg = sel.rearrange("p t (g e) -> p (t g) e", g=EG)
                at_pair = 0
                for d in range(1, EG):
                    own(dve.tensor_tensor(pairs[:, :, at_pair:at_pair + EG - d], selg[:, :, 0:EG - d], selg[:, :, d:EG], ALU.add))
                    at_pair += EG - d
                own.wait()
                do(dve.tensor_reduce(gsc[:, :], pairs[:, :, :], AX_X, ALU.max))
                gv = gsc[:, :].rearrange("p (t g) -> p t g", g=EG)
                other = gv.unsqueeze(2).to_broadcast([P, T9, EG, EG])
                this = gv.unsqueeze(3).to_broadcast([P, T9, EG, EG])
                ca, cb = (x.rearrange("p (t g) h -> p t g h", g=EG) for x in (cmp_a, cmp_b))
                own(dve.tensor_tensor(ca, other, this, ALU.is_gt))
                do(dve.tensor_tensor(cb, other, this, ALU.is_equal))
                do(dve.tensor_tensor(cmp_b.rearrange("p a h -> p (a h)").rearrange("p (t q) -> p t q", t=T9),
                                     cmp_b.rearrange("p a h -> p (a h)").rearrange("p (t q) -> p t q", t=T9),
                                     c("lower_g").unsqueeze(1).to_broadcast([P, T9, EG * EG]), ALU.mult))
                do(dve.tensor_tensor(cmp_a[:, :, :], cmp_a[:, :, :], cmp_b[:, :, :], ALU.add))
                do(dve.tensor_reduce(grank[:, :], cmp_a[:, :, :], AX_X, ALU.add))
                do(dve.tensor_scalar(grank[:, :], grank[:, :], float(TOPG) - 0.5, NEG, ALU.is_gt, ALU.mult))
                do(dve.tensor_tensor(selg, selg, grank[:, :].unsqueeze(2).to_broadcast([P, T9 * EG, EG]), ALU.add))
                for t in range(T9):
                    own(dve.max(top[:, t, :], sel[:, t, :]))
                own.wait()
                for t in range(T9):
                    own(dve.max_index(top_i[:, t, :], top[:, t, :], sel[:, t, :]))
                own.wait()
                do(dve.tensor_copy(top_f[:, :], top_i.rearrange("p t k -> p (t k)")))
                do(dve.tensor_tensor(onehot[:, :, :], top_f[:, :].unsqueeze(2).to_broadcast([P, T9 * TOPK, NE]),
                                     c("iota_e").unsqueeze(1).to_broadcast([P, T9 * TOPK, NE]), ALU.is_equal))
                oh = onehot.rearrange("p (t k) e -> p t k e", k=TOPK)
                do(dve.tensor_reduce(mask[:, :, :], onehot.rearrange("p (t k) e -> p t e k", k=TOPK), AX_X, ALU.add))
                dve.tensor_scalar(mask[:, 0, :], mask[:, 0, :], c("is_sample"), None, ALU.mult).then_inc(mask_made, 1)
                pk = picked.rearrange("p (t k) e -> p t k e", k=TOPK)
                do(dve.tensor_tensor(pk, oh, sig[:, :, :].unsqueeze(2).to_broadcast([P, T9, TOPK, NE]), ALU.mult))
                do(dve.tensor_reduce(wraw.rearrange("p t k -> p (t k)"), picked[:, :, :], AX_X, ALU.add))
                do(dve.tensor_reduce(wsum[:, 0, :], wraw[:, :, :], AX_X, ALU.add))
                do(dve.reciprocal(wsum[:, 1, :], wsum[:, 0, :]))
                do(dve.scalar_tensor_tensor(out=route_w[:, :, :], in0=wraw[:, :, :], scalar=SCALE_ROUTED,
                                            in1=wsum[:, 1, :].unsqueeze(2).to_broadcast([P, T9, TOPK]), op0=ALU.mult, op1=ALU.mult))
                dve.wait_ge(rank_mm, 1)
                do(dve.tensor_tensor(cntc[:, :, :], ps[0:NE, 3, 0:P].unsqueeze(2).to_broadcast([NE, P, 8]),
                                     c("steps_128", NE).unsqueeze(1).to_broadcast([NE, P, 8]), ALU.is_gt))
                do(dve.tensor_reduce(nbT[:, :], cntc[:, :, :], AX_X, ALU.add))
                dve.tensor_scalar(nbT[:, :], nbT[:, :], 1.0, None, ALU.add).then_inc(nbT_made, 1)
                dve.wait_ge(first_mm, 1)
                own(dve.tensor_copy(first_b[:, :], ps[:, 4, 0:NE]))
                do(dve.tensor_scalar(first_r[:, :], ps[:, 4, 0:NE], float(P), None, ALU.mult))
                do(dve.tensor_tensor(tots[:, :, :], ps[:, 0:2, :].rearrange("p b n -> p (b n)")[:, 0:T9 * NE].rearrange(
                    "p (t e) -> p t e", e=NE), first_r[:, :].unsqueeze(1).to_broadcast([P, T9, NE]), ALU.add))
                do(dve.tensor_tensor(pk, oh, tots[:, :, :].unsqueeze(2).to_broadcast([P, T9, TOPK, NE]), ALU.mult))
                do(dve.tensor_reduce(dst_f[:, :], picked[:, :, :], AX_X, ALU.add))
                do(dve.tensor_copy(dst_i[:, :], dst_f[:, :]))
                own(dve.tensor_scalar(addr[:, :], dst_i[:, :], P - 1, 8, ALU.bitwise_and, ALU.logical_shift_left))
                do(dve.tensor_scalar(dst_t[:, :], dst_i[:, :], 7, None, ALU.logical_shift_right))
                dve.tensor_tensor(addr[:, :], addr[:, :], dst_t[:, :], ALU.bitwise_or).then_inc(addr_made, 1)
                own(dve.tensor_scalar(sel[:, 0, :], first_b[:, :], c("block_id"), None, ALU.is_le))
                do(dve.tensor_scalar(sel[:, 1, :], first_b[:, :], c("block_id"), None, ALU.is_equal))
                own(dve.tensor_reduce(bt[:, 4:5], sel[:, 0, :], AX_X, ALU.add))
                do(dve.tensor_reduce(bt[:, 2:3], sel[:, 1, :], AX_X, ALU.add))
                do(dve.tensor_scalar(bt[:, 0:1], bt[:, 4:5], -1.0, None, ALU.add))
                do(dve.tensor_scalar(sel[:, 2, 0:NE // SLOTS], c("steps_3"), bt[:, 0:1], None, ALU.is_le))
                do(dve.tensor_reduce(bt[:, 5:6], sel[:, 2, 0:NE // SLOTS], AX_X, ALU.add))
                own(dve.memset(bt[:, 3:4], 0.0))
                do(dve.scalar_tensor_tensor(out=bt[:, 1:2], in0=bt[:, 5:6], scalar=-float(SLOTS), in1=bt[:, 0:1],
                                            op0=ALU.mult, op1=ALU.add))
                dve.tensor_copy(bt_i[:, :], bt[:, 0:4]).then_inc(bt_made, 1)

        free_semaphores()

        w_gu = place("w_gu", 41, [P, SLOTS, 2, KC * F])
        w_dn = place("w_dn", 89, [P, SLOTS, FC * D])
        xg = [place(f"xg{j}", 113 + 4 * j, [P, D]) for j in range(2)]
        xT = [place(f"xT{j}", 121 + 4 * j, [P, KC, P]) for j in range(2)]
        sg = [place(f"sg{j}", 129 + j, [P, F]) for j in range(2)]
        hb = [place(f"hb{j}", 131 + j, [P, F]) for j in range(2)]
        hT = [place(f"hT{j}", 133 + j, [P, FC, P]) for j in range(2)]
        yb = [place(f"yb{j}", 135 + 4 * j, [P, D]) for j in range(2)]
        tokb = place("tokb", 143, [P, NBLK + 2], I32)
        idx = [place(f"idx{j}", 143.75 + j / 16, [P, 1], I32) for j in range(2)]
        tokb_in = sem("tokb_in")
        we_in = [sem(f"we_in{j}") for j in range(2)]
        xg_in = [sem(f"xg_in{j}") for j in range(2)]
        rows_out = [sem(f"rows_out{j}") for j in range(2)]
        x_tr, xT_here, gu_mm, sg_here, hb_made, h_tr, hbT_here, dn_mm, y_here, idx_here = (
            sem("x_tr"), sem("xT_here"), sem("gu_mm"), sem("sg_here"), sem("hb_made"), sem("h_tr"), sem("hbT_here"),
            sem("dn_mm"), sem("y_here"), sem("idx_here"))
        dve4, pool4 = sem("dve4"), sem("pool4")
        WE = 48
        CR_DN = SLOTS
        CR = 2

        with nc.Block() as block:
            @block.sync
            def _(sp):
                sp.sem_inc(dn_mm, CR_DN)
                for j in range(2):
                    sp.sem_inc(we_in[j], WE)
                sp.dma_start(tokb[:, :], tok_d.rearrange("(p s) o -> p (s o)", p=P)[:, 0:NBLK + 2]).then_inc(tokb_in, 16)
                with sp.Fori(0, NBLK // 2) as it:
                    for j in range(2):
                        b = 2 * it + j
                        e = sp.value_load(tbl[0:1, bass.ds(b * 4, 1)], min_val=0, max_val=NE - 1)
                        slot = sp.value_load(tbl[0:1, bass.ds(b * 4 + 1, 1)], min_val=0, max_val=SLOTS - 1)
                        new = sp.value_load(tbl[0:1, bass.ds(b * 4 + 2, 1)], min_val=0, max_val=1)
                        computed = sp.lower_val(b + 1)
                        sp.wait_ge(we_in[j], WE * (it + 1))
                        sp.wait_ge(dn_mm, computed)
                        for n, w in enumerate((ew_gate, ew_up)):
                            sp.dma_start(w_gu[:, bass.ds(slot, 1), n, :].rearrange("p o f -> p (o f)"),
                                         w[0][bass.ds(e, 1)].rearrange("o (p k) f -> p (o k f)", k=KC),
                                         cond=new).then_inc(we_in[j], 16)
                        sp.dma_start(w_dn[:, bass.ds(slot, 1), :].rearrange("p o f -> p (o f)"),
                                     ew_down[0][bass.ds(e, 1)].rearrange("o (p c) n -> p (o c n)", c=FC),
                                     cond=new).then_inc(we_in[j], 16)
                for j in range(2):
                    sp.wait_ge(we_in[j], WE * (NBLK // 2 + 1))

            @block.gpsimd
            def _(pool):
                own = Own(pool, pool4)
                pool.sem_inc(x_tr, CR)
                pool.wait_ge(tokb_in, 16)
                with own.loop(NBLK // 2 + 1, 2) as it:
                    for j in range(2):
                        b = 2 * it + j
                        pool.wait_ge(x_tr, b + 1)
                        own(pool.tensor_copy(idx[j][:, :], tokb[:, bass.ds(b, 1)]))
                        own.wait()
                        pool.sem_inc(idx_here, 1)
                        pool.indirect_dma_start(out=xg[j][:, :], out_offset=None, in_=h2_d[:, :],
                                                in_offset=bass.IndirectOffsetOnAxis(ap=idx[j][:, 0:1], axis=0)
                                                ).then_inc(xg_in[j], 16)

            @block.scalar
            def _(act):
                for j in range(2):
                    act.sem_inc(rows_out[j], 16)
                act.sem_inc(hb_made, CR)
                with act.Fori(0, NBLK // 2) as it:
                    for j in range(2):
                        b = 2 * it + j
                        act.wait_ge(gu_mm, b + 1)
                        act.wait_ge(hb_made, b + 1)
                        act.activation(sg[j][:, :], ps[:, 2 + j, 0:F], ACT.Sigmoid).then_inc(sg_here, 1)
                    for j in range(2):
                        b = 2 * it + j
                        act.wait_ge(dn_mm, b + 1 + CR_DN)
                        act.wait_ge(rows_out[j], 16 * it + 16)
                        act.activation(yb[j][:, :], ps[:, 4 + 2 * j:6 + 2 * j, :].rearrange("p b n -> p (b n)"),
                                       ACT.Copy).then_inc(y_here, 1)
                        act.wait_ge(y_here, b + 1 + CR)
                        act.dma_start(rows_d[bass.ds(b * P, P), :], yb[j][:, :]).then_inc(rows_out[j], 16)
                for j in range(2):
                    act.wait_ge(rows_out[j], 16 * (NBLK // 2) + 16)

            @block.tensor
            def _(pe):
                def turn(b, it, j):
                    pe.wait_ge(xg_in[j], 16 * it + 16)
                    wait(pe, xT_here, b)
                    for k in range(KC):
                        last = pe.transpose(ps[:, k // 4, (k % 4) * P:(k % 4 + 1) * P], xg[j][:, k * P:(k + 1) * P], ident)
                    last.then_inc(x_tr, 1)

                def gate_up(b, it, j, slot):
                    pe.wait_ge(we_in[j], WE * (it + 2))
                    pe.wait_ge(xT_here, b + 1)
                    pe.wait_ge(hbT_here, b + 1)
                    for k in range(KC):
                        last = pe.matmul(ps[:, 2 + j, :].rearrange("p (a f) -> p a f", a=2), xT[j][:, k, :],
                                         w_gu[:, bass.ds(slot, 1), :, k * F:(k + 1) * F].rearrange("p o a f -> p (o a) f"),
                                         start=(k == 0), stop=(k == KC - 1))
                    last.then_inc(gu_mm, 1)

                def turn_h(b, j):
                    pe.wait_ge(hb_made, b + 1 + CR)
                    for ch in range(FC):
                        last = pe.transpose(ps[:, 2 + j, ch * P:(ch + 1) * P],
                                            hb[j].rearrange("t (p c) -> t c p", c=FC)[:, ch, :], ident)
                    last.then_inc(h_tr, 1)

                def down(b, j, slot):
                    pe.wait_ge(hbT_here, b + 1 + CR)
                    pe.wait_ge(y_here, b + 1)
                    for half in range(2):
                        for ch in range(FC):
                            last = pe.matmul(ps[:, 4 + 2 * j + half, :], hT[j][:, ch, :],
                                             w_dn[:, bass.ds(slot, 1), ch * D + 512 * half:ch * D + 512 * half + 512],
                                             start=(ch == 0), stop=(ch == FC - 1))
                    last.then_inc(dn_mm, 1)

                pe.sem_inc(y_here, CR)
                for b in range(2):
                    turn(b, 0, b)
                with pe.Fori(0, NBLK // 2) as it:
                    slots = [pe.value_load(tbl[0:1, bass.ds((2 * it + j) * 4 + 1, 1)], min_val=0, max_val=SLOTS - 1)
                             for j in range(2)]
                    for j in range(2):
                        gate_up(2 * it + j, it, j, slots[j])
                    for j in range(2):
                        b = 2 * it + j
                        turn_h(b, j)
                        turn(b + 2, it + 1, j)
                        down(b, j, slots[j])

            @block.vector
            def _(dve):
                own = Own(dve, dve4)

                def x_copy(b, j):
                    dve.wait_ge(x_tr, b + 1 + CR)
                    dve.wait_ge(gu_mm, b - 1)
                    dve.tensor_copy(xT[j].rearrange("p k t -> p (k t)"),
                                    ps[:, 0:2, :].rearrange("p b n -> p (b n)")).then_inc(xT_here, 1)

                def swiglu(b, j):
                    dve.wait_ge(sg_here, b + 1)
                    dve.wait_ge(h_tr, b + 1)
                    own(dve.tensor_tensor(sg[j][:, :], sg[j][:, :], ps[:, 2 + j, 0:F], ALU.mult))
                    own.wait()
                    dve.tensor_tensor(hb[j][:, :], sg[j][:, :], ps[:, 2 + j, F:2 * F], ALU.mult).then_inc(hb_made, 1)

                def h_copy(b, j):
                    dve.wait_ge(h_tr, b + 1 + CR)
                    dve.wait_ge(dn_mm, b + 2)
                    dve.tensor_copy(hT[j].rearrange("p c t -> p (c t)"), ps[:, 2 + j, 0:F]).then_inc(hbT_here, 1)

                dve.sem_inc(hbT_here, CR)
                dve.sem_inc(h_tr, CR)
                for b in range(2):
                    dve.wait_ge(x_tr, b + 1 + CR)
                    dve.tensor_copy(xT[b].rearrange("p k t -> p (k t)"),
                                    ps[:, 0:2, :].rearrange("p b n -> p (b n)")).then_inc(xT_here, 1)
                with own.loop(NBLK // 2, 2) as it:
                    b0, b1 = 2 * it, 2 * it + 1
                    swiglu(b0, 0)
                    h_copy(b0, 0)
                    swiglu(b1, 1)
                    x_copy(b0 + 2, 0)
                    h_copy(b1, 1)
                    x_copy(b1 + 2, 1)

        s_gu = place("s_gu", 41, [P, 2, KC * F])
        s_dn = place("s_dn", 57, [P, FC, D])
        rk = [place(f"rk{j}", 65 + 32 * j, [P, TOPK, D]) for j in range(2)]
        hx = [place(f"hx{j}", 129 + 4 * j, [P, KC, P]) for j in range(2)]
        xr5 = [place(f"xr5_{j}", 137 + 4 * j, [P, D]) for j in range(2)]
        h5 = place("h5", 145, [P, F])
        sg5 = place("sg5", 146, [P, F])
        hT5 = place("hT5", 147, [P, FC, P])
        acc = [place(f"acc{j}", 148 + 4 * j, [P, D]) for j in range(2)]
        g2s = place("g2s", 156, [NS, D])
        junk5 = place("junk5", 160, [P, D])
        s5 = place("s5", 164, [P, 8])
        wk = place("wk", 164.25, [P, TOPK])
        didx = [place(f"didx{j}", 164.5 + j / 8, [P, TOPK], I32) for j in range(2)]
        sw_in, g2s_in = sem("sw_in"), sem("g2s_in")
        hx_in = [sem(f"hx_in{j}") for j in range(2)]
        xr5_in = [sem(f"xr5_in{j}") for j in range(2)]
        rk_in = [sem(f"rk_in{j}") for j in range(2)]
        y_out = [sem(f"y_out{j}") for j in range(2)]
        gu5, sg5_here, h5_made, h5_tr, hT5_here, dn5, summed, ss5, ms5, rt5, y_made, didx_here = (
            sem("gu5"), sem("sg5_here"), sem("h5_made"), sem("h5_tr"), sem("hT5_here"), sem("dn5"), sem("summed"),
            sem("ss5"), sem("ms5"), sem("rt5"), sem("y_made"), sem("didx_here"))
        dn5_read, dve5, pool5 = sem("dn5_read"), sem("dve5"), sem("pool5")

        with nc.Block() as block:
            @block.sync
            def _(sp):
                def loads(s):
                    a, rows = tokens(s)
                    h_from = h2T_d[bass.ds(s.n, 1)].rearrange("o p (k t) -> p (o k) t", k=KC)[:, :, 0:rows]
                    x_from = x1_d[bass.ds(a, rows), :]
                    addressed(sp, h_from, x_from)
                    wait(sp, gu5, s.n - 1)
                    sp.dma_start(hx[s.par][:, :, 0:rows], h_from).then_inc(hx_in[s.par], 16)
                    wait(sp, y_made, s.n - 1)
                    sp.dma_start(xr5[s.par][0:rows, :], x_from).then_inc(xr5_in[s.par], 16)

                def stores(s):
                    a, rows = tokens(s)
                    y_to = y_sample.rearrange("b s d -> (b s) d") if rows == NS else y_prompt[0][bass.ds(a, P), :]
                    addressed(sp, y_to)
                    sp.wait_ge(y_made, s.n + 1)
                    sp.dma_start(y_to, acc[s.par][0:rows, :]).then_inc(y_out[s.par], 16)

                for j in range(2):
                    sp.sem_inc(y_out[j], 16)
                loads(fixed(0))
                for n, w in enumerate((sw_gate, sw_up)):
                    sp.dma_start(s_gu[:, n, :], w[0].rearrange("(p k) f -> p (k f)", k=KC)).then_inc(sw_in, 16)
                sp.dma_start(s_dn[:, :, :], sw_down[0].rearrange("(p c) n -> p c n", c=FC)).then_inc(sw_in, 16)
                sp.dma_start(g2s[:, :], mod_d[0:NS, G2 * D:(G2 + 1) * D]).then_inc(g2s_in, 16)
                loads(fixed(1))
                stores(fixed(0))
                with sp.Fori(0, 3) as it:
                    for s in (Step(2 * it + 1, 1, it), Step(2 * it + 2, 0, it + 1)):
                        loads(s.next)
                        stores(s)
                loads(fixed(8))
                stores(fixed(7))
                stores(fixed(8))
                for j in range(2):
                    sp.wait_ge(y_out[j], 16 * (NT // 2 + 1 - j) + 16)

            @block.gpsimd
            def _(pool):
                own = Own(pool, pool5)

                def gather(s, rows):
                    wait(pool, summed, s.n - 1)
                    own(pool.tensor_copy(didx[s.par][:, :], dst_i[:, bass.ds(s.n * TOPK, TOPK)]))
                    own.wait()
                    pool.sem_inc(didx_here, 1)
                    for k in range(TOPK):
                        pool.indirect_dma_start(out=rk[s.par][0:rows, k, :], out_offset=None, in_=rows_d[:, :],
                                                in_offset=bass.IndirectOffsetOnAxis(ap=didx[s.par][0:rows, k:k + 1], axis=0)
                                                ).then_inc(rk_in[s.par], 16)

                gather(fixed(0), NS)
                gather(fixed(1), P)
                gather(fixed(2), P)
                with own.loop(3, 2) as it:
                    for s in (Step(2 * it + 3, 1, it + 1), Step(2 * it + 4, 0, it + 2)):
                        gather(s, P)

            @block.scalar
            def _(act):
                def body(s, rows):
                    act.wait_ge(gu5, s.n + 1)
                    wait(act, h5_made, s.n)
                    act.activation(sg5[0:rows, :], ps[0:rows, 0, 0:F], ACT.Sigmoid).then_inc(sg5_here, 1)
                    act.wait_ge(summed, s.n + 1)
                    act.activation(junk5[0:rows, :], acc[s.par][0:rows, :], ACT.Square, accum_out=s5[0:rows, 0:1]).then_inc(ss5, 1)
                    act.wait_ge(ms5, s.n + 1)
                    act.activation(s5[0:rows, 2:3], s5[0:rows, 1:2], ACT.Sqrt).then_inc(rt5, 1)

                body(fixed(0), NS)
                with act.Fori(0, NT // 2) as it:
                    for s in (Step(2 * it + 1, 1, it), Step(2 * it + 2, 0, it + 1)):
                        body(s, P)

            @block.tensor
            def _(pe):
                def body(s, rows):
                    pe.wait_ge(hx_in[s.par], 16 * s.turn + 16)
                    wait(pe, hT5_here, s.n)
                    for k in range(KC):
                        last = pe.matmul(ps[0:rows, 0, :].rearrange("p (a f) -> p a f", a=2), hx[s.par][:, k, 0:rows],
                                         s_gu[:, :, k * F:(k + 1) * F], start=(k == 0), stop=(k == KC - 1))
                    last.then_inc(gu5, 1)
                    pe.wait_ge(h5_made, s.n + 1)
                    for ch in range(FC):
                        last = pe.transpose(ps[:, 1, ch * P:ch * P + rows], h5[0:rows, :].rearrange(
                            "t (p c) -> t c p", c=FC)[:, ch, :], c("ident", rows)[:, 0:rows])
                    last.then_inc(h5_tr, 1)
                    pe.wait_ge(hT5_here, s.n + 1)
                    wait(pe, dn5_read, s.n)
                    for half in range(2):
                        for ch in range(FC):
                            last = pe.matmul(ps[0:rows, 2 + half, :], hT5[:, ch, 0:rows],
                                             s_dn[:, ch, 512 * half:512 * half + 512], start=(ch == 0), stop=(ch == FC - 1))
                    last.then_inc(dn5, 1)

                pe.wait_ge(sw_in, 48)
                body(fixed(0), NS)
                with pe.Fori(0, NT // 2) as it:
                    for s in (Step(2 * it + 1, 1, it), Step(2 * it + 2, 0, it + 1)):
                        body(s, P)

            @block.vector
            def _(dve):
                own = Own(dve, dve5)

                def body(s, rows, g2):
                    y = acc[s.par][0:rows, :]
                    dve.wait_ge(sg5_here, s.n + 1)
                    wait(dve, h5_tr, s.n)
                    own(dve.tensor_tensor(sg5[0:rows, :], sg5[0:rows, :], ps[0:rows, 0, 0:F], ALU.mult))
                    own(dve.tensor_copy(wk[:, :], route_w[:, bass.ds(s.n, 1), :].rearrange("p o k -> p (o k)")))
                    own.wait()
                    dve.tensor_tensor(h5[0:rows, :], sg5[0:rows, :], ps[0:rows, 0, F:2 * F], ALU.mult).then_inc(h5_made, 1)
                    dve.wait_ge(h5_tr, s.n + 1)
                    wait(dve, dn5, s.n)
                    dve.tensor_copy(hT5[:, :, 0:rows], ps[:, 1, 0:FC * P].rearrange("p (c t) -> p c t", c=FC)[:, :, 0:rows]
                                    ).then_inc(hT5_here, 1)
                    dve.wait_ge(dn5, s.n + 1)
                    dve.wait_ge(rk_in[s.par], 16 * TOPK * (s.turn + 1))
                    dve.wait_ge(y_out[s.par], 16 * s.turn + 16)
                    dve.scalar_tensor_tensor(out=y, in0=rk[s.par][0:rows, 0, :], scalar=wk[0:rows, 0:1],
                                             in1=ps[0:rows, 2:4, :].rearrange("p b n -> p (b n)"), op0=ALU.mult,
                                             op1=ALU.add).then_inc(dn5_read, 1)
                    dve.wait_ge(dn5_read, s.n + 1)
                    for k in range(1, TOPK):
                        ins = dve.scalar_tensor_tensor(out=y, in0=rk[s.par][0:rows, k, :], scalar=wk[0:rows, k:k + 1], in1=y,
                                                       op0=ALU.mult, op1=ALU.add)
                        if k < TOPK - 1:
                            own(ins)
                            own.wait()
                    ins.then_inc(summed, 1)
                    dve.wait_ge(ss5, s.n + 1)
                    dve.tensor_scalar(s5[0:rows, 1:2], s5[0:rows, 0:1], 1.0 / D, EPS, ALU.mult, ALU.add).then_inc(ms5, 1)
                    dve.wait_ge(rt5, s.n + 1)
                    own(dve.reciprocal(s5[0:rows, 3:4], s5[0:rows, 2:3]))
                    own.wait()
                    own(dve.scalar_tensor_tensor(out=y, in0=y, scalar=s5[0:rows, 3:4], in1=g2, op0=ALU.mult, op1=ALU.mult))
                    own.wait()
                    dve.wait_ge(xr5_in[s.par], 16 * s.turn + 16)
                    dve.tensor_tensor(y, y, xr5[s.par][0:rows, :], ALU.add).then_inc(y_made, 1)

                dve.wait_ge(g2s_in, 16)
                body(fixed(0), NS, g2s[:, :])
                with own.loop(NT // 2, 2 * 10) as it:
                    for s in (Step(2 * it + 1, 1, it), Step(2 * it + 2, 0, it + 1)):
                        body(s, P, mods[:, G2, :])



_INS = ["x_prompt", "x_sample", "c_prompt", "c_sample", "cache_k", "cache_v", "state_pool", "page_table", "ada_w",
        "ada_b", "pre_mix_g", "post_mix_g", "pre_ffn_g", "post_ffn_g", "w_in", "w_out", "lambda_q1", "lambda_k1",
        "lambda_q2", "lambda_k2", "subln_g", "pool_w", "pool_scale", "router_w", "router_bias", "expert_w_gate",
        "expert_w_up", "expert_w_down", "shared_w_gate", "shared_w_up", "shared_w_down"]
_OUTS = [(1, SEQ, D), (NS, 1, D), (1, 1, SEQ, NH, 2 * HD), (1, 1, SEQ, NH, 2 * HD), (1, 1, BUF, NG * P),
         (1, NS, 1, NH, 2 * HD), (1, NS, 1, NH, 2 * HD), (1, NS, BUF, NG * P)]


def kernel(**inputs):
    import concourse.bacc as bacc
    from concourse.bass_utils import run_bass_kernel_spmd

    nc = bacc.Bacc("TRN2", target_bir_lowering=False, num_devices=1)
    arrays, args = {}, []
    given = {name: np.ascontiguousarray(inputs[name]) for name in _INS}
    given["const"] = constants()[0]
    given["const_int"] = int_constants()
    for name, a in given.items():
        arrays[f"in_{name}"] = a
        args.append(nc.dram_tensor(f"in_{name}", a.shape, mybir.dt.from_np(a.dtype), kind="ExternalInput").ap())
    outs = [nc.dram_tensor(f"out_{i}", shape, F32, kind="ExternalOutput").ap() for i, shape in enumerate(_OUTS)]
    build(nc, args, outs)
    r = run_bass_kernel_spmd(nc, [arrays], core_ids=[0])
    return tuple(r.results[0][f"out_{i}"] for i in range(len(_OUTS)))
```

```python
import math
from contextlib import ExitStack, contextmanager

import numpy as np

import concourse.bass as bass
from concourse import mybir

F32 = mybir.dt.float32
I32 = mybir.dt.int32
U32 = mybir.dt.uint32
ALU = mybir.AluOpType
ACT = mybir.ActivationFunctionType
AX_X = mybir.AxisListType.X
RED = bass.bass_isa.ReduceOp

P = 128
D = 1024
KC = D // P
SEQ = 1024
NT = SEQ // P
NS = 8
PAST = 2048
PAGE = 128
NPG = PAST // PAGE
NH = 4
HD = 64
HM = 2 * NH
AW = NH * 2 * HD
POOL_WINDOWS = (2, 4, 8, 16)
NG = len(POOL_WINDOWS)
BUF = max(POOL_WINDOWS) - 1
IN_COLS = 3 * AW + NG * P
NE = 64
TOPK = 8
EG = 8
TOPG = 4
F = 256
FC = F // P
SCALE_ROUTED = 2.5
EPS = 1e-6
LAM_INIT = 0.8 - 0.6 * math.exp(0.0)
NTOK = SEQ + NS
NBLK = NTOK * TOPK // P + NE
NBLK += NBLK % 2
NEG = -1e30
SLOTS = 4
EARLY = 2
W_SLOT, W_NEW, W_USED = (1, 4), (16, 32), 64
MODS = 6



def constants():
    parts, at, pos = [], {}, 0

    def put(name, a):
        nonlocal pos
        full = np.zeros((P, a.shape[1]), np.float32)
        full[:a.shape[0]] = a
        parts.append(full)
        at[name] = (pos, pos + a.shape[1])
        pos += a.shape[1]

    r = np.arange(P)
    put("ident", np.eye(P))
    put("causal", np.where(r[None, :] <= r[:, None], 0.0, NEG))
    put("before", (r[:, None] < r[None, :]).astype(np.float32))
    put("ones", np.ones((P, P)))
    half = HD // 2
    inv = (10000.0 ** (-np.arange(half) / half)).astype(np.float32)
    pos_of = np.concatenate([np.full((P, 1), PAST), np.arange(SEQ).reshape(NT, P).T], 1).astype(np.float32)
    ang = (pos_of[:, :, None] * inv.astype(np.float32)[None, None, :]).astype(np.float32).astype(np.float64)
    put("cos", np.concatenate([np.cos(ang), np.cos(ang)], 2).reshape(P, -1))
    put("sin", np.concatenate([-np.sin(ang), np.sin(ang)], 2).reshape(P, -1))
    t_in, t_out = r[:, None], r[None, :]
    first, later, prev, samp = [], [], [], []
    for w in POOL_WINDOWS:
        inside = (t_out - t_in >= 0) & (t_out - t_in < w)
        first.append(np.where(inside, 1.0 / np.minimum(t_out + 1, w), 0) - np.eye(P))
        later.append(np.where(inside, 1.0 / w, 0) - np.eye(P))
        prev.append(np.where(t_out + P - t_in < w, 1.0 / w, 0))
        s = np.zeros((P, NS))
        for q in range(NS):
            for j in range(BUF - (w - 1), BUF):
                s[q * BUF + j, q] = 1.0 / w
            s[NS * BUF + q, q] = 1.0 / w - 1.0
        samp.append(s)
    put("band", np.concatenate(first + later, 1))
    put("band_prev", np.concatenate(prev, 1))
    put("band_samp", np.concatenate(samp, 1))
    put("iota_e", np.tile(np.arange(NE), (P, 1)))
    put("lower_g", np.tile((np.arange(EG)[None, :] < np.arange(EG)[:, None]).reshape(1, -1), (P, 1)))
    put("steps_128", np.tile(P * np.arange(1, 9), (P, 1)))
    put("steps_slots", np.tile(SLOTS * np.arange(1, NE // SLOTS + 1), (P, 1)))
    put("block_id", r[:, None])
    put("iota_p", np.tile(r, (P, 1)))
    put("ids", np.stack([np.where(r < NS, SEQ + r - NTOK, 0)] + [t * P + r - NTOK for t in range(NT)], 1))
    put("eps", np.full((P, 1), EPS))
    put("is_sample", (r[:, None] < NS))
    return np.concatenate(parts, 1).astype(np.float32), at


class Step:

    def __init__(self, n, par, turn):
        self.n, self.par, self.turn = n, par, turn

    @property
    def next(self):
        return Step(self.n + 1, 1 - self.par, self.turn + self.par)

    @property
    def last(self):
        return Step(self.n - 1, 1 - self.par, self.turn - 1 + self.par)


def fixed(n):
    return Step(n, n % 2, n // 2)


def wait(eng, sem, value):
    if not isinstance(value, int) or value > 0:
        eng.wait_ge(sem, value)


def addressed(eng, *aps):
    for ap in aps:
        if not isinstance(ap.offset, int):
            eng.lower_val(ap.offset * 4)
    return aps


class Own:

    def __init__(self, eng, sem):
        self.eng, self.sem, self.base, self.n = eng, sem, 0, 0

    def __call__(self, ins):
        ins.then_inc(self.sem, 1)
        self.n += 1
        return ins

    def wait(self):
        self.eng.wait_ge(self.sem, self.base + self.n)

    @contextmanager
    def loop(self, count, per):
        start = self.base + self.n
        with self.eng.Fori(0, count) as i:
            self.base, self.n = i * per + start, 0
            yield i
            assert self.n == per, f"{self.n} steps in the loop, not {per}"
        self.base, self.n = start + count * per, 0

    @contextmanager
    def over_pairs(self, loop, per):
        start = self.base + self.n
        with loop as (it, word):
            self.base, self.n = it * per + start, 0
            yield it, word
            assert self.n == per, f"{self.n} steps in the loop, not {per}"


def build(nc, ins, outs):
    (x_prompt, x_sample, c_prompt, c_sample, cache_k, cache_v, state_pool, page_table, ada_w, ada_b,
     pre_mix_g, post_mix_g, pre_ffn_g, post_ffn_g, w_in, w_out, lq1, lk1, lq2, lk2, subln_g, pool_w,
     pool_scale, router_w, router_bias, ew_gate, ew_up, ew_down, sw_gate, sw_up, sw_down, const_d) = ins
    y_prompt, y_sample, k_prompt, v_prompt, pool_prompt, k_sample, v_sample, pool_sample = outs
    _, at = constants()
    ctx = ExitStack()
    with ctx:
        ctx.enter_context(nc.allow_non_contiguous_dma(reason="small tables"))
        base = nc.sbuf_base + (-nc.sbuf_base) % 64

        def place(name, kb, shape, dt=F32):
            return nc.alloc_sbuf_tensor_at(name, shape, dt, offset=base + int(kb * 1024))

        used = []

        def sem(name, keep=False):
            s = nc.alloc_semaphore(name)
            if not keep:
                used.append(s)
            return s

        def free_semaphores():
            nc.clear_and_free_semaphores(used)
            nc.all_engine_barrier()
            used.clear()

        def dram(name, shape, dt=F32):
            return nc.dram_tensor(name, shape, dt, kind="Internal").ap()

        ps = ctx.enter_context(nc.psum_tensor("ps", [P, 8, 512], F32))

        mod_d = dram("mod_d", (NS + 1, MODS * D))
        q_samp_d = dram("q_samp_d", (NS, AW))
        v_samp_d = dram("v_samp_d", (NS, AW))
        qT_d = dram("qT_d", (NH, P, SEQ))
        mix_d = dram("mix_d", (NT + 1, P, KC, P))
        x1_d = dram("x1_d", (NTOK, D))
        h2_d = dram("h2_d", (NTOK + 1, D))
        h2T_d = dram("h2T_d", (NT + 1, P, KC * P))
        blk_d = dram("blk_d", (P, 4), I32)
        rows_d = dram("rows_d", (NBLK * P, D))

        NCONST = const_d.shape[1]
        const = place("const", 0, [P, NCONST])
        tbl = place("tbl", 14.5, [1, 4 * P], I32)
        words = place("words", 16.5625, [1, P // 2], I32)
        neglam = place("neglam", 16.9375, [P, 1])
        subln = place("subln", 16.96875, [P, 1])
        mods = place("mods", 17, [P, MODS, D])
        assert NCONST * 4 <= 14.5 * 1024

        def c(name, rows=P):
            a, b = at[name]
            return const[0:rows, a:b]

        ident = c("ident")
        B1, A1, G1, B2, A2, G2 = range(MODS)

        w_in_sb = place("w_in_sb", 139, [P, KC, IN_COLS])
        adaw = [place(f"adaw{j}", 41 + 16 * j, [P, KC, 512]) for j in range(3)]
        modr = place("modr", 89, [NS + 1, MODS * D])
        gains = place("gains", 113, [NS + 1, 4, D])
        c_all = place("c_all", 129, [NS + 1, D])
        c_act = place("c_act", 133, [NS + 1, D])
        cT = place("cT", 137, [P, KC, 16])
        lqk = place("lqk", 137.5, [P, 4, HD])
        lsum = place("lsum", 138.5, [P, 4])
        w_in_here = sem("w_in_here")
        pages_in, subln_in = sem("pages_in"), sem("subln_in")
        const_in, c_in, gain_in, lam_in = sem("const_in"), sem("c_in"), sem("gain_in"), sem("lam_in")
        ada_in = [sem(f"ada_in{j}") for j in range(3)]
        c_silu, c_sig, cT_tr, cT_here = sem("c_silu"), sem("c_sig"), sem("cT_tr"), sem("cT_here")
        ada_mm, ada_added, mods_made, mod_out, mods_in = (
            sem("ada_mm"), sem("ada_added"), sem("mods_made"), sem("mod_out"), sem("mods_in"))
        lam_dot, lam_exp, dve0 = sem("lam_dot"), sem("lam_exp"), sem("dve0")
        ada_v = ada_w[0].rearrange("(p k) n -> p k n", k=KC)
        NCH = MODS * D // 512

        with nc.Block() as block:
            @block.sync
            def _(sp):
                sp.dma_start(const[:, :], const_d).then_inc(const_in, 16)
                sp.dma_start(c_all[0:NS, :], c_sample).then_inc(c_in, 16)
                sp.dma_start(c_all[NS:NS + 1, :], c_prompt).then_inc(c_in, 16)
                for n in range(3):
                    sp.dma_start(adaw[n][:, :, :], ada_v[:, :, n * 512:(n + 1) * 512]).then_inc(ada_in[n], 16)
                sp.dma_start(modr[:, :], ada_b[0].partition_broadcast(NS + 1)).then_inc(gain_in, 16)
                for j, g in enumerate((pre_mix_g, post_mix_g, pre_ffn_g, post_ffn_g)):
                    sp.dma_start(gains[:, j, :], g[0].partition_broadcast(NS + 1)).then_inc(gain_in, 16)
                for j, l in enumerate((lq1, lk1, lq2, lk2)):
                    sp.dma_start(lqk[:, j, :], l[0].partition_broadcast(P)).then_inc(lam_in, 16)
                sp.dma_start(subln[:, :], subln_g[0].rearrange("(p o) -> p o", o=1)).then_inc(subln_in, 16)
                sp.dma_start(tbl[:, 0:NS * NPG], page_table.rearrange("a b -> (a b)").rearrange(
                    "(o n) -> o n", o=1)).then_inc(pages_in, 16)
                for n in range(3, NCH):
                    sp.wait_ge(ada_mm, n - 2)
                    sp.dma_start(adaw[n % 3][:, :, :], ada_v[:, :, n * 512:(n + 1) * 512]).then_inc(ada_in[n % 3], 16)
                sp.dma_start(w_in_sb[:, :, :], w_in[0].rearrange("(p k) n -> p k n", k=KC)).then_inc(w_in_here, 16)
                sp.wait_ge(pages_in, 16)
                sp.wait_ge(mods_made, 1)
                sp.dma_start(mod_d, modr[:, :]).then_inc(mod_out, 16)
                sp.wait_ge(mod_out, 16)
                sp.dma_start(mods.rearrange("p m d -> p (m d)"), mod_d[NS].partition_broadcast(P)).then_inc(mods_in, 16)
                sp.wait_ge(mods_in, 16)

            @block.scalar
            def _(act):
                act.wait_ge(c_in, 32)
                act.activation(c_act[:, :], c_all[:, :], ACT.Sigmoid).then_inc(c_sig, 1)
                act.wait_ge(cT_tr, 1)
                act.activation(cT[:, :, 0:NS + 1], ps[:, 0, 0:KC * (NS + 1)].rearrange("p (k n) -> p k n", k=KC),
                               ACT.Copy).then_inc(cT_here, 1)
                act.wait_ge(lam_dot, 1)
                act.activation(lsum[:, 2:4], lsum[:, 0:2], ACT.Exp).then_inc(lam_exp, 1)

            @block.tensor
            def _(pe):
                pe.wait_ge(const_in, 16)
                pe.wait_ge(c_silu, 1)
                cv = c_act.rearrange("n (p k) -> n k p", k=KC)
                for k in range(KC):
                    m = pe.transpose(ps[:, 0, k * (NS + 1):(k + 1) * (NS + 1)], cv[:, k, :], c("ident", NS + 1)[:, 0:NS + 1])
                m.then_inc(cT_tr, 1)
                pe.wait_ge(cT_here, 1)
                for n in range(NCH):
                    pe.wait_ge(ada_in[n % 3], 16 * (n // 3 + 1))
                    if n >= 2:
                        pe.wait_ge(ada_added, n - 1)
                    for k in range(KC):
                        m = pe.matmul(ps[0:NS + 1, 1 + n % 2, :], cT[:, k, 0:NS + 1], adaw[n % 3][:, k, :],
                                      start=(k == 0), stop=(k == KC - 1))
                    m.then_inc(ada_mm, 1)

            @block.vector
            def _(dve):
                own = Own(dve, dve0)
                dve.wait_ge(c_sig, 1)
                dve.tensor_tensor(c_act[:, :], c_act[:, :], c_all[:, :], ALU.mult).then_inc(c_silu, 1)
                dve.wait_ge(lam_in, 64)
                for j in range(2):
                    own(dve.tensor_tensor(lqk[:, 2 * j, :], lqk[:, 2 * j, :], lqk[:, 2 * j + 1, :], ALU.mult))
                own.wait()
                dve.tensor_reduce(lsum[:, 0:2], lqk.rearrange("p (a b) d -> p a b d", b=2)[:, :, 0, :], AX_X,
                                  ALU.add).then_inc(lam_dot, 1)
                dve.wait_ge(lam_exp, 1)
                own(dve.tensor_tensor(lsum[:, 0:1], lsum[:, 3:4], lsum[:, 2:3], ALU.subtract))
                own.wait()
                own(dve.tensor_scalar(neglam[:, :], lsum[:, 0:1], -LAM_INIT, None, ALU.add))
                dve.wait_ge(subln_in, 16)
                own(dve.tensor_scalar(subln[:, :], subln[:, :], 1.0 - LAM_INIT, None, ALU.mult))
                dve.wait_ge(gain_in, 80)
                for n in range(NCH):
                    dve.wait_ge(ada_mm, n + 1)
                    col = modr[:, n * 512:(n + 1) * 512]
                    dve.tensor_tensor(col, ps[0:NS + 1, 1 + n % 2, :], col, ALU.add).then_inc(ada_added, 1)
                dve.wait_ge(ada_added, NCH)
                own.wait()
                mv = modr.rearrange("n (m d) -> n m d", m=MODS)
                for m, g, plus in ((A1, 0, 1.0), (G1, 1, 0.0), (A2, 2, 1.0), (G2, 3, 0.0)):
                    own(dve.scalar_tensor_tensor(out=mv[:, m, :], in0=mv[:, m, :], scalar=plus, in1=gains[:, g, :],
                                                 op0=ALU.add, op1=ALU.mult))
                own.wait()
                dve.sem_inc(mods_made, 1)

        kT = place("kT", 41, [P, NH, SEQ])
        v_all = place("v_all", 57, [P, NT, AW])
        xb = [place(f"xb{j}", 73 + 4 * j, [P, D]) for j in range(2)]
        hbuf = place("hbuf", 81, [P, D])
        tmp = place("tmp", 85, [P, D])
        hT = place("hT", 89, [P, KC, P])
        ra = place("ra", 93, [P, 2 * HM, HD])
        rb = place("rb", 97, [P, 2 * HM, HD])
        qk = place("qk", 101, [P, 2 * HM, HD])
        zb = [place(f"zb{j}", 105 + 2 * j, [P, AW]) for j in range(2)]
        dT = place("dT", 109, [P, NG, P])
        yT = place("yT", 111, [P, NG, P])
        qTs = place("qTs", 113, [P, NH, P])
        vs = place("vs", 115, [NS, AW])
        zc = place("zc", 117, [P, AW])
        kring = [place(f"kring{j}", 119 + 2 * j, [P, AW]) for j in range(4)]
        prod = [place(f"prod{j}", 127 + 2 * j, [P, AW]) for j in range(2)]
        qbc = [place(f"qbc{j}", 131 + 2 * j, [P, AW]) for j in range(2)]
        zs = place("zs", 135, [NS, AW])
        wp = place("wp", 137, [P, NG, P])
        sc = place("sc", 203, [P, NS, NPG + 1, HM])
        st = place("st", 207.375, [P, 16])
        ms1 = place("ms1", 41, [NS, 2, D])
        ssn = place("ssn", 207.5, [NS, HM])
        psc = st[:, 8:12]
        st_ss, st_ms, st_rt, st_r = (st[:, j:j + 1] for j in range(4))

        x_in = [sem(f"x_in{j}") for j in range(2)]
        ms_in, wp_in, zc_in, zc_z = sem("ms_in"), sem("wp_in"), sem("zc_in"), sem("zc_z")
        ms_ready, rt_ready, h_made, hT_tr, hT_here = (
            sem("ms_ready"), sem("rt_ready"), sem("h_made"), sem("hT_tr"), sem("hT_here"))
        z_proj, v_proj, qk_proj = sem("z_proj"), sem("v_proj"), sem("qk_proj")
        z_here, v_here, rope_read, qk_ready = sem("z_here"), sem("v_here"), sem("rope_read"), sem("qk_ready")
        pool_mm, dT_here, y_mm, yT_here = sem("pool_mm"), sem("dT_here"), sem("y_mm"), sem("yT_here")
        qk_tr, qkT_here = sem("qk_tr"), sem("qkT_here")
        k_out, v_out, qT_out, mix_out, misc_out = (
            sem("k_out"), sem("v_out"), sem("qT_out"), sem("mix_out"), sem("misc_out"))
        qs_ready, qs_out, sc_new, sc_new_in = sem("qs_ready"), sem("qs_out"), sem("sc_new"), sem("sc_new_in")
        k_in = [sem(f"k_in{j}") for j in range(4)]
        q_in = [sem(f"q_in{j}") for j in range(2)]
        z_zero = sem("z_zero")
        prod_made, prod_read, dve1 = sem("prod_made"), sem("prod_read"), sem("dve1")
        ck, cv = (t[0].rearrange("g p h d -> g p (h d)") for t in (cache_k, cache_v))

        with nc.Block() as block:
            @block.sync
            def _(sp):
                def load_x(s):
                    src = x_sample.rearrange("b s d -> (b s) d") if isinstance(s.n, int) and s.n == 0 else \
                        x_prompt[0][bass.ds((s.n - 1) * P, P), :]
                    rows = src.shape[0]
                    addressed(sp, src)
                    wait(sp, h_made, s.n - 1)
                    sp.dma_start(xb[s.par][0:rows, :], src).then_inc(x_in[s.par], 16)

                def load_keys(s):
                    seq = s.n - 1
                    query, = addressed(sp, q_samp_d[bass.ds(seq, 1), :].rearrange("o d -> (o d)").partition_broadcast(P))
                    sp.wait_ge(prod_made, NPG * s.n)
                    sp.dma_start(qbc[s.par][:, :], query).then_inc(q_in[s.par], 16)
                    for g in range(NPG):
                        page = sp.value_load(tbl[0:1, bass.ds(seq * NPG + g, 1)], min_val=0, max_val=cache_k.shape[1] - 1)
                        keys, = addressed(sp, ck[bass.ds(page, 1)].rearrange("o p d -> p (o d)"))
                        sp.wait_ge(prod_made, NPG * seq + g - 3 + 2 * NPG)
                        sp.dma_start(kring[g % 4][:, :], keys).then_inc(k_in[g % 4], 16)

                def stores(s):
                    k_to, k_from, q_to, y_to = addressed(
                        sp, k_prompt[0, 0][bass.ds((s.n - 1) * P, P)].rearrange("t h d -> t (h d)"),
                        qk[:, HM:, :].rearrange("p a d -> p (a d)"),
                        qT_d[:, :, bass.ds((s.n - 1) * P, P)].rearrange("h p t -> p h t"),
                        mix_d[bass.ds(s.n, 1), :, NH:, :].rearrange("o p c t -> p (o c) t"))
                    sp.wait_ge(qk_ready, s.n + 1)
                    sp.dma_start(k_to, k_from).then_inc(k_out, 16)
                    sp.wait_ge(qkT_here, s.n + 1)
                    sp.dma_start(q_to, qTs[:, :, :]).then_inc(qT_out, 16)
                    sp.wait_ge(yT_here, s.n + 1)
                    sp.dma_start(y_to, yT[:, :, :]).then_inc(mix_out, 16)

                sp.sem_inc(qT_out, 16)
                sp.dma_start(ms1[:, :, :], mod_d[0:NS, 0:2 * D].rearrange("n (m d) -> n m d", m=2)).then_inc(ms_in, 16)
                load_x(fixed(0))
                load_x(fixed(1))
                sp.dma_start(wp[:, :, :], pool_w[0].rearrange("g c f -> c g f")).then_inc(wp_in, 16)
                sp.dma_start(psc, pool_scale[0].rearrange("(g p) -> p g", p=P)).then_inc(wp_in, 16)
                sp.dma_start(zc[0:NS * BUF, :], state_pool[0].rearrange("b r c -> (b r) c")).then_inc(zc_in, 16)
                sp.dma_start(pool_sample[0, :, 0:BUF - 1, :], state_pool[0, :, 1:BUF, :]).then_inc(misc_out, 16)
                sp.wait_ge(z_here, 1)
                sp.dma_start(zc[NS * BUF:P, :], zs[:, :]).then_inc(zc_z, 16)
                sp.dma_start(pool_sample[0, :, BUF - 1, :], zs[:, :]).then_inc(misc_out, 16)
                sp.wait_ge(v_here, 1)
                sp.dma_start(v_sample[0, :, 0].rearrange("b h d -> b (h d)"), vs[:, :]).then_inc(misc_out, 16)
                sp.dma_start(v_samp_d, vs[:, :]).then_inc(misc_out, 16)
                sp.wait_ge(qk_ready, 1)
                sp.dma_start(k_sample[0, :, 0].rearrange("b h d -> b (h d)"),
                             qk[0:NS, HM:, :].rearrange("p a d -> p (a d)")).then_inc(k_out, 16)
                sp.wait_ge(qs_ready, 1)
                sp.dma_start(q_samp_d, ra[0:NS, 0:HM, :].rearrange("p a d -> p (a d)")).then_inc(qs_out, 16)
                sp.wait_ge(sc_new, 1)
                for q in range(NS):
                    sp.dma_start(sc[0:1, q, NPG, :], ssn[q:q + 1, :]).then_inc(sc_new_in, 16)
                sp.wait_ge(yT_here, 1)
                sp.dma_start(mix_d[0, :, NH:, 0:NS], yT[:, :, 0:NS]).then_inc(mix_out, 16)
                sp.wait_ge(qs_out, 16)
                with sp.Fori(0, 3) as it:
                    for s in (Step(2 * it + 1, 1, it), Step(2 * it + 2, 0, it + 1)):
                        load_x(s.next)
                        load_keys(s)
                        stores(s)
                for n in (7, 8):
                    if n < NT:
                        load_x(fixed(n + 1))
                    load_keys(fixed(n))
                    stores(fixed(n))
                sp.wait_ge(v_here, NT + 1)
                sp.dma_start(v_prompt[0, 0].rearrange("(n p) h d -> p n (h d)", p=P), v_all[:, :, :]).then_inc(v_out, 16)
                sp.dma_start(pool_prompt[0, 0], zb[0][P - BUF:P, :]).then_inc(misc_out, 16)
                for s_, v in ((k_out, 16 * (NT + 1)), (v_out, 16), (qT_out, 16 * (NT + 1)), (mix_out, 16 * (NT + 1)),
                              (misc_out, 80), (sc_new_in, 16 * NS)):
                    sp.wait_ge(s_, v)

            @block.gpsimd
            def _(pool):
                def products(s):
                    pool.wait_ge(q_in[s.par], 16 * (s.turn + s.par))
                    for g in range(NPG):
                        q = NPG * (s.n - 1) + g
                        pool.wait_ge(k_in[g % 4], (s.n - 1) * 64 + 16 * (g // 4 + 1))
                        wait(pool, prod_read, q - 1)
                        pool.tensor_tensor(prod[g % 2][:, :], kring[g % 4][:, :], qbc[s.par][:, :], ALU.mult
                                           ).then_inc(prod_made, 1)

                pool.sem_inc(prod_made, 2 * NPG)
                products(fixed(1))
                with pool.Fori(0, 3) as it:
                    for s in (Step(2 * it + 2, 0, it + 1), Step(2 * it + 3, 1, it + 1)):
                        products(s)
                products(fixed(8))

            @block.scalar
            def _(act):
                def root(s, rows=P):
                    wait(act, ms_ready, s.n + 1)
                    act.activation(st_rt[0:rows], st_ms[0:rows], ACT.Sqrt).then_inc(rt_ready, 1)

                def hT_copy(s, rows):
                    act.wait_ge(hT_tr, s.n + 1)
                    wait(act, qk_proj, s.n)
                    act.activation(hT[:, :, 0:rows], ps[:, 0:2, :].rearrange("p b (k t) -> p (b k) t", t=P)[:, :, 0:rows],
                                   ACT.Copy).then_inc(hT_here, 1)

                def z_v(s, rows, z_to, v_to):
                    act.wait_ge(z_proj, s.n + 1)
                    wait(act, pool_mm, s.n)
                    act.activation(z_to, ps[0:rows, 4, :], ACT.Copy).then_inc(z_here, 1)
                    act.wait_ge(v_proj, s.n + 1)
                    act.activation(v_to, ps[0:rows, 5, :], ACT.Copy).then_inc(v_here, 1)

                def dT_copy(s, rows):
                    act.wait_ge(pool_mm, s.n + 1)
                    wait(act, y_mm, s.n)
                    act.activation(dT[:, :, 0:rows], ps[:, 6, :].rearrange("p (g t) -> p g t", t=P)[:, :, 0:rows],
                                   ACT.Copy).then_inc(dT_here, 1)

                def qkT_copy(s):
                    act.wait_ge(qk_tr, s.n + 1)
                    wait(act, qT_out, 16 * s.n)
                    act.activation(qTs[:, :, :], ps[:, 0, :].rearrange("p (h t) -> p h t", t=P), ACT.Copy, scale=HD ** -0.5)
                    act.activation(kT[:, :, bass.ds((s.n - 1) * P, P)], ps[:, 1, :].rearrange("p (h t) -> p h t", t=P),
                                   ACT.Copy).then_inc(qkT_here, 1)

                def step(s):
                    z_v(s, P, zb[s.par][:, :], v_all[:, bass.ds(s.n - 1, 1), :].rearrange("p o d -> p (o d)"))

                act.sem_inc(qkT_here, 1)
                root(fixed(0), NS)
                hT_copy(fixed(0), NS)
                z_v(fixed(0), NS, zs[:, :], vs[:, :])
                root(fixed(1))
                hT_copy(fixed(1), P)
                dT_copy(fixed(0), NS)

                def body(s, last=False):
                    step(s)
                    if not last:
                        root(s.next)
                        hT_copy(s.next, P)
                    dT_copy(s, P)
                    qkT_copy(s)

                with act.Fori(0, 3) as it:
                    for s in (Step(2 * it + 1, 1, it), Step(2 * it + 2, 0, it + 1)):
                        body(s)
                body(fixed(7))
                body(fixed(8), last=True)

            @block.tensor
            def _(pe):
                def turn_h(s, rows):
                    pe.wait_ge(h_made, s.n + 1)
                    wait(pe, qkT_here, s.n - 1)
                    for k in range(KC):
                        m = pe.transpose(ps[:, k // 4, (k % 4) * P:(k % 4) * P + rows], hbuf[0:rows, k * P:(k + 1) * P],
                                         c("ident", rows)[:, 0:rows])
                    m.then_inc(hT_tr, 1)

                def project(s, rows):
                    pe.wait_ge(hT_here, s.n + 1)
                    for bank, col, done, free in ((4, 3 * AW, z_proj, z_here), (5, 2 * AW, v_proj, v_here),
                                                  (2, 0, None, rope_read), (3, AW, qk_proj, rope_read)):
                        wait(pe, free, s.n)
                        for k in range(KC):
                            m = pe.matmul(ps[0:rows, bank, :], hT[:, k, 0:rows], w_in_sb[:, k, col:col + AW],
                                          start=(k == 0), stop=(k == KC - 1))
                        if done is not None:
                            m.then_inc(done, 1)

                def pool_in(s, first):
                    pe.wait_ge(z_here, s.n + 1)
                    wait(pe, dT_here, s.n)
                    for g in range(NG):
                        col = slice(g * P, (g + 1) * P)
                        pe.matmul(ps[:, 6, col], zb[s.par][:, col],
                                  const[:, bass.ds(at["band"][0] + first * (NG * P) + g * P, P)], start=True, stop=False)
                        m = pe.matmul(ps[:, 6, col], zb[1 - s.par][:, col],
                                      const[:, at["band_prev"][0] + g * P:at["band_prev"][0] + (g + 1) * P],
                                      start=False, stop=True)
                    m.then_inc(pool_mm, 1)

                def pool_out(s, rows):
                    pe.wait_ge(dT_here, s.n + 1)
                    wait(pe, yT_here, s.n)
                    for g in range(NG):
                        m = pe.matmul(ps[:, 7, g * P:g * P + rows], wp[:, g, :], dT[:, g, 0:rows], start=True, stop=True)
                    m.then_inc(y_mm, 1)

                def turn_qk(s):
                    pe.wait_ge(qk_ready, s.n + 1)
                    last = s.n if isinstance(s.n, int) else 0
                    if last < NT:
                        pe.wait_ge(hT_here, s.n + 2)
                    qkf = qk.rearrange("p a d -> p (a d)")
                    for h in range(2 * NH):
                        m = pe.transpose(ps[:, h // NH, (h % NH) * P:(h % NH + 1) * P], qkf[:, h * P:(h + 1) * P], ident)
                    m.then_inc(qk_tr, 1)

                pe.sem_inc(qk_tr, 1)
                pe.wait_ge(w_in_here, 16)
                pe.wait_ge(z_zero, 1)
                pe.wait_ge(wp_in, 32)
                turn_h(fixed(0), NS)
                project(fixed(0), NS)
                turn_h(fixed(1), P)
                pe.wait_ge(zc_in, 16)
                pe.wait_ge(zc_z, 16)
                for g in range(NG):
                    m = pe.matmul(ps[:, 6, g * P:g * P + NS], zc[:, g * P:(g + 1) * P],
                                  c("band_samp")[:, g * NS:(g + 1) * NS], start=True, stop=True)
                m.then_inc(pool_mm, 1)
                pool_out(fixed(0), NS)

                def body(s, first, last=False):
                    project(s, P)
                    if not last:
                        turn_h(s.next, P)
                    pool_in(s, first)
                    turn_qk(s)
                    pool_out(s, P)

                with pe.Fori(0, 3) as it:
                    body(Step(2 * it + 1, 1, it), (it + 3) // 4)
                    body(Step(2 * it + 2, 0, it + 1), 1)
                body(fixed(7), 1)
                body(fixed(8), 1, last=True)

            @block.vector
            def _(dve):
                own = Own(dve, dve1)

                def modulate(s, rows, a1, b1):
                    x = xb[s.par][0:rows, :]
                    dve.wait_ge(x_in[s.par], 16 * (s.turn + 1))
                    wait(dve, h_made, s.n)
                    own.wait()
                    own(dve.scalar_tensor_tensor(out=tmp[0:rows, :], in0=x, scalar=1.0, in1=x, op0=ALU.mult, op1=ALU.mult,
                                                 accum_out=st_ss[0:rows]))
                    own.wait()
                    dve.tensor_scalar(st_ms[0:rows], st_ss[0:rows], 1.0 / D, EPS, ALU.mult, ALU.add).then_inc(ms_ready, 1)
                    dve.wait_ge(rt_ready, s.n + 1)
                    own(dve.reciprocal(st_r[0:rows], st_rt[0:rows]))
                    own.wait()
                    own(dve.scalar_tensor_tensor(out=tmp[0:rows, :], in0=x, scalar=st_r[0:rows], in1=a1,
                                                 op0=ALU.mult, op1=ALU.mult))
                    own.wait()
                    wait(dve, hT_tr, s.n)
                    dve.tensor_tensor(hbuf[0:rows, :].rearrange("t (k p) -> t p k", k=KC),
                                      tmp[0:rows, :].rearrange("t (p k) -> t p k", k=KC),
                                      b1.rearrange("t (p k) -> t p k", k=KC), ALU.add).then_inc(h_made, 1)

                def key_sums(s, pages):
                    for g in pages:
                        dve.wait_ge(prod_made, NPG * (s.n - 1) + g + 1 + 2 * NPG)
                        dve.tensor_reduce(sc[:, bass.ds(s.n - 1, 1), g, :].rearrange("p o m -> p (o m)"),
                                          prod[g % 2].rearrange("p (m d) -> p m d", d=HD), AX_X, ALU.add).then_inc(prod_read, 1)

                def rope(s, rows):
                    half = HD // 2
                    dve.wait_ge(qk_proj, s.n + 1)
                    own.wait()
                    src = ps[0:rows, 2:4, :].rearrange("p b (a d) -> p (b a) d", d=HD)
                    cos = const[0:rows, bass.ds(at["cos"][0] + s.n * HD, HD)].unsqueeze(1).to_broadcast([rows, 2 * HM, HD])
                    sin = [const[0:rows, bass.ds(at["sin"][0] + s.n * HD + half * j, half)].unsqueeze(1).to_broadcast(
                        [rows, 2 * HM, half]) for j in range(2)]
                    own(dve.tensor_tensor(ra[0:rows], src, cos, ALU.mult))
                    own(dve.tensor_tensor(rb[0:rows, :, 0:half], src[:, :, half:], sin[0], ALU.mult))
                    own(dve.tensor_tensor(rb[0:rows, :, half:], src[:, :, 0:half], sin[1], ALU.mult))
                    own.wait()
                    dve.sem_inc(rope_read, 1)
                    wait(dve, k_out, 16 * s.n)
                    wait(dve, qk_tr, s.n)
                    own(dve.tensor_tensor(qk[0:rows], ra[0:rows], rb[0:rows], ALU.add))
                    own.wait()
                    dve.sem_inc(qk_ready, 1)

                def pooled(s, rows):
                    dve.wait_ge(y_mm, s.n + 1)
                    wait(dve, mix_out, 16 * s.n)
                    dve.tensor_tensor(yT[:, :, 0:rows], ps[:, 7, :].rearrange("p (g t) -> p g t", t=P)[:, :, 0:rows],
                                      psc.unsqueeze(2).to_broadcast([P, NG, rows]), ALU.mult).then_inc(yT_here, 1)

                dve.memset(sc[:, :, NPG, :], NEG)
                dve.memset(zb[0][:, :], 0.0).then_inc(z_zero, 1)
                dve.wait_ge(ms_in, 16)
                modulate(fixed(0), NS, ms1[:, 1, :], ms1[:, 0, :])
                modulate(fixed(1), P, mods[:, A1, :], mods[:, B1, :])
                rope(fixed(0), NS)
                own(dve.tensor_scalar(ra[0:NS, 0:HM, :], qk[0:NS, 0:HM, :], HD ** -0.5, None, ALU.mult))
                own.wait()
                dve.sem_inc(qs_ready, 1)
                own(dve.tensor_tensor(rb[0:NS, 0:HM, :], ra[0:NS, 0:HM, :], qk[0:NS, HM:, :], ALU.mult))
                own.wait()
                dve.tensor_reduce(ssn[:, :], rb[0:NS, 0:HM, :], AX_X, ALU.add).then_inc(sc_new, 1)
                dve.wait_ge(wp_in, 32)
                pooled(fixed(0), NS)
                dve.wait_ge(qs_out, 16)

                def body(s, last=False):
                    if not last:
                        modulate(s.next, P, mods[:, A1, :], mods[:, B1, :])
                    key_sums(s, range(0, NPG // 2))
                    rope(s, P)
                    key_sums(s, range(NPG // 2, NPG))
                    pooled(s, P)

                with own.loop(3, 14) as it:
                    for s in (Step(2 * it + 1, 1, it), Step(2 * it + 2, 0, it + 1)):
                        body(s)
                body(fixed(7))
                body(fixed(8), last=True)

        exps = [[place(f"exps{j}{m}", 73 + 8 * j + 4 * m, [P, SEQ]) for m in range(2)] for j in range(2)]
        wts = [place(f"wts{j}", 89 + 4 * j, [P, SEQ]) for j in range(2)]
        wtsT = [place(f"wtsT{j}", 97 + 4 * j, [P, NT, P]) for j in range(2)]
        qz = [place(f"qz{m}", 105 + 4 * m, [P, SEQ]) for m in range(2)]
        o_h = place("o_h", 113, [P, NT, P])
        mixh = place("mixh", 117, [P, NT, P])
        vring = [place(f"vring{j}", 121 + 2 * j, [P, AW]) for j in range(8)]
        wV = place("wV", 137, [P, NS, NPG + 1, NH])
        junk = place("junk", 140, [P, P])
        vnew = [place(f"vnew{j}", 144 + 2 * j, [1, AW]) for j in range(2)]
        s2 = [place(f"s2{j}", 148 + 0.0625 * j, [P, 16]) for j in range(2)]
        so = place("so", 148.25, [P, 32])
        dm = place("dm", 148.5, [P, 4, NS * HM])
        zero = place("zero", 150, [P, P])
        oTs = place("oTs", 151, [P, NS * NH])
        od = place("od", 151.25, [NS * NH, 2, P])
        sd = place("sd", 152.5, [NS * NH, 4])
        mixs = place("mixs", 153, [P, NH, NS])
        wtmp = place("wtmp", 154, [P, NS, NPG + 1, NH])
        w_out_sb = place("w_out_sb", 160, [P, KC, D])
        w_out_here = sem("w_out_here", keep=True)
        qz_in, qz_free, zeroed = sem("qz_in"), sem("qz_free"), sem("zeroed")
        vn_in = [sem(f"vn_in{j}") for j in range(2)]
        v_in = [sem(f"v_in{j}") for j in range(8)]
        v_used, dec_mm, dec_here = sem("v_used"), sem("dec_mm"), sem("dec_here")
        s_done = [sem(f"s_done{m}") for m in range(2)]
        nmax_here = [sem(f"nmax_here{m}") for m in range(2)]
        exp_done = [sem(f"exp_done{m}") for m in range(2)]
        w_made, wt_tr, wt_here, pv_done, o_here, o_sq = (
            sem("w_made"), sem("wt_tr"), sem("wt_here"), sem("pv_done"), sem("o_here"), sem("o_sq"))
        ms2, rt2, o_scaled, oT_tr, mixh_here, mixh_out = (
            sem("ms2"), sem("rt2"), sem("o_scaled"), sem("oT_tr"), sem("mixh_here"), sem("mixh_out"))
        dmax, gmax, sc_sub, sc_exp, dsum, gsum, wv_made, dve2 = (
            sem("dmax"), sem("gmax"), sem("sc_sub"), sem("sc_exp"), sem("dsum"), sem("gsum"), sem("wv_made"), sem("dve2"))
        od_tr, od_ms, od_rt, od_made, odT_tr, mixs_here, mixs_out = (
            sem("od_tr"), sem("od_ms"), sem("od_rt"), sem("od_made"), sem("odT_tr"), sem("mixs_here"), sem("mixs_out"))
        CR_EXP, CR_W, CR_WTT, CR_WT, CR_PV, CR_O, CR_DEC, CR_DECM, CR_MIX, CR_QZ, CR_V = 1, 2, 2, 1, 2, 1, 1, 2, 1, 1, 8

        with nc.Block() as block:
            @block.sync
            def _(sp):
                sp.dma_start(w_out_sb[:, :, :], w_out[0].rearrange("(c p) n -> p c n", p=P)).then_inc(w_out_here, 16)
                sp.wait_ge(zeroed, 3)
                with sp.Fori(0, NH) as hd:
                    top, low = addressed(sp, qT_d[bass.ds(hd, 1), 0:HD, :].rearrange("o p t -> p (o t)"),
                                         qT_d[bass.ds(hd, 1), HD:P, :].rearrange("o p t -> p (o t)"))
                    sp.wait_ge(qz_free, hd + CR_QZ)
                    sp.dma_start(qz[0][0:HD, :], top).then_inc(qz_in, 16)
                    sp.dma_start(qz[1][HD:P, :], low).then_inc(qz_in, 16)
                    for j in range(2):
                        row, = addressed(sp, v_samp_d[bass.ds(2 * hd + j, 1), :])
                        sp.wait_ge(dec_mm, 2 * hd + j - 1 + CR_DECM)
                        sp.dma_start(vnew[j][:, :], row).then_inc(vn_in[j], 16)
                    for q in range(2 * NPG):
                        page = sp.value_load(tbl[0:1, bass.ds(hd * (2 * NPG) + q, 1)], min_val=0, max_val=cache_v.shape[1] - 1)
                        vals, = addressed(sp, cv[bass.ds(page, 1)].rearrange("o p d -> p (o d)"))
                        sp.wait_ge(v_used, hd * (2 * NPG) + q - 7 + CR_V)
                        sp.dma_start(vring[q % 8][:, :], vals).then_inc(v_in[q % 8], 16)
                sp.wait_ge(mixs_here, 1)
                sp.dma_start(mix_d[0, :, 0:NH, 0:NS], mixs[:, :, :]).then_inc(mixs_out, 16)
                sp.wait_ge(mixs_out, 16)

            @block.gpsimd
            def _(pool):
                pool.wait_ge(dmax, 1)
                pool.partition_all_reduce(dm[:, 1, :], dm[:, 0, :], P, RED.max).then_inc(gmax, 1)
                pool.wait_ge(dsum, 1)
                pool.partition_all_reduce(dm[:, 3, :], dm[:, 2, :], P, RED.add).then_inc(gsum, 1)

            @block.scalar
            def _(act):
                act.sem_inc(exp_done[0], CR_EXP)
                act.sem_inc(exp_done[1], CR_EXP)
                act.sem_inc(wt_here, CR_WT)
                act.sem_inc(dec_here, CR_DEC)
                act.sem_inc(mixh_here, CR_MIX)
                act.sem_inc(mixh_out, 16)
                act.wait_ge(sc_sub, 1)
                scf = sc.rearrange("p s g c -> p (s g c)")
                act.activation(scf, scf, ACT.Exp).then_inc(sc_exp, 1)

                def decoded(seq):
                    act.wait_ge(dec_mm, seq + 1 + CR_DECM)
                    act.activation(oTs[:, bass.ds(seq * NH, NH)], ps[:, 7, 0:NH], ACT.Copy).then_inc(dec_here, 1)

                with act.Fori(0, NH) as hd:
                    def turned(i):
                        s = hd * NT + i
                        act.wait_ge(wt_tr, s + 1 + CR_WTT)
                        act.wait_ge(pv_done, s - 1 + CR_PV)
                        act.activation(wtsT[i % 2][:, 0:i + 1, :], ps[:, 4:6, :].rearrange("p b (k t) -> p (b k) t", t=P)[:, 0:i + 1],
                                       ACT.Copy).then_inc(wt_here, 1)

                    def square(i):
                        act.wait_ge(o_here, hd * NT + i + 1 + CR_O)
                        if i:
                            act.wait_ge(o_sq, hd * NT + i)
                        act.activation(junk[:, :], o_h[:, i, :], ACT.Square, accum_out=so[:, i:i + 1]).then_inc(o_sq, 1)

                    for i in range(NT):
                        s = hd * NT + i
                        if i == NT // 2:
                            decoded(2 * hd)
                        for m in range(2):
                            act.wait_ge(nmax_here[m], s + 1)
                            act.wait_ge(w_made, s - 1 + CR_W)
                            act.activation(exps[i % 2][m][:, 0:(i + 1) * P],
                                           ps[:, 2 * m:2 * m + 2, :].rearrange("p b t -> p (b t)")[:, 0:(i + 1) * P], ACT.Exp,
                                           bias=s2[i % 2][:, m:m + 1], accum_out=s2[i % 2][:, 2 + m:3 + m]).then_inc(exp_done[m], 1)
                        if i >= 1:
                            turned(i - 1)
                        if i >= 2:
                            square(i - 2)
                    turned(NT - 1)
                    square(NT - 2)
                    square(NT - 1)
                    act.wait_ge(ms2, hd + 1)
                    act.activation(so[:, 16:24], so[:, 8:16], ACT.Sqrt).then_inc(rt2, 1)
                    decoded(2 * hd + 1)
                    mix_to, = addressed(act, mix_d[1:NT + 1, :, bass.ds(hd, 1), :].rearrange("n p o t -> p n (o t)"))
                    act.wait_ge(oT_tr, hd + 1)
                    act.wait_ge(mixh_out, 16 * hd + 16)
                    act.activation(mixh[:, :, :], ps[:, 4:6, :].rearrange("p b (k t) -> p (b k) t", t=P), ACT.Copy,
                                   scale=subln[:, 0:1]).then_inc(mixh_here, 1)
                    act.wait_ge(mixh_here, hd + 1 + CR_MIX)
                    act.dma_start(mix_to, mixh[:, :, :]).then_inc(mixh_out, 16)
                act.wait_ge(od_ms, 1)
                act.activation(sd[:, 2:3], sd[:, 1:2], ACT.Sqrt).then_inc(od_rt, 1)
                act.wait_ge(mixh_out, 16 * NH + 16)

            @block.tensor
            def _(pe):
                pe.sem_inc(wt_tr, CR_WTT)
                pe.sem_inc(pv_done, CR_PV)
                pe.sem_inc(dec_mm, CR_DECM)
                pe.sem_inc(qz_free, CR_QZ)
                pe.sem_inc(v_used, CR_V)
                pe.wait_ge(zeroed, 3)
                pe.wait_ge(wv_made, 1)
                with pe.Fori(0, NH) as hd:
                    def scores(i):
                        s = hd * NT + i
                        if i == 0:
                            pe.wait_ge(qz_in, 32 * hd + 32)
                        for m in range(2):
                            pe.wait_ge(exp_done[m], s + CR_EXP)
                            for b in range(i // 4 + 1):
                                n = min(512, (i + 1) * P - 512 * b)
                                last = pe.matmul(ps[:, 2 * m + b, 0:n], qz[m][:, i * P:(i + 1) * P],
                                                 kT[:, bass.ds(hd, 1), 512 * b:512 * b + n].rearrange("p o t -> p (o t)"),
                                                 start=True, stop=True)
                            c0 = (i % 4) * P
                            last = pe.matmul(ps[:, 2 * m + i // 4, c0:c0 + P], ident, c("causal"), start=False, stop=True,
                                             skip_group_check=True)
                            last.then_inc(s_done[m], 1)
                        if i == NT - 1:
                            pe.wait_ge(s_done[1], hd * NT + NT)
                            pe.sem_inc(qz_free, 1)

                    def values(i):
                        for j in range(4):
                            q = 4 * i + j
                            seq, g = 2 * hd + q // NPG, q % NPG
                            if g == 0:
                                pe.wait_ge(dec_here, seq + CR_DEC)
                                pe.matmul(ps[:, 7, 0:NH], zero[:, :], zero[:, 0:NH], start=True, stop=True)
                            pe.wait_ge(v_in[q % 8], 64 * hd + 16 * (q // 8 + 1))
                            for h in range(NH):
                                last = pe.matmul(ps[:, 7, h:h + 1], vring[q % 8][:, h * P:(h + 1) * P],
                                                 wV[:, bass.ds(seq, 1), g, h:h + 1].rearrange("p o h -> p (o h)"),
                                                 start=False, stop=True, skip_group_check=True)
                            last.then_inc(v_used, 1)
                            if g == NPG - 1:
                                pe.wait_ge(vn_in[q // NPG], 16 * hd + 16)
                                for h in range(NH):
                                    last = pe.matmul(ps[:, 7, h:h + 1], vnew[q // NPG][:, h * P:(h + 1) * P],
                                                     wV[0:1, bass.ds(seq, 1), NPG, h:h + 1].rearrange("p o h -> p (o h)"),
                                                     start=False, stop=True, skip_group_check=True)
                                last.then_inc(dec_mm, 1)

                    def turn(i):
                        s = hd * NT + i
                        pe.wait_ge(w_made, s + 1 + CR_W)
                        pe.wait_ge(wt_here, s + CR_WT)
                        if i == 0:
                            pe.wait_ge(mixh_here, hd + CR_MIX)
                        for j in range(i + 1):
                            last = pe.transpose(ps[:, 4 + j // 4, (j % 4) * P:(j % 4 + 1) * P], wts[i % 2][:, j * P:(j + 1) * P], ident)
                        last.then_inc(wt_tr, 1)

                    def product(i):
                        s = hd * NT + i
                        pe.wait_ge(wt_here, s + 1 + CR_WT)
                        pe.wait_ge(o_here, s + CR_O)
                        for j in range(i + 1):
                            last = pe.matmul(ps[:, 6, 0:P], wtsT[i % 2][:, j, :], v_all[:, j, bass.ds(hd * P, P)],
                                             start=(j == 0), stop=(j == i))
                        last.then_inc(pv_done, 1)

                    for i in range(NT):
                        scores(i)
                        values(i)
                        if i >= 1:
                            turn(i - 1)
                            product(i - 1)
                    turn(NT - 1)
                    product(NT - 1)
                    pe.wait_ge(o_scaled, hd + 1)
                    for i in range(NT):
                        last = pe.transpose(ps[:, 4 + i // 4, (i % 4) * P:(i % 4 + 1) * P], o_h[:, i, :], ident)
                    last.then_inc(oT_tr, 1)
                pe.wait_ge(dec_here, NS + CR_DEC)
                pe.transpose(ps[0:NS * NH, 0, 0:P], oTs[:, :], ident).then_inc(od_tr, 1)
                pe.wait_ge(od_made, 1)
                pe.transpose(ps[:, 1, 0:NS * NH], od[:, 1, :], c("ident", NS * NH)[:, 0:NS * NH]).then_inc(odT_tr, 1)

            @block.vector
            def _(dve):
                own = Own(dve, dve2)
                dve.sem_inc(w_made, CR_W)
                dve.sem_inc(o_here, CR_O)
                dve.memset(zero[:, :], 0.0).then_inc(zeroed, 1)
                dve.memset(qz[0][:, :], 0.0).then_inc(zeroed, 1)
                dve.memset(qz[1][:, :], 0.0).then_inc(zeroed, 1)
                dmv = dm.rearrange("p a (s c) -> p a s c", s=NS)
                by_page = sc.rearrange("p s g c -> p s c g")
                dve.tensor_reduce(dmv[:, 0], by_page, AX_X, ALU.max).then_inc(dmax, 1)
                dve.wait_ge(gmax, 1)
                dve.tensor_tensor(sc[:, :, :, :], sc[:, :, :, :], dmv[:, 1].unsqueeze(2).to_broadcast([P, NS, NPG + 1, HM]),
                                  ALU.subtract).then_inc(sc_sub, 1)
                dve.wait_ge(sc_exp, 1)
                dve.tensor_reduce(dmv[:, 2], by_page, AX_X, ALU.add).then_inc(dsum, 1)
                dve.wait_ge(gsum, 1)
                own(dve.reciprocal(dm[:, 0, :], dm[:, 3, :]))
                own.wait()
                r = dm[:, 0, :].rearrange("p (s h m) -> p s h m", s=NS, m=2)
                own(dve.tensor_scalar(r[:, :, :, 1], r[:, :, :, 1], neglam[:, 0:1], None, ALU.mult))
                own.wait()
                e = sc.rearrange("p s g (h m) -> p s g h m", m=2)
                own(dve.tensor_tensor(wV[:, :, :, :], e[:, :, :, :, 0],
                                      r[:, :, :, 0].unsqueeze(2).to_broadcast([P, NS, NPG + 1, NH]), ALU.mult))
                own(dve.tensor_tensor(wtmp[:, :, :, :], e[:, :, :, :, 1],
                                      r[:, :, :, 1].unsqueeze(2).to_broadcast([P, NS, NPG + 1, NH]), ALU.mult))
                own.wait()
                dve.tensor_tensor(wV[:, :, :, :], wV[:, :, :, :], wtmp[:, :, :, :], ALU.add).then_inc(wv_made, 1)

                with own.loop(NH, 8 * 3 + 1) as hd:
                    def maxima(i):
                        s = hd * NT + i
                        for m in range(2):
                            dve.wait_ge(s_done[m], s + 1)
                            dve.tensor_reduce(s2[i % 2][:, m:m + 1],
                                              ps[:, 2 * m:2 * m + 2, :].rearrange("p b t -> p (b t)")[:, 0:(i + 1) * P], AX_X,
                                              ALU.max, negate=True).then_inc(nmax_here[m], 1)

                    def combine(i):
                        s = hd * NT + i
                        st_, k = s2[i % 2], (i + 1) * P
                        for m in range(2):
                            dve.wait_ge(exp_done[m], s + 1 + CR_EXP)
                        own(dve.reciprocal(st_[:, 4:6], st_[:, 2:4]))
                        own.wait()
                        own(dve.tensor_scalar(st_[:, 6:7], st_[:, 5:6], neglam[:, 0:1], None, ALU.mult))
                        own.wait()
                        own(dve.tensor_scalar(exps[i % 2][1][:, 0:k], exps[i % 2][1][:, 0:k], st_[:, 6:7], None, ALU.mult))
                        own.wait()
                        dve.wait_ge(wt_tr, s - 1 + CR_WTT)
                        dve.scalar_tensor_tensor(out=wts[i % 2][:, 0:k], in0=exps[i % 2][0][:, 0:k], scalar=st_[:, 4:5],
                                                 in1=exps[i % 2][1][:, 0:k], op0=ALU.mult, op1=ALU.add).then_inc(w_made, 1)

                    def o_copy(i):
                        dve.wait_ge(pv_done, hd * NT + i + 1 + CR_PV)
                        dve.tensor_copy(o_h[:, i, :], ps[:, 6, 0:P]).then_inc(o_here, 1)

                    for i in range(NT):
                        maxima(i)
                        if i >= 1:
                            combine(i - 1)
                        if i >= 2:
                            o_copy(i - 2)
                    combine(NT - 1)
                    o_copy(NT - 2)
                    o_copy(NT - 1)
                    dve.wait_ge(o_sq, hd * NT + NT)
                    dve.tensor_scalar(so[:, 8:16], so[:, 0:8], 1.0 / P, EPS, ALU.mult, ALU.add).then_inc(ms2, 1)
                    dve.wait_ge(rt2, hd + 1)
                    own(dve.reciprocal(so[:, 24:32], so[:, 16:24]))
                    own.wait()
                    dve.tensor_tensor(o_h[:, :, :], o_h[:, :, :], so[:, 24:32].unsqueeze(2).to_broadcast([P, NT, P]),
                                      ALU.mult).then_inc(o_scaled, 1)
                    dve.wait_ge(oT_tr, hd + 1)
                dve.wait_ge(od_tr, 1)
                own(dve.tensor_copy(od[:, 0, :], ps[0:NS * NH, 0, 0:P]))
                own.wait()
                own(dve.scalar_tensor_tensor(out=od[:, 1, :], in0=od[:, 0, :], scalar=1.0, in1=od[:, 0, :], op0=ALU.mult,
                                             op1=ALU.mult, accum_out=sd[:, 0:1]))
                own.wait()
                dve.tensor_scalar(sd[:, 1:2], sd[:, 0:1], 1.0 / P, EPS, ALU.mult, ALU.add).then_inc(od_ms, 1)
                dve.wait_ge(od_rt, 1)
                own(dve.reciprocal(sd[:, 3:4], sd[:, 2:3]))
                own.wait()
                dve.tensor_scalar(od[:, 1, :], od[:, 0, :], sd[:, 3:4], None, ALU.mult).then_inc(od_made, 1)
                dve.wait_ge(odT_tr, 1)
                dve.tensor_scalar(mixs[:, :, :], ps[:, 1, 0:NS * NH].rearrange("p (s h) -> p h s", h=NH), subln[:, 0:1], None,
                                  ALU.mult).then_inc(mixs_here, 1)

        free_semaphores()

        T9 = NT + 1
        mixr = [place(f"mixr{j}", 41 + 4 * j, [P, KC, P]) for j in range(2)]
        xr = [place(f"xr{j}", 49 + 4 * j, [P, D]) for j in range(2)]
        x1b = [place(f"x1b{j}", 57 + 4 * j, [P, D]) for j in range(2)]
        t3 = place("t3", 65, [P, D])
        h2b = [place(f"h2b{j}", 69 + 4 * j, [P, D]) for j in range(2)]
        h2T = [place(f"h2T{j}", 77 + 4 * j, [P, KC, P]) for j in range(2)]
        rw = place("rw", 85, [P, KC, NE])
        msamp = place("msamp", 87, [NS, 3, D])
        lg = place("lg", 113, [P, T9, NE])
        sig = place("sig", 115.5, [P, T9, NE])
        sel = place("sel", 118, [P, T9, NE])
        mask = place("mask", 120.5, [P, T9, NE])
        pairs = place("pairs", 123, [P, T9 * EG, 28])
        cmp_a = place("cmp_a", 131, [P, T9 * EG, EG])
        cmp_b = place("cmp_b", 133.5, [P, T9 * EG, EG])
        onehot = place("onehot", 136, [P, T9 * TOPK, NE])
        picked = place("picked", 17, [P, T9 * TOPK, NE])
        s3 = place("s3", 192, [P, 8])
        junk3 = place("junk3", 192.125, [P, D])
        gsc = place("gsc", 196.25, [P, T9 * EG])
        grank = place("grank", 196.75, [P, T9 * EG])
        top = place("top", 197.25, [P, T9, TOPK])
        top_i = place("top_i", 197.75, [P, T9, TOPK], U32)
        top_f = place("top_f", 198.25, [P, T9 * TOPK])
        wraw = place("wraw", 198.75, [P, T9, TOPK])
        wsum = place("wsum", 199.25, [P, 2, T9])
        dst_f = place("dst_f", 199.5, [P, T9 * TOPK])
        first_b = place("first_b", 200, [P, NE])
        first_r = place("first_r", 200.25, [P, NE])
        rbias = place("rbias", 200.5, [P, NE])
        bt = place("bt", 200.75, [P, 8])
        bt_i = place("bt_i", 200.8125, [P, 4], I32)
        nbT = place("nbT", 201, [NE, P])
        tots = place("tots", 123, [P, T9, NE])
        cntc = place("cntc", 126, [NE, P, 8])
        blk_t = place("blk_t", 202, [P, T9 * TOPK], I32)
        dst_b = place("dst_b", 202.3125, [P, T9 * TOPK])
        dst_p = place("dst_p", 202.625, [P, T9 * TOPK])
        OH = 4
        oh_p = [place(f"oh_p{j}", 160 + 4 * j, [P, TOPK, P]) for j in range(OH)]
        oh_b = [place(f"oh_b{j}", 176 + 4 * j, [P, TOPK, P]) for j in range(OH)]
        tok_f = place("tok_f", 130.25, [P, NBLK + 2])
        zrow = place("zrow", 205, [2, D // 2])
        route_w = place("route_w", 203, [P, T9, TOPK])
        dst_i = place("dst_i", 203.5, [P, T9 * TOPK], I32)
        tokb = place("tokb", 204, [P, NBLK + 2], I32)

        w_dn = place("w_dn", 41, [P, SLOTS, FC * D])
        w_gu = place("w_gu", 73, [P, SLOTS, 2, KC * F])
        early_in = sem("early_in", keep=True)

        m_in = [sem(f"m_in{j}") for j in range(2)]
        xr_in = [sem(f"xr_in{j}") for j in range(2)]
        rw_in, msamp_in, rb_in = sem("rw_in"), sem("msamp_in"), sem("rb_in")
        out_mm, ss_here, ms_a, rt_a, t_made, x1_made = (
            sem("out_mm"), sem("ss_here"), sem("ms_a"), sem("rt_a"), sem("t_made"), sem("x1_made"))
        ms_b, rt_b, h2_made, h2_tr, h2T_here, r_mm, lg_here = (
            sem("ms_b"), sem("rt_b"), sem("h2_made"), sem("h2_tr"), sem("h2T_here"), sem("r_mm"), sem("lg_here"))
        x1_out = [sem(f"x1_out{j}") for j in range(2)]
        h2_out = [sem(f"h2_out{j}") for j in range(2)]
        h2T_out = [sem(f"h2T_out{j}") for j in range(2)]
        sig_here, mask_made, rank_mm, nbT_made, first_mm, bt_made, bt_out = (
            sem("sig_here"), sem("mask_made"), sem("rank_mm"), sem("nbT_made"), sem("first_mm"),
            sem("bt_made"), sem("bt_out"))
        oh_p_made, oh_b_made, oh_b_ids, tok_mm = sem("oh_p_made"), sem("oh_b_made"), sem("oh_b_ids"), sem("tok_mm")
        z_made, z_out, bt_in, dve3 = sem("z_made"), sem("z_out"), sem("bt_in"), sem("dve3")

        def tokens(s):
            return (SEQ, NS) if isinstance(s.n, int) and s.n == 0 else ((s.n - 1) * P, P)

        with nc.Block() as block:
            @block.sync
            def _(sp):
                def loads(s):
                    a, rows = tokens(s)
                    x_from = x_sample.rearrange("b s d -> (b s) d") if rows == NS else x_prompt[0][bass.ds(a, P), :]
                    m_from = mix_d[0, :, :, 0:NS] if rows == NS else mix_d[bass.ds(s.n, 1)].rearrange("o p c t -> p (o c) t")
                    addressed(sp, x_from, m_from)
                    wait(sp, out_mm, s.n - 1)
                    sp.dma_start(mixr[s.par][:, :, 0:rows], m_from).then_inc(m_in[s.par], 16)
                    wait(sp, x1_made, s.n - 1)
                    sp.dma_start(xr[s.par][0:rows, :], x_from).then_inc(xr_in[s.par], 16)

                def stores(s):
                    a, rows = tokens(s)
                    x1_to, h2_to = x1_d[bass.ds(a, rows), :], h2_d[bass.ds(a, rows), :]
                    hT_to = h2T_d[bass.ds(s.n, 1)].rearrange("o p (k t) -> p (o k) t", k=KC)[:, :, 0:rows]
                    addressed(sp, x1_to, h2_to, hT_to)
                    sp.wait_ge(x1_made, s.n + 1)
                    sp.dma_start(x1_to, x1b[s.par][0:rows, :]).then_inc(x1_out[s.par], 16)
                    sp.wait_ge(h2_made, s.n + 1)
                    sp.dma_start(h2_to, h2b[s.par][0:rows, :]).then_inc(h2_out[s.par], 16)
                    sp.wait_ge(h2T_here, s.n + 1)
                    sp.dma_start(hT_to, h2T[s.par][:, :, 0:rows]).then_inc(h2T_out[s.par], 16)

                for j in range(2):
                    sp.sem_inc(x1_out[j], 16)
                    sp.sem_inc(h2_out[j], 16)
                    sp.sem_inc(h2T_out[j], 16)
                loads(fixed(0))
                sp.dma_start(msamp[:, :, :], mod_d[0:NS, 2 * D:5 * D].rearrange("n (m d) -> n m d", m=3)).then_inc(msamp_in, 16)
                loads(fixed(1))
                sp.dma_start(rw[:, :, :], router_w[0].rearrange("(p k) e -> p k e", k=KC)).then_inc(rw_in, 16)
                sp.dma_start(rbias[:, :], router_bias[0].partition_broadcast(P)).then_inc(rb_in, 16)
                sp.wait_ge(z_made, 1)
                sp.dma_start(h2_d[NTOK:NTOK + 1, :].rearrange("o (a b) -> (o a) b", a=2),
                             zrow[:, :]).then_inc(z_out, 16)
                stores(fixed(0))
                with sp.Fori(0, 3) as it:
                    for s in (Step(2 * it + 1, 1, it), Step(2 * it + 2, 0, it + 1)):
                        loads(s.next)
                        stores(s)
                loads(fixed(8))
                stores(fixed(7))
                stores(fixed(8))
                for j in range(2):
                    for o in (x1_out, h2_out, h2T_out):
                        sp.wait_ge(o[j], 16 * (NT // 2 + 1 - j) + 16)
                sp.wait_ge(z_out, 16)
                sp.wait_ge(lg_here, T9)
                for e in range(EARLY):
                    for n, w in enumerate((ew_gate, ew_up)):
                        sp.dma_start(w_gu[:, e, n, :], w[0, e].rearrange("(p k) f -> p (k f)", k=KC)).then_inc(early_in, 16)
                    sp.dma_start(w_dn[:, e, :], ew_down[0, e].rearrange("(p c) n -> p (c n)", c=FC)).then_inc(early_in, 16)
                sp.wait_ge(bt_made, 1)
                sp.dma_start(blk_d, bt_i[:, :]).then_inc(bt_out, 16)
                sp.wait_ge(bt_out, 16)
                sp.dma_start(tbl[:, :], blk_d.rearrange("(o b) c -> o (b c)", o=1)).then_inc(bt_in, 16)
                sp.wait_ge(bt_in, 16)
            @block.scalar
            def _(act):
                def body(s, rows):
                    act.wait_ge(out_mm, s.n + 1)
                    act.activation(junk3[0:rows, :], ps[0:rows, 2 * s.par:2 * s.par + 2, :].rearrange("p b n -> p (b n)"),
                                   ACT.Square, accum_out=s3[0:rows, 0:1]).then_inc(ss_here, 1)
                    act.wait_ge(ms_a, s.n + 1)
                    act.activation(s3[0:rows, 2:3], s3[0:rows, 1:2], ACT.Sqrt).then_inc(rt_a, 1)
                    act.wait_ge(ms_b, s.n + 1)
                    act.activation(s3[0:rows, 6:7], s3[0:rows, 5:6], ACT.Sqrt).then_inc(rt_b, 1)
                    act.wait_ge(h2_tr, s.n + 1)
                    wait(act, r_mm, s.n)
                    act.wait_ge(h2T_out[s.par], 16 * s.turn + 16)
                    act.activation(h2T[s.par][:, :, 0:rows], ps[:, 4:6, :].rearrange("p b (k t) -> p (b k) t", t=P)[:, :, 0:rows],
                                   ACT.Copy).then_inc(h2T_here, 1)
                    act.wait_ge(r_mm, s.n + 1)
                    act.activation(lg[0:rows, bass.ds(s.n, 1), :].rearrange("p o e -> p (o e)"), ps[0:rows, 6, 0:NE],
                                   ACT.Copy).then_inc(lg_here, 1)

                act.wait_ge(z_made, 1)
                body(fixed(0), NS)
                with act.Fori(0, NT // 2) as it:
                    for s in (Step(2 * it + 1, 1, it), Step(2 * it + 2, 0, it + 1)):
                        body(s, P)
                act.wait_ge(lg_here, T9)
                act.activation(sig[:, :, :], lg[:, :, :], ACT.Sigmoid).then_inc(sig_here, 1)
                for t in range(T9):
                    act.wait_ge(oh_b_made, t + 1)
                    act.activation(oh_b[t % OH][:, :, :], oh_b[t % OH][:, :, :], ACT.Copy,
                                   scale=c("ids")[:, t:t + 1]).then_inc(oh_b_ids, 1)

            @block.tensor
            def _(pe):
                def out(s, rows):
                    pe.wait_ge(m_in[s.par], 16 * s.turn + 16)
                    wait(pe, t_made, s.n - 1)
                    for half in range(2):
                        for k in range(KC):
                            last = pe.matmul(ps[0:rows, 2 * s.par + half, :], mixr[s.par][:, k, 0:rows],
                                             w_out_sb[:, k, 512 * half:512 * half + 512], start=(k == 0), stop=(k == KC - 1))
                    last.then_inc(out_mm, 1)

                def route(s, rows):
                    pe.wait_ge(h2_made, s.n + 1)
                    wait(pe, h2T_here, s.n)
                    for k in range(KC):
                        last = pe.transpose(ps[:, 4 + k // 4, (k % 4) * P:(k % 4) * P + rows], h2b[s.par][0:rows, k * P:(k + 1) * P],
                                            c("ident", rows)[:, 0:rows])
                    last.then_inc(h2_tr, 1)
                    pe.wait_ge(h2T_here, s.n + 1)
                    wait(pe, lg_here, s.n)
                    for k in range(KC):
                        last = pe.matmul(ps[0:rows, 6, 0:NE], h2T[s.par][:, k, 0:rows], rw[:, k, :], start=(k == 0), stop=(k == KC - 1))
                    last.then_inc(r_mm, 1)

                pe.wait_ge(w_out_here, 16)
                pe.wait_ge(rw_in, 16)
                out(fixed(0), NS)
                out(fixed(1), P)
                route(fixed(0), NS)
                with pe.Fori(0, 3) as it:
                    for s in (Step(2 * it + 1, 1, it), Step(2 * it + 2, 0, it + 1)):
                        out(s.next, P)
                        route(s, P)
                out(fixed(8), P)
                route(fixed(7), P)
                route(fixed(8), P)

                pe.wait_ge(mask_made, 1)
                for t in range(T9):
                    dst = ps[:, 0, t * NE:(t + 1) * NE] if t < NT else ps[:, 1, 0:NE]
                    pe.matmul(dst, c("before"), mask[:, t, :], start=True, stop=(t == 0))
                    for u in range(t):
                        pe.matmul(dst, c("ones"), mask[:, u, :], start=False, stop=(u == t - 1))
                for t in range(T9):
                    last = pe.matmul(ps[0:NE, 3, 0:P], mask[:, t, :], c("ones"), start=(t == 0), stop=(t == T9 - 1))
                last.then_inc(rank_mm, 1)
                pe.wait_ge(nbT_made, 1)
                pe.matmul(ps[:, 4, 0:NE], nbT[:, :], c("before", NE)[:, 0:NE], start=True, stop=True)
                pe.matmul(ps[:, 4, NE:NE + 1], nbT[:, :], c("ones", NE)[:, 0:1], start=True, stop=True).then_inc(first_mm, 1)
                for t in range(T9):
                    pe.wait_ge(oh_p_made, t + 1)
                    pe.wait_ge(oh_b_ids, t + 1)
                    for k in range(TOPK):
                        last = pe.matmul(ps[:, 5, 0:NBLK], oh_p[t % OH][:, k, :], oh_b[t % OH][:, k, 0:NBLK],
                                         start=(t == 0 and k == 0), stop=(t == T9 - 1 and k == TOPK - 1))
                    last.then_inc(tok_mm, 1)

            @block.vector
            def _(dve):
                own = Own(dve, dve3)

                def body(s, rows, g1, b2, a2):
                    m = ps[0:rows, 2 * s.par:2 * s.par + 2, :].rearrange("p b n -> p (b n)")
                    x1, t = x1b[s.par][0:rows, :], t3[0:rows, :]
                    dve.wait_ge(ss_here, s.n + 1)
                    dve.tensor_scalar(s3[0:rows, 1:2], s3[0:rows, 0:1], 1.0 / D, EPS, ALU.mult, ALU.add).then_inc(ms_a, 1)
                    dve.wait_ge(rt_a, s.n + 1)
                    own(dve.reciprocal(s3[0:rows, 3:4], s3[0:rows, 2:3]))
                    own.wait()
                    wait(dve, h2_made, s.n)
                    dve.scalar_tensor_tensor(out=t, in0=m, scalar=s3[0:rows, 3:4], in1=g1, op0=ALU.mult, op1=ALU.mult
                                             ).then_inc(t_made, 1)
                    dve.wait_ge(t_made, s.n + 1)
                    dve.wait_ge(xr_in[s.par], 16 * s.turn + 16)
                    dve.wait_ge(x1_out[s.par], 16 * s.turn + 16)
                    dve.tensor_tensor(x1, t, xr[s.par][0:rows, :], ALU.add).then_inc(x1_made, 1)
                    dve.wait_ge(x1_made, s.n + 1)
                    own(dve.scalar_tensor_tensor(out=t, in0=x1, scalar=1.0, in1=x1, op0=ALU.mult, op1=ALU.mult,
                                                 accum_out=s3[0:rows, 4:5]))
                    own.wait()
                    dve.tensor_scalar(s3[0:rows, 5:6], s3[0:rows, 4:5], 1.0 / D, EPS, ALU.mult, ALU.add).then_inc(ms_b, 1)
                    dve.wait_ge(rt_b, s.n + 1)
                    own(dve.reciprocal(s3[0:rows, 7:8], s3[0:rows, 6:7]))
                    own.wait()
                    own(dve.scalar_tensor_tensor(out=t, in0=x1, scalar=s3[0:rows, 7:8], in1=a2, op0=ALU.mult, op1=ALU.mult))
                    own.wait()
                    dve.wait_ge(h2_out[s.par], 16 * s.turn + 16)
                    wait(dve, h2_tr, s.n - 1 if isinstance(s.n, int) else s.n)
                    dve.tensor_tensor(h2b[s.par][0:rows, :].rearrange("t (k p) -> t p k", k=KC),
                                      t.rearrange("t (p k) -> t p k", k=KC), b2.rearrange("t (p k) -> t p k", k=KC),
                                      ALU.add).then_inc(h2_made, 1)

                own(dve.memset(lg[:, 0, :], 0.0))
                own.wait()
                dve.memset(zrow[:, :], 0.0).then_inc(z_made, 1)
                dve.wait_ge(msamp_in, 16)
                body(fixed(0), NS, msamp[:, 0, :], msamp[:, 1, :], msamp[:, 2, :])
                with own.loop(NT // 2, 8) as it:
                    for s in (Step(2 * it + 1, 1, it), Step(2 * it + 2, 0, it + 1)):
                        body(s, P, mods[:, G1, :], mods[:, B2, :], mods[:, A2, :])

                def do(ins):
                    own(ins)
                    own.wait()

                dve.wait_ge(rb_in, 16)
                dve.wait_ge(sig_here, 1)
                do(dve.tensor_tensor(sel[:, :, :], sig[:, :, :], rbias[:, :].unsqueeze(1).to_broadcast([P, T9, NE]), ALU.add))
                selg = sel.rearrange("p t (g e) -> p (t g) e", g=EG)
                at_pair = 0
                for d in range(1, EG):
                    own(dve.tensor_tensor(pairs[:, :, at_pair:at_pair + EG - d], selg[:, :, 0:EG - d], selg[:, :, d:EG], ALU.add))
                    at_pair += EG - d
                own.wait()
                do(dve.tensor_reduce(gsc[:, :], pairs[:, :, :], AX_X, ALU.max))
                gv = gsc[:, :].rearrange("p (t g) -> p t g", g=EG)
                other = gv.unsqueeze(2).to_broadcast([P, T9, EG, EG])
                this = gv.unsqueeze(3).to_broadcast([P, T9, EG, EG])
                ca, cb = (x.rearrange("p (t g) h -> p t g h", g=EG) for x in (cmp_a, cmp_b))
                own(dve.tensor_tensor(ca, other, this, ALU.is_gt))
                do(dve.tensor_tensor(cb, other, this, ALU.is_equal))
                do(dve.tensor_tensor(cmp_b.rearrange("p a h -> p (a h)").rearrange("p (t q) -> p t q", t=T9),
                                     cmp_b.rearrange("p a h -> p (a h)").rearrange("p (t q) -> p t q", t=T9),
                                     c("lower_g").unsqueeze(1).to_broadcast([P, T9, EG * EG]), ALU.mult))
                do(dve.tensor_tensor(cmp_a[:, :, :], cmp_a[:, :, :], cmp_b[:, :, :], ALU.add))
                do(dve.tensor_reduce(grank[:, :], cmp_a[:, :, :], AX_X, ALU.add))
                do(dve.tensor_scalar(grank[:, :], grank[:, :], float(TOPG) - 0.5, NEG, ALU.is_gt, ALU.mult))
                do(dve.tensor_tensor(selg, selg, grank[:, :].unsqueeze(2).to_broadcast([P, T9 * EG, EG]), ALU.add))
                for t in range(T9):
                    own(dve.max(top[:, t, :], sel[:, t, :]))
                own.wait()
                for t in range(T9):
                    own(dve.max_index(top_i[:, t, :], top[:, t, :], sel[:, t, :]))
                own.wait()
                do(dve.tensor_copy(top_f[:, :], top_i.rearrange("p t k -> p (t k)")))
                do(dve.tensor_tensor(onehot[:, :, :], top_f[:, :].unsqueeze(2).to_broadcast([P, T9 * TOPK, NE]),
                                     c("iota_e").unsqueeze(1).to_broadcast([P, T9 * TOPK, NE]), ALU.is_equal))
                oh = onehot.rearrange("p (t k) e -> p t k e", k=TOPK)
                do(dve.tensor_reduce(mask[:, :, :], onehot.rearrange("p (t k) e -> p t e k", k=TOPK), AX_X, ALU.add))
                dve.tensor_scalar(mask[:, 0, :], mask[:, 0, :], c("is_sample"), None, ALU.mult).then_inc(mask_made, 1)
                pk = picked.rearrange("p (t k) e -> p t k e", k=TOPK)
                do(dve.tensor_tensor(pk, oh, sig[:, :, :].unsqueeze(2).to_broadcast([P, T9, TOPK, NE]), ALU.mult))
                do(dve.tensor_reduce(wraw.rearrange("p t k -> p (t k)"), picked[:, :, :], AX_X, ALU.add))
                do(dve.tensor_reduce(wsum[:, 0, :], wraw[:, :, :], AX_X, ALU.add))
                do(dve.reciprocal(wsum[:, 1, :], wsum[:, 0, :]))
                do(dve.scalar_tensor_tensor(out=route_w[:, :, :], in0=wraw[:, :, :], scalar=SCALE_ROUTED,
                                            in1=wsum[:, 1, :].unsqueeze(2).to_broadcast([P, T9, TOPK]), op0=ALU.mult, op1=ALU.mult))
                dve.wait_ge(rank_mm, 1)
                do(dve.tensor_tensor(cntc[:, :, :], ps[0:NE, 3, 0:P].unsqueeze(2).to_broadcast([NE, P, 8]),
                                     c("steps_128", NE).unsqueeze(1).to_broadcast([NE, P, 8]), ALU.is_gt))
                do(dve.tensor_reduce(nbT[:, :], cntc[:, :, :], AX_X, ALU.add))
                dve.tensor_scalar(nbT[:, :], nbT[:, :], 1.0, None, ALU.add).then_inc(nbT_made, 1)
                dve.wait_ge(first_mm, 1)
                own(dve.tensor_copy(first_b[:, :], ps[:, 4, 0:NE]))
                do(dve.tensor_scalar(first_r[:, :], ps[:, 4, 0:NE], float(P), None, ALU.mult))
                do(dve.tensor_tensor(tots[:, :, :], ps[:, 0:2, :].rearrange("p b n -> p (b n)")[:, 0:T9 * NE].rearrange(
                    "p (t e) -> p t e", e=NE), first_r[:, :].unsqueeze(1).to_broadcast([P, T9, NE]), ALU.add))
                do(dve.tensor_tensor(pk, oh, tots[:, :, :].unsqueeze(2).to_broadcast([P, T9, TOPK, NE]), ALU.mult))
                do(dve.tensor_reduce(dst_f[:, :], picked[:, :, :], AX_X, ALU.add))
                do(dve.tensor_copy(dst_i[:, :], dst_f[:, :]))
                do(dve.tensor_scalar(blk_t[:, :], dst_i[:, :], 7, None, ALU.logical_shift_right))
                do(dve.tensor_copy(dst_b[:, :], blk_t[:, :]))
                do(dve.scalar_tensor_tensor(out=dst_p[:, :], in0=dst_b[:, :], scalar=-float(P), in1=dst_f[:, :],
                                            op0=ALU.mult, op1=ALU.add))
                for t in range(T9):
                    if t >= OH:
                        dve.wait_ge(tok_mm, t - OH + 1)
                    dve.tensor_tensor(oh_b[t % OH][:, :, :], c("iota_p").unsqueeze(1).to_broadcast([P, TOPK, P]),
                                      dst_b[:, t * TOPK:(t + 1) * TOPK].unsqueeze(2).to_broadcast([P, TOPK, P]),
                                      ALU.is_equal).then_inc(oh_b_made, 1)
                    dve.tensor_tensor(oh_p[t % OH][:, :, :], c("iota_p").unsqueeze(1).to_broadcast([P, TOPK, P]),
                                      dst_p[:, t * TOPK:(t + 1) * TOPK].unsqueeze(2).to_broadcast([P, TOPK, P]),
                                      ALU.is_equal).then_inc(oh_p_made, 1)
                own(dve.tensor_scalar(sel[:, 0, :], first_b[:, :], c("block_id"), None, ALU.is_le))
                do(dve.tensor_scalar(sel[:, 1, :], first_b[:, :], c("block_id"), None, ALU.is_equal))
                own(dve.tensor_reduce(bt[:, 4:5], sel[:, 0, :], AX_X, ALU.add))
                do(dve.tensor_reduce(bt[:, 2:3], sel[:, 1, :], AX_X, ALU.add))
                do(dve.tensor_scalar(bt[:, 0:1], bt[:, 4:5], -1.0, None, ALU.add))
                do(dve.scalar_tensor_tensor(out=bt[:, 2:3], in0=bt[:, 0:1], scalar=EARLY - 0.5, in1=bt[:, 2:3],
                                            op0=ALU.is_gt, op1=ALU.mult))
                do(dve.tensor_scalar(sel[:, 2, 0:NE // SLOTS], c("steps_slots"), bt[:, 0:1], None, ALU.is_le))
                do(dve.tensor_reduce(bt[:, 5:6], sel[:, 2, 0:NE // SLOTS], AX_X, ALU.add))
                do(dve.tensor_copy(bt[:, 6:7], ps[:, 4, NE:NE + 1]))
                own(dve.scalar_tensor_tensor(out=bt[:, 3:4], in0=bt[:, 6:7], scalar=c("block_id"), in1=bt[:, 6:7],
                                             op0=ALU.is_gt, op1=ALU.mult))
                do(dve.scalar_tensor_tensor(out=bt[:, 1:2], in0=bt[:, 5:6], scalar=-float(SLOTS), in1=bt[:, 0:1],
                                            op0=ALU.mult, op1=ALU.add))
                dve.tensor_copy(bt_i[:, :], bt[:, 0:4]).then_inc(bt_made, 1)
                do(dve.memset(tok_f[:, NBLK:NBLK + 2], 0.0))
                dve.wait_ge(tok_mm, T9)
                do(dve.tensor_copy(tok_f[:, 0:NBLK], ps[:, 5, 0:NBLK]))
                do(dve.tensor_scalar(tokb[:, :], tok_f[:, :], float(NTOK), None, ALU.add))
                dve.wait_ge(bt_in, 16)
                pair = tbl[0:1, :].rearrange("o (q r) -> o q r", r=8)
                do(dve.tensor_scalar(words[:, :], pair[:, :, 3], 0.0, float(W_USED), ALU.is_gt, ALU.mult))
                for place_in_word, col in ((W_SLOT[0], 1), (W_SLOT[1], 5), (W_NEW[0], 2), (W_NEW[1], 6)):
                    do(dve.scalar_tensor_tensor(out=words[:, :], in0=pair[:, :, col], scalar=float(place_in_word),
                                                in1=words[:, :], op0=ALU.mult, op1=ALU.add))

        free_semaphores()

        xg = [place(f"xg{j}", 137 + 4 * j, [P, D]) for j in range(2)]
        xT = [place(f"xT{j}", 145 + 4 * j, [P, KC, P]) for j in range(2)]
        sg = [place(f"sg{j}", 153 + j, [P, F]) for j in range(2)]
        hb = [place(f"hb{j}", 155 + j, [P, F]) for j in range(2)]
        hT = [place(f"hT{j}", 157 + j, [P, FC, P]) for j in range(2)]
        yb = [place(f"yb{j}", 159 + 4 * j, [P, D]) for j in range(2)]
        idx = [place(f"idx{j}", 167 + j / 16, [P, 1], I32) for j in range(2)]
        zrows = place("zrows", 168, [P, 2 * D])
        s_gu = place("s_gu", 176, [P, 2, KC * F])
        s_dn = place("s_dn", 192, [P, FC, D])
        sw_in = sem("sw_in", keep=True)
        zrows_made, z_rows_out = sem("zrows_made"), sem("z_rows_out")
        we_in = [sem(f"we_in{j}") for j in range(2)]
        xg_in = [sem(f"xg_in{j}") for j in range(2)]
        rows_out = [sem(f"rows_out{j}") for j in range(2)]
        x_tr, xT_here, gu_mm, sg_here, hb_made, h_tr, hbT_here, dn_mm, y_here, idx_here = (
            sem("x_tr"), sem("xT_here"), sem("gu_mm"), sem("sg_here"), sem("hb_made"), sem("h_tr"), sem("hbT_here"),
            sem("dn_mm"), sem("y_here"), sem("idx_here"))
        dve4, pool4, ended4 = sem("dve4"), sem("pool4"), sem("ended4")
        WE = 48
        CR_DN = SLOTS
        CR = 2

        @contextmanager
        def pairs_of_blocks(eng):
            with eng.Fori(0, NBLK // 2) as it:
                word = eng.value_load(words[0:1, bass.ds(it, 1)], min_val=0, max_val=2 * W_USED - 1)
                with eng.If(word // W_USED):
                    yield it, word

        def slot_of(word, j):
            return (word // W_SLOT[j]) % SLOTS

        def pairs_done(eng):
            return (eng.value_load(tbl[0:1, 3:4], min_val=NE, max_val=NBLK) + 1) // 2

        with nc.Block() as block:
            @block.sync
            def _(sp):
                sp.sem_inc(dn_mm, CR_DN)
                for j in range(2):
                    sp.sem_inc(we_in[j], WE)
                for n, w in enumerate((sw_gate, sw_up)):
                    sp.dma_start(s_gu[:, n, :], w[0].rearrange("(p k) f -> p (k f)", k=KC)).then_inc(sw_in, 16)
                sp.dma_start(s_dn[:, :, :], sw_down[0].rearrange("(p c) n -> p c n", c=FC)).then_inc(sw_in, 16)
                blocks = sp.value_load(tbl[0:1, 3:4], min_val=NE, max_val=NBLK)
                sp.wait_ge(zrows_made, 1)
                with pairs_of_blocks(sp) as (it, word):
                    for j in range(2):
                        b = 2 * it + j
                        e = sp.value_load(tbl[0:1, bass.ds(b * 4, 1)], min_val=0, max_val=NE - 1)
                        slot, new = slot_of(word, j), (word // W_NEW[j]) % 2
                        computed = sp.lower_val(b + 1)
                        sp.wait_ge(we_in[j], WE * (it + 1))
                        sp.wait_ge(dn_mm, computed)
                        for n, w in enumerate((ew_gate, ew_up)):
                            sp.dma_start(w_gu[:, bass.ds(slot, 1), n, :].rearrange("p o f -> p (o f)"),
                                         w[0][bass.ds(e, 1)].rearrange("o (p k) f -> p (o k f)", k=KC),
                                         cond=new).then_inc(we_in[j], 16)
                        sp.dma_start(w_dn[:, bass.ds(slot, 1), :].rearrange("p o f -> p (o f)"),
                                     ew_down[0][bass.ds(e, 1)].rearrange("o (p c) n -> p (o c n)", c=FC),
                                     cond=new).then_inc(we_in[j], 16)
                    far = NBLK // 2 - 1 - it
                    sp.dma_start(rows_d[bass.ds(far * (2 * P), 2 * P), :].rearrange("(p r) d -> p (r d)", p=P), zrows[:, :],
                                 cond=(far * 2 - blocks + NBLK) // NBLK).then_inc(z_rows_out, 16)
                pairs = pairs_done(sp)
                done, filled = sp.lower_val(WE * (pairs + 1)), sp.lower_val(16 * pairs)
                for j in range(2):
                    sp.wait_ge(we_in[j], done)
                sp.wait_ge(z_rows_out, filled)
                sp.sem_inc(ended4, 1)

            @block.gpsimd
            def _(pool):
                own = Own(pool, pool4)
                pool.sem_inc(x_tr, CR)

                def gather(b, j):
                    pool.wait_ge(x_tr, b + 1)
                    own(pool.tensor_copy(idx[j][:, :], tokb[:, bass.ds(b, 1)]))
                    own.wait()
                    pool.sem_inc(idx_here, 1)
                    pool.indirect_dma_start(out=xg[j][:, :], out_offset=None, in_=h2_d[:, :],
                                            in_offset=bass.IndirectOffsetOnAxis(ap=idx[j][:, 0:1], axis=0)
                                            ).then_inc(xg_in[j], 16)

                for j in range(2):
                    gather(j, j)
                with own.over_pairs(pairs_of_blocks(pool), 2) as (it, _):
                    for j in range(2):
                        gather(2 * it + 2 + j, j)

            @block.scalar
            def _(act):
                for j in range(2):
                    act.sem_inc(rows_out[j], 16)
                act.sem_inc(hb_made, CR)
                with pairs_of_blocks(act) as (it, _):
                    for j in range(2):
                        b = 2 * it + j
                        act.wait_ge(gu_mm, b + 1)
                        act.wait_ge(hb_made, b + 1)
                        act.activation(sg[j][:, :], ps[:, 2 + j, 0:F], ACT.Sigmoid).then_inc(sg_here, 1)
                    for j in range(2):
                        b = 2 * it + j
                        act.wait_ge(dn_mm, b + 1 + CR_DN)
                        act.wait_ge(rows_out[j], 16 * it + 16)
                        act.activation(yb[j][:, :], ps[:, 4 + 2 * j:6 + 2 * j, :].rearrange("p b n -> p (b n)"),
                                       ACT.Copy).then_inc(y_here, 1)
                        act.wait_ge(y_here, b + 1 + CR)
                        act.dma_start(rows_d[bass.ds(b * P, P), :], yb[j][:, :]).then_inc(rows_out[j], 16)
                done = act.lower_val(16 * (pairs_done(act) + 1))
                for j in range(2):
                    act.wait_ge(rows_out[j], done)
                act.sem_inc(ended4, 1)

            @block.tensor
            def _(pe):
                def turn(b, it, j):
                    pe.wait_ge(xg_in[j], 16 * it + 16)
                    wait(pe, xT_here, b)
                    for k in range(KC):
                        last = pe.transpose(ps[:, k // 4, (k % 4) * P:(k % 4 + 1) * P], xg[j][:, k * P:(k + 1) * P], ident)
                    last.then_inc(x_tr, 1)

                def gate_up(b, it, j, slot):
                    pe.wait_ge(we_in[j], WE * (it + 2))
                    pe.wait_ge(xT_here, b + 1)
                    pe.wait_ge(hbT_here, b + 1)
                    for k in range(KC):
                        last = pe.matmul(ps[:, 2 + j, :].rearrange("p (a f) -> p a f", a=2), xT[j][:, k, :],
                                         w_gu[:, bass.ds(slot, 1), :, k * F:(k + 1) * F].rearrange("p o a f -> p (o a) f"),
                                         start=(k == 0), stop=(k == KC - 1))
                    last.then_inc(gu_mm, 1)

                def turn_h(b, j):
                    pe.wait_ge(hb_made, b + 1 + CR)
                    for ch in range(FC):
                        last = pe.transpose(ps[:, 2 + j, ch * P:(ch + 1) * P],
                                            hb[j].rearrange("t (p c) -> t c p", c=FC)[:, ch, :], ident)
                    last.then_inc(h_tr, 1)

                def down(b, j, slot):
                    pe.wait_ge(hbT_here, b + 1 + CR)
                    pe.wait_ge(y_here, b + 1)
                    for half in range(2):
                        for ch in range(FC):
                            last = pe.matmul(ps[:, 4 + 2 * j + half, :], hT[j][:, ch, :],
                                             w_dn[:, bass.ds(slot, 1), ch * D + 512 * half:ch * D + 512 * half + 512],
                                             start=(ch == 0), stop=(ch == FC - 1))
                    last.then_inc(dn_mm, 1)

                pe.wait_ge(early_in, 16 * 3 * EARLY)
                pe.sem_inc(y_here, CR)
                for b in range(2):
                    turn(b, 0, b)
                with pairs_of_blocks(pe) as (it, word):
                    slots = [slot_of(word, j) for j in range(2)]
                    for j in range(2):
                        gate_up(2 * it + j, it, j, slots[j])
                    for j in range(2):
                        b = 2 * it + j
                        turn_h(b, j)
                        turn(b + 2, it + 1, j)
                        down(b, j, slots[j])

            @block.vector
            def _(dve):
                own = Own(dve, dve4)

                def x_copy(b, j):
                    dve.wait_ge(x_tr, b + 1 + CR)
                    dve.wait_ge(gu_mm, b - 1)
                    dve.tensor_copy(xT[j].rearrange("p k t -> p (k t)"),
                                    ps[:, 0:2, :].rearrange("p b n -> p (b n)")).then_inc(xT_here, 1)

                def swiglu(b, j):
                    dve.wait_ge(sg_here, b + 1)
                    dve.wait_ge(h_tr, b + 1)
                    own(dve.tensor_tensor(sg[j][:, :], sg[j][:, :], ps[:, 2 + j, 0:F], ALU.mult))
                    own.wait()
                    dve.tensor_tensor(hb[j][:, :], sg[j][:, :], ps[:, 2 + j, F:2 * F], ALU.mult).then_inc(hb_made, 1)

                def h_copy(b, j):
                    dve.wait_ge(h_tr, b + 1 + CR)
                    dve.wait_ge(dn_mm, b + 2)
                    dve.tensor_copy(hT[j].rearrange("p c t -> p (c t)"), ps[:, 2 + j, 0:F]).then_inc(hbT_here, 1)

                dve.memset(zrows[:, :], 0.0).then_inc(zrows_made, 1)
                dve.sem_inc(hbT_here, CR)
                dve.sem_inc(h_tr, CR)
                for b in range(2):
                    dve.wait_ge(x_tr, b + 1 + CR)
                    dve.tensor_copy(xT[b].rearrange("p k t -> p (k t)"),
                                    ps[:, 0:2, :].rearrange("p b n -> p (b n)")).then_inc(xT_here, 1)
                with own.over_pairs(pairs_of_blocks(dve), 2) as (it, _):
                    b0, b1 = 2 * it, 2 * it + 1
                    swiglu(b0, 0)
                    h_copy(b0, 0)
                    swiglu(b1, 1)
                    x_copy(b0 + 2, 0)
                    h_copy(b1, 1)
                    x_copy(b1 + 2, 1)

        rk = [place(f"rk{j}", 65 + 32 * j, [P, TOPK, D]) for j in range(2)]
        hx = [place(f"hx{j}", 129 + 4 * j, [P, KC, P]) for j in range(2)]
        xr5 = [place(f"xr5_{j}", 137 + 4 * j, [P, D]) for j in range(2)]
        h5 = place("h5", 145, [P, F])
        sg5 = place("sg5", 146, [P, F])
        hT5 = place("hT5", 147, [P, FC, P])
        acc = [place(f"acc{j}", 148 + 4 * j, [P, D]) for j in range(2)]
        g2s = place("g2s", 156, [NS, D])
        junk5 = place("junk5", 160, [P, D])
        s5 = place("s5", 164, [P, 8])
        rms = [place(f"rms{j}", 164.03125 + j / 32, [P, 2]) for j in range(2)]
        wk = place("wk", 164.25, [P, TOPK])
        didx = [place(f"didx{j}", 164.5 + j / 8, [P, TOPK], I32) for j in range(2)]
        g2s_in = sem("g2s_in")
        hx_in = [sem(f"hx_in{j}") for j in range(2)]
        xr5_in = [sem(f"xr5_in{j}") for j in range(2)]
        rk_in = [sem(f"rk_in{j}") for j in range(2)]
        y_out = [sem(f"y_out{j}") for j in range(2)]
        gu5, sg5_here, h5_made, h5_tr, hT5_here, dn5, summed, ss5, scaled, rt5, y_made, didx_here = (
            sem("gu5"), sem("sg5_here"), sem("h5_made"), sem("h5_tr"), sem("hT5_here"), sem("dn5"), sem("summed"),
            sem("ss5"), sem("scaled"), sem("rt5"), sem("y_made"), sem("didx_here"))
        dn5_read, dve5, pool5 = sem("dn5_read"), sem("dve5"), sem("pool5")

        def load_h2(eng, s):
            _, rows = tokens(s)
            eng.dma_start(hx[s.par][:, :, 0:rows], h2T_d[bass.ds(s.n, 1)].rearrange("o p (k t) -> p (o k) t", k=KC)[:, :, 0:rows]
                          ).then_inc(hx_in[s.par], 16)

        with nc.Block() as block:
            @block.sync
            def _(sp):
                def load_x1(s):
                    a, rows = tokens(s)
                    x_from, = addressed(sp, x1_d[bass.ds(a, rows), :])
                    wait(sp, y_made, s.n - 1)
                    sp.dma_start(xr5[s.par][0:rows, :], x_from).then_inc(xr5_in[s.par], 16)

                def stores(s):
                    a, rows = tokens(s)
                    y_to = y_sample.rearrange("b s d -> (b s) d") if rows == NS else y_prompt[0][bass.ds(a, P), :]
                    addressed(sp, y_to)
                    sp.wait_ge(y_made, s.n + 1)
                    sp.dma_start(y_to, acc[s.par][0:rows, :]).then_inc(y_out[s.par], 16)

                for j in range(2):
                    sp.sem_inc(y_out[j], 16)
                load_h2(sp, fixed(0))
                load_h2(sp, fixed(1))
                sp.dma_start(g2s[:, :], mod_d[0:NS, G2 * D:(G2 + 1) * D]).then_inc(g2s_in, 16)
                for n in range(2):
                    load_x1(fixed(n))
                stores(fixed(0))
                load_x1(fixed(2))
                with sp.Fori(0, 3) as it:
                    for s in (Step(2 * it + 1, 1, it), Step(2 * it + 2, 0, it + 1)):
                        stores(s)
                        load_x1(s.next.next)
                stores(fixed(7))
                stores(fixed(8))
                for j in range(2):
                    sp.wait_ge(y_out[j], 16 * (NT // 2 + 1 - j) + 16)

            @block.gpsimd
            def _(pool):
                own = Own(pool, pool5)

                def gather(s, rows):
                    wait(pool, summed, s.n - 1)
                    own(pool.tensor_copy(didx[s.par][:, :], dst_i[:, bass.ds(s.n * TOPK, TOPK)]))
                    own.wait()
                    pool.sem_inc(didx_here, 1)
                    for k in range(TOPK):
                        pool.indirect_dma_start(out=rk[s.par][0:rows, k, :], out_offset=None, in_=rows_d[:, :],
                                                in_offset=bass.IndirectOffsetOnAxis(ap=didx[s.par][0:rows, k:k + 1], axis=0)
                                                ).then_inc(rk_in[s.par], 16)

                gather(fixed(0), NS)
                gather(fixed(1), P)
                gather(fixed(2), P)
                with own.loop(3, 2) as it:
                    for s in (Step(2 * it + 3, 1, it + 1), Step(2 * it + 4, 0, it + 2)):
                        gather(s, P)

            @block.scalar
            def _(act):
                def gated(s, rows, more=True):
                    act.wait_ge(gu5, s.n + 1)
                    wait(act, h5_made, s.n)
                    act.activation(sg5[0:rows, :], ps[0:rows, 0, 0:F], ACT.Sigmoid).then_inc(sg5_here, 1)
                    if more:
                        load_h2(act, s.next.next)

                def norm(s, rows):
                    act.wait_ge(summed, s.n + 1)
                    wait(act, rt5, s.n)
                    act.activation(junk5[0:rows, :], acc[s.par][0:rows, :], ACT.Square, accum_out=s5[0:rows, 0:1]).then_inc(ss5, 1)
                    act.wait_ge(ss5, s.n + 1)
                    wait(act, scaled, s.n - 1)
                    act.activation(rms[s.par][0:rows, 0:1], s5[0:rows, 0:1], ACT.Sqrt, bias=c("eps", rows), scale=1.0 / D
                                   ).then_inc(rt5, 1)

                gated(fixed(0), NS)
                gated(fixed(1), P)
                gated(fixed(2), P)
                norm(fixed(0), NS)
                with act.Fori(0, 2) as it:
                    for s in (Step(2 * it + 1, 1, it), Step(2 * it + 2, 0, it + 1)):
                        gated(s.next.next, P)
                        norm(s, P)
                for n in (7, 8):
                    gated(fixed(n), P, more=False)
                    norm(fixed(n - 2), P)
                norm(fixed(7), P)
                norm(fixed(8), P)

            @block.tensor
            def _(pe):
                def body(s, rows):
                    pe.wait_ge(hx_in[s.par], 16 * s.turn + 16)
                    wait(pe, hT5_here, s.n)
                    for k in range(KC):
                        last = pe.matmul(ps[0:rows, 0, :].rearrange("p (a f) -> p a f", a=2), hx[s.par][:, k, 0:rows],
                                         s_gu[:, :, k * F:(k + 1) * F], start=(k == 0), stop=(k == KC - 1))
                    last.then_inc(gu5, 1)
                    pe.wait_ge(h5_made, s.n + 1)
                    for ch in range(FC):
                        last = pe.transpose(ps[:, 1, ch * P:ch * P + rows], h5[0:rows, :].rearrange(
                            "t (p c) -> t c p", c=FC)[:, ch, :], c("ident", rows)[:, 0:rows])
                    last.then_inc(h5_tr, 1)
                    pe.wait_ge(hT5_here, s.n + 1)
                    wait(pe, dn5_read, s.n - 1)
                    for half in range(2):
                        for ch in range(FC):
                            last = pe.matmul(ps[0:rows, 2 + 2 * s.par + half, :], hT5[:, ch, 0:rows],
                                             s_dn[:, ch, 512 * half:512 * half + 512], start=(ch == 0), stop=(ch == FC - 1))
                    last.then_inc(dn5, 1)

                pe.wait_ge(sw_in, 48)
                body(fixed(0), NS)
                with pe.Fori(0, NT // 2) as it:
                    for s in (Step(2 * it + 1, 1, it), Step(2 * it + 2, 0, it + 1)):
                        body(s, P)

            @block.vector
            def _(dve):
                own = Own(dve, dve5)

                def hidden(s, rows):
                    dve.wait_ge(sg5_here, s.n + 1)
                    wait(dve, h5_tr, s.n)
                    own(dve.tensor_tensor(sg5[0:rows, :], sg5[0:rows, :], ps[0:rows, 0, 0:F], ALU.mult))
                    own.wait()
                    dve.tensor_tensor(h5[0:rows, :], sg5[0:rows, :], ps[0:rows, 0, F:2 * F], ALU.mult).then_inc(h5_made, 1)
                    dve.wait_ge(h5_tr, s.n + 1)
                    wait(dve, dn5, s.n)
                    dve.tensor_copy(hT5[:, :, 0:rows], ps[:, 1, 0:FC * P].rearrange("p (c t) -> p c t", c=FC)[:, :, 0:rows]
                                    ).then_inc(hT5_here, 1)

                def total(s, rows):
                    y = acc[s.par][0:rows, :]
                    own(dve.tensor_copy(wk[:, :], route_w[:, bass.ds(s.n, 1), :].rearrange("p o k -> p (o k)")))
                    own.wait()
                    dve.wait_ge(dn5, s.n + 1)
                    dve.wait_ge(rk_in[s.par], 16 * TOPK * (s.turn + 1))
                    dve.wait_ge(y_out[s.par], 16 * s.turn + 16)
                    dve.scalar_tensor_tensor(out=y, in0=rk[s.par][0:rows, 0, :], scalar=wk[0:rows, 0:1],
                                             in1=ps[0:rows, 2 + 2 * s.par:4 + 2 * s.par, :].rearrange("p b n -> p (b n)"), op0=ALU.mult,
                                             op1=ALU.add).then_inc(dn5_read, 1)
                    dve.wait_ge(dn5_read, s.n + 1)
                    for k in range(1, TOPK):
                        ins = dve.scalar_tensor_tensor(out=y, in0=rk[s.par][0:rows, k, :], scalar=wk[0:rows, k:k + 1], in1=y,
                                                       op0=ALU.mult, op1=ALU.add)
                        if k < TOPK - 1:
                            own(ins)
                            own.wait()
                    ins.then_inc(summed, 1)

                def finish(s, rows, g2):
                    y = acc[s.par][0:rows, :]
                    dve.wait_ge(rt5, s.n + 1)
                    own(dve.reciprocal(rms[s.par][0:rows, 1:2], rms[s.par][0:rows, 0:1]))
                    own.wait()
                    dve.scalar_tensor_tensor(out=y, in0=y, scalar=rms[s.par][0:rows, 1:2], in1=g2, op0=ALU.mult, op1=ALU.mult
                                             ).then_inc(scaled, 1)
                    dve.wait_ge(scaled, s.n + 1)
                    dve.wait_ge(xr5_in[s.par], 16 * s.turn + 16)
                    dve.tensor_tensor(y, y, xr5[s.par][0:rows, :], ALU.add).then_inc(y_made, 1)

                dve.wait_ge(g2s_in, 16)
                g2 = mods[:, G2, :]
                hidden(fixed(0), NS)
                hidden(fixed(1), P)
                total(fixed(0), NS)
                hidden(fixed(2), P)
                total(fixed(1), P)
                finish(fixed(0), NS, g2s[:, :])
                with own.loop(3, 2 * 9) as it:
                    for s in (Step(2 * it + 2, 0, it + 1), Step(2 * it + 3, 1, it + 1)):
                        hidden(s.next, P)
                        total(s, P)
                        finish(s.last, P, g2)
                total(fixed(8), P)
                finish(fixed(7), P, g2)
                finish(fixed(8), P, g2)



_INS = ["x_prompt", "x_sample", "c_prompt", "c_sample", "cache_k", "cache_v", "state_pool", "page_table", "ada_w",
        "ada_b", "pre_mix_g", "post_mix_g", "pre_ffn_g", "post_ffn_g", "w_in", "w_out", "lambda_q1", "lambda_k1",
        "lambda_q2", "lambda_k2", "subln_g", "pool_w", "pool_scale", "router_w", "router_bias", "expert_w_gate",
        "expert_w_up", "expert_w_down", "shared_w_gate", "shared_w_up", "shared_w_down"]
_OUTS = [(1, SEQ, D), (NS, 1, D), (1, 1, SEQ, NH, 2 * HD), (1, 1, SEQ, NH, 2 * HD), (1, 1, BUF, NG * P),
         (1, NS, 1, NH, 2 * HD), (1, NS, 1, NH, 2 * HD), (1, NS, BUF, NG * P)]


def kernel(**inputs):
    import concourse.bacc as bacc
    from concourse.bass_utils import run_bass_kernel_spmd

    nc = bacc.Bacc("TRN2", target_bir_lowering=False, num_devices=1)
    arrays, args = {}, []
    given = {name: np.ascontiguousarray(inputs[name]) for name in _INS}
    given["const"] = constants()[0]
    for name, a in given.items():
        arrays[f"in_{name}"] = a
        args.append(nc.dram_tensor(f"in_{name}", a.shape, mybir.dt.from_np(a.dtype), kind="ExternalInput").ap())
    outs = [nc.dram_tensor(f"out_{i}", shape, F32, kind="ExternalOutput").ap() for i, shape in enumerate(_OUTS)]
    build(nc, args, outs)
    r = run_bass_kernel_spmd(nc, [arrays], core_ids=[0])
    return tuple(r.results[0][f"out_{i}"] for i in range(len(_OUTS)))
```
